# Optimizing a Trainium2 kernel written in Bass

```python
import math
import jax, jax.numpy as jnp
from jax import lax
import numpy as np

D_MODEL = 1024
BATCH = 1
SEQ = 512
DEPTH = 1

HEAD_DIM = 64
BLOCK_Q = 128
RMS_EPS = 1e-6
NEG_INF = -1e30
TINY = 1e-30

FOX_HEADS = 4
FORGET_BIAS_INIT = 3.0
DIL_WINDOWS = (128, 512, 2048)
DIL_RATES = (1, 4, 16)
DIL_HEADS_PER_GROUP = 2
DIL_HEADS = DIL_HEADS_PER_GROUP * len(DIL_WINDOWS)
NSA_HEADS = 6
NSA_KV_GROUPS = 2
NSA_CMP_BLOCK = 32
NSA_CMP_STRIDE = 16
NSA_CMP_HIDDEN = 256
NSA_SEL_BLOCK = 64
NSA_SEL_TOPK = 8
NSA_WINDOW = 512
FORCE_SCORE = 1e6
ALIBI_HEADS = DIL_HEADS + NSA_HEADS
D_FF = 2816
CONV_WIDTH = 3

FOX_W = FOX_HEADS * HEAD_DIM
DIL_W = DIL_HEADS * HEAD_DIM
NSA_W = NSA_HEADS * HEAD_DIM
NSA_KV_W = NSA_KV_GROUPS * HEAD_DIM
IN_SPLITS = (FOX_W, FOX_W, FOX_W, FOX_HEADS,
             DIL_W, DIL_W, DIL_W,
             NSA_W, NSA_KV_W, NSA_KV_W, NSA_KV_W, NSA_KV_W, NSA_KV_W, NSA_KV_W, NSA_HEADS * 3,
             3 * D_MODEL)
D_IN = sum(IN_SPLITS)


def rms_norm(x, g):
    xf = x.astype(jnp.float32)
    y = xf * lax.rsqrt(jnp.mean(xf * xf, axis=-1, keepdims=True) + RMS_EPS)
    return (y * g.astype(jnp.float32)).astype(x.dtype)

def alibi_slopes(n):
    return jnp.exp2(-8.0 * jnp.arange(1, n + 1, dtype=jnp.float32) / n)

def masked_softmax(s, mask):
    s = jnp.where(mask, s, NEG_INF)
    m = jnp.max(s, axis=-1, keepdims=True)
    e = jnp.where(mask, jnp.exp(s - m), 0.0)
    l = jnp.maximum(jnp.sum(e, axis=-1, keepdims=True), TINY)
    return e / l, (m + jnp.log(l))[..., 0]

def fox_attention(q, k, v, f_logit):
    B_, S, H, dh = q.shape
    nb = S // BLOCK_Q
    scale = dh ** -0.5
    c = jnp.cumsum(jax.nn.log_sigmoid(f_logit.astype(jnp.float32)), axis=1)
    c = jnp.transpose(c, (0, 2, 1))
    q_blocks = q.reshape(B_, nb, BLOCK_Q, H, dh).transpose(1, 0, 2, 3, 4)
    c_blocks = c.reshape(B_, H, nb, BLOCK_Q).transpose(2, 0, 1, 3)
    kpos = jnp.arange(S)

    def body(args):
        qb, cb, i = args
        qpos = i * BLOCK_Q + jnp.arange(BLOCK_Q)
        s = jnp.einsum('bqhd,bkhd->bhqk', qb, k).astype(jnp.float32) * scale
        s = s + cb[..., :, None] - c[:, :, None, :]
        p, _ = masked_softmax(s, kpos[None, :] <= qpos[:, None])
        return jnp.einsum('bhqk,bkhd->bqhd', p.astype(v.dtype), v)

    out = lax.map(body, (q_blocks, c_blocks, jnp.arange(nb)))
    return out.transpose(1, 0, 2, 3, 4).reshape(B_, S, H * dh)

def dilated_attention(q, k, v, slopes):
    B_, S, H, dh = q.shape
    P = DIL_HEADS_PER_GROUP
    nb = S // BLOCK_Q
    scale = dh ** -0.5
    q_blocks = q.reshape(B_, nb, BLOCK_Q, H, dh).transpose(1, 0, 2, 3, 4)

    def body(args):
        qb, i = args
        qpos = i * BLOCK_Q + jnp.arange(BLOCK_Q)
        outs, lses = [], []
        for g, (w, r) in enumerate(zip(DIL_WINDOWS, DIL_RATES)):
            hs = slice(g * P, (g + 1) * P)
            offs = r * jnp.arange(w // r + 1)
            kidx = qpos[:, None] - offs[None, :]
            valid = kidx >= 0
            kidx = jnp.maximum(kidx, 0)
            kg = k[:, :, hs][:, kidx]
            vg = v[:, :, hs][:, kidx]
            s = jnp.einsum('bqhd,bqkhd->bhqk', qb[:, :, hs], kg).astype(jnp.float32) * scale
            s = s - slopes[hs][None, :, None, None] * offs.astype(jnp.float32)[None, None, None, :]
            p, lse = masked_softmax(s, valid[None, None])
            outs.append(jnp.einsum('bhqk,bqkhd->bqhd', p.astype(vg.dtype), vg))
            lses.append(lse)
        alpha = jax.nn.softmax(jnp.stack(lses, 0), axis=0)
        o = jnp.stack(outs, 0) * alpha.transpose(0, 1, 3, 2)[..., None].astype(qb.dtype)
        return o.transpose(1, 2, 0, 3, 4).reshape(B_, BLOCK_Q, H * dh)

    out = lax.map(body, (q_blocks, jnp.arange(nb)))
    return out.transpose(1, 0, 2, 3).reshape(B_, S, H * dh)

def compress_blocks(kv, pe, w1, w2):
    B_, S, G, dh = kv.shape
    n_cmp = (S - NSA_CMP_BLOCK) // NSA_CMP_STRIDE + 1
    idx = jnp.arange(n_cmp)[:, None] * NSA_CMP_STRIDE + jnp.arange(NSA_CMP_BLOCK)[None, :]
    blocks = kv[:, idx] + pe[None, None, :, None, :]
    flat = blocks.transpose(0, 1, 3, 2, 4).reshape(B_, n_cmp, G, NSA_CMP_BLOCK * dh)
    return jax.nn.gelu(flat @ w1) @ w2

def nsa_attention(q, k_cmp, v_cmp, k_sel, v_sel, k_win, v_win, gate_logits, slopes,
                  cmp_pe, k_w1, k_w2, v_w1, v_w2):
    B_, S, H, dh = q.shape
    G = NSA_KV_GROUPS
    R = H // G
    nb = S // BLOCK_Q
    scale = dh ** -0.5
    kc = compress_blocks(k_cmp, cmp_pe, k_w1, k_w2)
    vc = compress_blocks(v_cmp, cmp_pe, v_w1, v_w2)
    n_cmp = kc.shape[1]
    cmp_end = jnp.arange(n_cmp) * NSA_CMP_STRIDE + NSA_CMP_BLOCK - 1
    cmp_start = cmp_end - (NSA_CMP_BLOCK - 1)
    n_sel = S // NSA_SEL_BLOCK
    sel_idx = jnp.arange(n_sel)
    sel_start = sel_idx * NSA_SEL_BLOCK
    overlap = ((cmp_start[:, None] < sel_start[None, :] + NSA_SEL_BLOCK)
               & (cmp_end[:, None] >= sel_start[None, :])).astype(jnp.float32)
    top_k = min(NSA_SEL_TOPK, n_sel)
    n_tok = top_k * NSA_SEL_BLOCK
    slope = slopes.reshape(G, R)[None, :, :, None, None]
    ks_t = k_sel.transpose(0, 2, 1, 3)
    vs_t = v_sel.transpose(0, 2, 1, 3)
    pad = ((0, 0), (NSA_WINDOW, 0), (0, 0), (0, 0))
    kw_pad = jnp.pad(k_win, pad)
    vw_pad = jnp.pad(v_win, pad)
    gather = jax.vmap(jax.vmap(lambda t, ii: t[ii]))
    q_blocks = q.reshape(B_, nb, BLOCK_Q, G, R, dh).transpose(1, 0, 2, 3, 4, 5)
    g_blocks = jax.nn.sigmoid(gate_logits).reshape(B_, nb, BLOCK_Q, G, R, 3).transpose(1, 0, 2, 3, 4, 5)

    def body(args):
        qb, gb, i = args
        q0 = i * BLOCK_Q
        qpos = q0 + jnp.arange(BLOCK_Q)
        s = jnp.einsum('bqgrd,bcgd->bgrqc', qb, kc).astype(jnp.float32) * scale
        s = s - slope * (qpos[:, None] - cmp_end[None, :]).astype(jnp.float32)
        p_c, _ = masked_softmax(s, cmp_end[None, :] <= qpos[:, None])
        o_c = jnp.einsum('bgrqc,bcgd->bqgrd', p_c.astype(vc.dtype), vc)
        imp = jnp.einsum('bgrqc,cj->bgqj', p_c, overlap)
        qblk = qpos // NSA_SEL_BLOCK
        causal = sel_start[None, :] <= qpos[:, None]
        forced = ((sel_idx[None, :] == 0) | (sel_idx[None, :] == qblk[:, None])
                  | (sel_idx[None, :] == qblk[:, None] - 1))
        score = jnp.where(causal & forced, FORCE_SCORE, jnp.where(causal, imp, -1.0))
        _, blk = lax.top_k(score, top_k)
        blk_ok = blk * NSA_SEL_BLOCK <= qpos[None, None, :, None]
        tok = (blk[..., None] * NSA_SEL_BLOCK + jnp.arange(NSA_SEL_BLOCK)).reshape(B_, G, BLOCK_Q, n_tok)
        tok_ok = jnp.repeat(blk_ok, NSA_SEL_BLOCK, axis=-1) & (tok <= qpos[None, None, :, None])
        kg = gather(ks_t, tok)
        vg = gather(vs_t, tok)
        s = jnp.einsum('bqgrd,bgqtd->bgrqt', qb, kg).astype(jnp.float32) * scale
        s = s - slope * (qpos[None, None, :, None] - tok)[:, :, None].astype(jnp.float32)
        p_s, _ = masked_softmax(s, tok_ok[:, :, None])
        o_s = jnp.einsum('bgrqt,bgqtd->bqgrd', p_s.astype(vg.dtype), vg)
        kw = lax.dynamic_slice_in_dim(kw_pad, q0, NSA_WINDOW + BLOCK_Q, axis=1)
        vw = lax.dynamic_slice_in_dim(vw_pad, q0, NSA_WINDOW + BLOCK_Q, axis=1)
        kpos = q0 - NSA_WINDOW + jnp.arange(NSA_WINDOW + BLOCK_Q)
        diff = qpos[:, None] - kpos[None, :]
        mask_w = (kpos[None, :] >= 0) & (diff >= 0) & (diff < NSA_WINDOW)
        s = jnp.einsum('bqgrd,bkgd->bgrqk', qb, kw).astype(jnp.float32) * scale
        s = s - slope * diff.astype(jnp.float32)
        p_w, _ = masked_softmax(s, mask_w)
        o_w = jnp.einsum('bgrqk,bkgd->bqgrd', p_w.astype(vw.dtype), vw)
        gb = gb.astype(qb.dtype)
        o = gb[..., 0:1] * o_c + gb[..., 1:2] * o_s + gb[..., 2:3] * o_w
        return o.reshape(B_, BLOCK_Q, H * dh)

    out = lax.map(body, (q_blocks, g_blocks, jnp.arange(nb)))
    return out.transpose(1, 0, 2, 3).reshape(B_, S, H * dh)

def conv_ffn(h, w_up, conv_w, conv_b, w_down):
    a, b = jnp.split(h @ w_up, 2, axis=-1)
    a = lax.conv_general_dilated(a, conv_w.reshape(CONV_WIDTH, 1, D_FF), window_strides=(1,),
                                 padding=[(CONV_WIDTH - 1, 0)],
                                 dimension_numbers=('NWC', 'WIO', 'NWC'),
                                 feature_group_count=D_FF) + conv_b
    return (jax.nn.gelu(a) * b) @ w_down

def first_inputs(seed: int = 0) -> dict:
    key = jax.random.key(seed)
    ks = jax.random.split(key, 20)
    f32 = jnp.float32

    def nrm(k, shape, scale):
        return jax.random.normal(k, shape, f32) * scale

    L = DEPTH
    fo = 3 * FOX_W
    b_in = nrm(ks[3], (L, D_IN), 0.02).at[:, fo:fo + FOX_HEADS].add(FORGET_BIAS_INIT)
    return {
        "x": nrm(ks[0], (BATCH, SEQ, D_MODEL), 1.0),
        "norm1_g": 1.0 + nrm(ks[1], (L, D_MODEL), 0.02),
        "w_in": nrm(ks[2], (L, D_MODEL, D_IN), D_MODEL ** -0.5),
        "b_in": b_in,
        "cmp_pe": nrm(ks[4], (L, NSA_CMP_BLOCK, HEAD_DIM), 0.02),
        "cmp_k_w1": nrm(ks[5], (L, NSA_CMP_BLOCK * HEAD_DIM, NSA_CMP_HIDDEN), (NSA_CMP_BLOCK * HEAD_DIM) ** -0.5),
        "cmp_k_w2": nrm(ks[6], (L, NSA_CMP_HIDDEN, HEAD_DIM), NSA_CMP_HIDDEN ** -0.5),
        "cmp_v_w1": nrm(ks[7], (L, NSA_CMP_BLOCK * HEAD_DIM, NSA_CMP_HIDDEN), (NSA_CMP_BLOCK * HEAD_DIM) ** -0.5),
        "cmp_v_w2": nrm(ks[8], (L, NSA_CMP_HIDDEN, HEAD_DIM), NSA_CMP_HIDDEN ** -0.5),
        "w_pa": nrm(ks[9], (L, FOX_W, D_MODEL), FOX_W ** -0.5),
        "w_pb": nrm(ks[10], (L, DIL_W, D_MODEL), DIL_W ** -0.5),
        "w_pc": nrm(ks[11], (L, NSA_W, D_MODEL), NSA_W ** -0.5),
        "w_o": nrm(ks[12], (L, D_MODEL, D_MODEL), D_MODEL ** -0.5),
        "norm2_g": 1.0 + nrm(ks[13], (L, D_MODEL), 0.02),
        "w_up": nrm(ks[14], (L, D_MODEL, 2 * D_FF), D_MODEL ** -0.5),
        "conv_w": nrm(ks[15], (L, CONV_WIDTH, D_FF), CONV_WIDTH ** -0.5),
        "conv_b": nrm(ks[16], (L, D_FF), 0.02),
        "w_down": nrm(ks[17], (L, D_FF, D_MODEL), D_FF ** -0.5),
        "final_g": 1.0 + nrm(ks[18], (D_MODEL,), 0.02),
    }

def first_block(x, norm1_g, w_in, b_in, cmp_pe, cmp_k_w1, cmp_k_w2, cmp_v_w1, cmp_v_w2,
              w_pa, w_pb, w_pc, w_o, norm2_g, w_up, conv_w, conv_b, w_down, final_g):
    B_, S, D = x.shape
    dh = HEAD_DIM
    G = NSA_KV_GROUPS
    slopes = alibi_slopes(ALIBI_HEADS)
    dil_slopes = slopes[0::2]
    nsa_slopes = slopes[1::2]
    split_at = np.cumsum(IN_SPLITS)[:-1].tolist()
    for l in range(DEPTH):
        h = rms_norm(x, norm1_g[l])
        proj = h @ w_in[l] + b_in[l]
        (qa, ka, va, fa, qb, kb, vb, qc, kc_, vc_, ksl, vsl, kwn, vwn, gc, gates) = jnp.split(proj, split_at, axis=-1)
        y_a = fox_attention(qa.reshape(B_, S, FOX_HEADS, dh), ka.reshape(B_, S, FOX_HEADS, dh),
                            va.reshape(B_, S, FOX_HEADS, dh), fa)
        y_b = dilated_attention(qb.reshape(B_, S, DIL_HEADS, dh), kb.reshape(B_, S, DIL_HEADS, dh),
                                vb.reshape(B_, S, DIL_HEADS, dh), dil_slopes)
        y_c = nsa_attention(qc.reshape(B_, S, NSA_HEADS, dh),
                            kc_.reshape(B_, S, G, dh), vc_.reshape(B_, S, G, dh),
                            ksl.reshape(B_, S, G, dh), vsl.reshape(B_, S, G, dh),
                            kwn.reshape(B_, S, G, dh), vwn.reshape(B_, S, G, dh),
                            gc.reshape(B_, S, NSA_HEADS, 3), nsa_slopes,
                            cmp_pe[l], cmp_k_w1[l], cmp_k_w2[l], cmp_v_w1[l], cmp_v_w2[l])
        g = jax.nn.sigmoid(gates).reshape(B_, S, 3, D)
        merged = (g[:, :, 0] * (y_a @ w_pa[l]) + g[:, :, 1] * (y_b @ w_pb[l])
                  + g[:, :, 2] * (y_c @ w_pc[l]))
        x = x + merged @ w_o[l]
        x = x + conv_ffn(rms_norm(x, norm2_g[l]), w_up[l], conv_w[l], conv_b[l], w_down[l])
    return rms_norm(x, final_g)


D_CONV = 512
CONV_GROUPS = 8
HG_HEADS = 4
HG_KD = 128
HG_VD = 128
D_HG = HG_HEADS * HG_KD
D_MIX = D_CONV + D_HG
D_IN_2 = 3 * D_CONV + 4 * D_HG
CHUNK = 32
PEER_HEADS = 8
N_KEYS = 128
N_EXPERTS = N_KEYS * N_KEYS
D_QUERY = 256
HALF_Q = D_QUERY // 2
PEER_TOPK = 16
TOKEN_BLOCK = 128
EPS = 1e-6


def rmsnorm(x, gain):
    x32 = x.astype(jnp.float32)
    y = x32 * lax.rsqrt(jnp.mean(x32 * x32, axis=-1, keepdims=True) + EPS)
    return (y * gain.astype(jnp.float32)).astype(x.dtype)

def group_rmsnorm(x, gain, groups):
    shp = x.shape
    xg = x.reshape(shp[:-1] + (groups, shp[-1] // groups)).astype(jnp.float32)
    y = xg * lax.rsqrt(jnp.mean(xg * xg, axis=-1, keepdims=True) + EPS)
    return (y.reshape(shp) * gain.astype(jnp.float32)).astype(x.dtype)

def short_conv_mixer(c_gate, h, b_gate, conv_w, gain):
    u = c_gate * h
    s = u.shape[1]
    up = jnp.pad(u, ((0, 0), (CONV_WIDTH - 1, 0), (0, 0)))
    y = conv_w[0] * up[:, 0:s]
    for j in range(1, CONV_WIDTH):
        y = y + conv_w[j] * up[:, j:j + s]
    y = b_gate * y
    return group_rmsnorm(y, gain, CONV_GROUPS)

def hgrn2_mixer(q, f_pre, v, g, lb, gain):
    f32 = jnp.float32
    bsz, s, _ = q.shape
    n_chunks = s // CHUNK

    def heads(t):
        return t.reshape(bsz, n_chunks, CHUNK, HG_HEADS, -1).transpose(0, 3, 1, 2, 4)

    qh = heads(jax.nn.silu(q.astype(f32)) * (HG_KD ** -0.5))
    f = lb + (1.0 - lb) * jax.nn.sigmoid(f_pre.astype(f32))
    kh = heads(1.0 - f)
    logf = heads(jnp.log(f))
    vh = heads(v.astype(f32))
    G = jnp.cumsum(logf, axis=3)
    G_last = G[:, :, :, -1:, :]
    q_dec = qh * jnp.exp(G)
    k_dec = kh * jnp.exp(-G)
    causal = jnp.tril(jnp.ones((CHUNK, CHUNK), dtype=bool))
    A = jnp.einsum('bhnck,bhnsk->bhncs', q_dec, k_dec)
    A = jnp.where(causal, A, 0.0)
    o_intra = jnp.einsum('bhncs,bhnsv->bhncv', A, vh)
    k_end = kh * jnp.exp(G_last - G)
    decay = jnp.exp(G_last[:, :, :, 0, :])

    def step(state, xs):
        dec_n, k_n, v_n, q_n = xs
        o_n = jnp.einsum('bhck,bhkv->bhcv', q_n, state)
        state = dec_n[..., None] * state + jnp.einsum('bhck,bhcv->bhkv', k_n, v_n)
        return state, o_n

    state0 = jnp.zeros((bsz, HG_HEADS, HG_KD, HG_VD), f32)
    _, o_inter = lax.scan(step, state0, (jnp.moveaxis(decay, 2, 0), jnp.moveaxis(k_end, 2, 0),
                                         jnp.moveaxis(vh, 2, 0), jnp.moveaxis(q_dec, 2, 0)))
    o = o_intra + jnp.moveaxis(o_inter, 0, 2)
    o = o * lax.rsqrt(jnp.mean(o * o, axis=-1, keepdims=True) + EPS) * gain.astype(f32)
    o = o * jax.nn.silu(heads(g.astype(f32)))
    o = o.transpose(0, 2, 3, 1, 4).reshape(bsz, s, HG_HEADS * HG_VD)
    return o.astype(q.dtype)

def peer_ffn(x, wq, keys, u_tab, v_tab):
    bsz, s, d = x.shape
    t = bsz * s
    xt = x.reshape(t, d)
    q = (xt @ wq).reshape(t, PEER_HEADS, 2, HALF_Q)
    scores = jnp.einsum('thpd,hpnd->thpn', q, keys).astype(jnp.float32)
    s_top, i_top = lax.top_k(scores, PEER_TOPK)
    cand = (s_top[:, :, 0, :, None] + s_top[:, :, 1, None, :]).reshape(t, PEER_HEADS, PEER_TOPK * PEER_TOPK)
    c_score, c_idx = lax.top_k(cand, PEER_TOPK)
    i1 = jnp.take_along_axis(i_top[:, :, 0], c_idx // PEER_TOPK, axis=-1)
    i2 = jnp.take_along_axis(i_top[:, :, 1], c_idx % PEER_TOPK, axis=-1)
    expert = i1 * N_KEYS + i2
    gates = jax.nn.softmax(c_score, axis=-1)
    n_blocks = t // TOKEN_BLOCK

    def block(args):
        xb, eb, gb = args
        u = jnp.take(u_tab, eb, axis=0)
        a = jax.nn.gelu(jnp.einsum('td,thkd->thk', xb, u).astype(jnp.float32), approximate=False)
        w = (gb * a).astype(xb.dtype)
        vv = jnp.take(v_tab, eb, axis=0)
        return jnp.einsum('thk,thkd->td', w, vv)

    y = lax.map(block, (xt.reshape(n_blocks, TOKEN_BLOCK, d),
                        expert.reshape(n_blocks, TOKEN_BLOCK, PEER_HEADS, PEER_TOPK),
                        gates.reshape(n_blocks, TOKEN_BLOCK, PEER_HEADS, PEER_TOPK)))
    return y.reshape(bsz, s, d)

def second_inputs(seed: int = 0) -> dict:
    key = jax.random.key(seed)
    ks = jax.random.split(key, 16)
    f32 = jnp.float32
    nrm = lambda k, shp: jax.random.normal(k, shp, f32)
    return {
        "x": nrm(ks[0], (BATCH, SEQ, D_MODEL)),
        "norm_mix": 1.0 + 0.02 * nrm(ks[1], (DEPTH, D_MODEL)),
        "w_in": nrm(ks[2], (DEPTH, D_MODEL, D_IN_2)) * D_MODEL ** -0.5,
        "conv_w": nrm(ks[3], (DEPTH, CONV_WIDTH, D_CONV)) * CONV_WIDTH ** -0.5,
        "conv_gain": 1.0 + 0.02 * nrm(ks[4], (DEPTH, D_CONV)),
        "hg_lb_logits": 0.1 * nrm(ks[5], (DEPTH + 1, D_HG)),
        "hg_gain": 1.0 + 0.02 * nrm(ks[6], (DEPTH, HG_VD)),
        "w_out": nrm(ks[7], (DEPTH, D_MIX, D_MODEL)) * D_MIX ** -0.5,
        "norm_ffn": 1.0 + 0.02 * nrm(ks[8], (DEPTH, D_MODEL)),
        "peer_wq": nrm(ks[9], (DEPTH, D_MODEL, PEER_HEADS * D_QUERY)) * D_MODEL ** -0.5,
        "peer_keys": nrm(ks[10], (DEPTH, PEER_HEADS, 2, N_KEYS, HALF_Q)) * HALF_Q ** -0.5,
        "peer_u": nrm(ks[11], (DEPTH, N_EXPERTS, D_MODEL)) * D_MODEL ** -0.5,
        "peer_v": nrm(ks[12], (DEPTH, N_EXPERTS, D_MODEL)) * PEER_HEADS ** -0.5,
        "norm_f": 1.0 + 0.02 * nrm(ks[13], (D_MODEL,)),
    }

def second_block(x, norm_mix, w_in, conv_w, conv_gain, hg_lb_logits, hg_gain, w_out,
              norm_ffn, peer_wq, peer_keys, peer_u, peer_v, norm_f):
    lb_all = jnp.cumsum(jax.nn.softmax(hg_lb_logits.astype(jnp.float32), axis=0), axis=0)
    splits = [D_CONV, 2 * D_CONV, 3 * D_CONV, 3 * D_CONV + D_HG, 3 * D_CONV + 2 * D_HG, 3 * D_CONV + 3 * D_HG]
    for l in range(DEPTH):
        h = rmsnorm(x, norm_mix[l])
        proj = h @ w_in[l]
        c_gate, hc, b_gate, q, f_pre, v, g = jnp.split(proj, splits, axis=-1)
        conv_out = short_conv_mixer(c_gate, hc, b_gate, conv_w[l], conv_gain[l])
        hg_out = hgrn2_mixer(q, f_pre, v, g, lb_all[l], hg_gain[l])
        mix = jnp.concatenate([conv_out, hg_out], axis=-1)
        x = x + mix @ w_out[l]
        h2 = rmsnorm(x, norm_ffn[l])
        x = x + peer_ffn(h2, peer_wq[l], peer_keys[l], peer_u[l], peer_v[l])
    return rmsnorm(x, norm_f)


def setup_inputs(seed=0):
    out = dict(first_inputs(seed))
    for name, value in second_inputs(seed + 1).items():
        if name != "x":
            out[name + "_2"] = value
    return out


def reference(
    x, norm1_g, w_in, b_in, cmp_pe, cmp_k_w1, cmp_k_w2, cmp_v_w1, cmp_v_w2, w_pa, w_pb, w_pc,
    w_o, norm2_g, w_up, conv_w, conv_b, w_down, final_g, norm_mix_2, w_in_2, conv_w_2,
    conv_gain_2, hg_lb_logits_2, hg_gain_2, w_out_2, norm_ffn_2, peer_wq_2, peer_keys_2,
    peer_u_2, peer_v_2, norm_f_2,
):
    x = first_block(
        x, norm1_g, w_in, b_in, cmp_pe, cmp_k_w1, cmp_k_w2, cmp_v_w1, cmp_v_w2, w_pa, w_pb,
        w_pc, w_o, norm2_g, w_up, conv_w, conv_b, w_down, final_g,
    )
    return second_block(
        x, norm_mix_2, w_in_2, conv_w_2, conv_gain_2, hg_lb_logits_2, hg_gain_2, w_out_2,
        norm_ffn_2, peer_wq_2, peer_keys_2, peer_u_2, peer_v_2, norm_f_2,
    )


_drawn_inputs = setup_inputs


def setup_inputs(seed=0):
    import zlib

    import numpy as np

    out = dict(_drawn_inputs(seed))
    spreads = {}
    factors = {'norm1_g': 2.678,
     'cmp_pe': 4.601,
     'conv_gain_2': 32.67,
     'hg_lb_logits_2': 5.667,
     'hg_gain_2': 50.961,
     'norm_f_2': 21.362,
     'norm2_g': 3.677,
     'conv_b': 5.22,
     'norm_ffn_2': 18.71}
    for name, (base, spread) in spreads.items():
        noise = np.random.default_rng([zlib.crc32(name.encode()), seed]).standard_normal(out[name].shape)
        drawn = base * np.exp(spread * noise) if base else spread * noise
        out[name] = __import__('jax').numpy.asarray(drawn.astype(out[name].dtype))
    for name, factor in factors.items():
        out[name] = (out[name] * factor).astype(out[name].dtype)
    return out
```

```python
from contextlib import ExitStack

import numpy as np
import concourse.bass as bass
from concourse import mybir

ALU = mybir.AluOpType
ACT = mybir.ActivationFunctionType
F32 = mybir.dt.float32
U32 = mybir.dt.uint32
AX = mybir.AxisListType.X

P = 128
S = 512
D = 1024
NT = S // P
NEG = -1e30
TINY = 1e-30
FF = 2816
NFF = FF // P

QA, KA, VA, FA = 0, 256, 512, 768
QB, KB, VB = 772, 1156, 1540
QC, KC, VC, KSL, VSL, KWN, VWN, GC, GATES = 1924, 2308, 2436, 2564, 2692, 2820, 2948, 3076, 3094

COL = {}
_at = 0
for _name, _n in (("g1", 8), ("b_qa", 2), ("b_ka", 2), ("b_qb", 3), ("b_kb", 3), ("b_qc", 3), ("b_kc", 1),
                  ("b_vc", 1), ("b_ksl", 1), ("b_kwn", 1), ("b_fa", 1), ("b_gate", 24), ("g2", 8),
                  ("cw", 66), ("cb", 22), ("gm2", 8), ("cw2", 12), ("cg2", 4), ("lb", 8), ("hg", 1),
                  ("gf2", 8), ("pe", 32)):
    COL[_name] = _at
    _at += _n
NCOL = _at

ROW = {}
_at = 0
for _name, _n in (("bv", 914), ("final_g", 1024), ("norm_ffn", 1024), ("norm_f", 1024)):
    ROW[_name] = _at
    _at += _n
NROW = _at

CON = {}
_at = 0
for _name, _n in (("ident", 128), ("iota", 16), ("eps", 1), ("tab", 13 * 512), ("ctab", 768), ("cmask", 768),
                  ("hmask", 128), ("smask", 512), ("blk", 128), ("all", 128)):
    CON[_name] = _at
    _at += _n
NCON = _at


def constants():
    c = np.zeros((P, NCON), np.float32)
    p = np.arange(P)
    c[:, CON["ident"]:CON["ident"] + P] = np.eye(P, dtype=np.float32)
    c[:, CON["iota"]:CON["iota"] + 16] = np.arange(16, dtype=np.float32)
    c[:, CON["eps"]] = 1e-6
    slopes = np.exp2(-8.0 * np.arange(1, 13, dtype=np.float32) / 12).astype(np.float32)
    dist = p[:, None] - (np.arange(512)[None, :] - 384)
    dil, nsa = slopes[0::2], slopes[1::2]
    tabs = [np.where(dist >= 0, 0.0, NEG)]
    for h in range(6):
        w, r = ((128, 1), (512, 4), (2048, 16))[h // 2]
        ok = (dist >= 0) & (dist <= w) & (dist % r == 0)
        tabs.append(np.where(ok, -dil[h] * dist.astype(np.float32), NEG))
    for h in range(6):
        tabs.append(np.where(dist >= 0, -nsa[h] * dist.astype(np.float32), NEG))
    c[:, CON["tab"]:CON["tab"] + 13 * 512] = np.concatenate(tabs, 1).astype(np.float32)
    ct = np.full((P, 2, NT, 3, 32), NEG, np.float32)
    cm = np.zeros((P, 2, NT, 3, 32), np.float32)
    end = np.arange(31) * 16 + 31
    for par in range(2):
        for i in range(NT):
            d = (i * P + p)[:, None] - end[None, :]
            for hh in range(3):
                ct[:, par, i, hh, :31] = np.where(d >= 0, -nsa[2 * hh + par] * d.astype(np.float32), NEG)
                cm[:, par, i, hh, :31] = d >= 0
    c[:, CON["ctab"]:CON["ctab"] + 768] = ct.reshape(P, 768)
    c[:, CON["cmask"]:CON["cmask"] + 768] = cm.reshape(P, 768)
    c[:, CON["hmask"]:CON["hmask"] + P] = (p[:, None] // 32 == p[None, :] // 32) & (p[:, None] <= p[None, :])
    c[:, CON["smask"]:CON["smask"] + 512] = np.arange(512) % 32 != 0
    c[:, CON["blk"]:CON["blk"] + P] = (p[:, None] // 64 == p[None, :] // 64) / 64.0
    c[:, CON["all"]:CON["all"] + P] = 1 / 128.0
    return c


class Queue:

    def __init__(self, sem):
        self.sem, self.n, self.ops, self.seen = sem, 0, [], {}

    def wait(self, *tokens):
        for t in tokens:
            if t is None:
                continue
            if isinstance(t, list):
                self.wait(*t)
                continue
            sem, value = t
            if self.seen.get(id(sem), 0) >= value:
                continue
            self.seen[id(sem)] = value
            self.ops.append(lambda e, sem=sem, value=value: e.wait_ge(sem, value))

    def __call__(self, fn, *tokens):
        self.wait(*tokens)
        self.n += 1
        self.ops.append(lambda e: fn(e).then_inc(self.sem, 1))
        return (self.sem, self.n)

    def quiet(self, fn, *tokens):
        self.wait(*tokens)
        self.ops.append(fn)

    def dma(self, fn, sem, *tokens):
        self.wait(*tokens)
        sem[1] += 16
        self.ops.append(lambda e, s=sem[0]: fn(e).then_inc(s, 16))
        return (sem[0], sem[1])

    @property
    def last(self):
        return (self.sem, self.n)


def build(nc, a):
    ctx = ExitStack()
    with ctx:
        def newsem(name):
            return ctx.enter_context(nc.semaphore(name))

        arena = ctx.enter_context(nc.sbuf_tensor("arena", [P, 53000], F32))
        banks = [ctx.enter_context(nc.psum_tensor(f"bank{i}", [P, 512], F32)) for i in range(8)]
        PE, DVE, AC, GP, SP = (Queue(newsem(n)) for n in ("s_pe", "s_dve", "s_act", "s_pool", "s_sp"))
        block = ctx.enter_context(nc.Block())

        top = [0]

        def carve(*shape):
            n = 1
            for s in shape:
                n *= s
            at = top[0]
            top[0] += n
            assert top[0] <= 53000, top[0]
            v = arena[:, at:at + n]
            if len(shape) == 2:
                v = v.rearrange("p (a b) -> p a b", a=shape[0])
            elif len(shape) == 3:
                v = v.rearrange("p (a b c) -> p a b c", a=shape[0], b=shape[1])
            elif len(shape) == 4:
                v = v.rearrange("p (a b c d) -> p a b c d", a=shape[0], b=shape[1], c=shape[2])
            return v

        X = carve(NT, D)
        HTF = carve(8 * S)
        HT = HTF.rearrange("p (c n) -> p c n", c=8)
        COLS = carve(NCOL)
        FIX = carve(145)
        IDENT, IOTA, EPS = FIX[:, 0:128], FIX[:, 128:144], FIX[:, 144:145]
        SS = carve(16)
        RING = 4
        ring = [carve(2048) for _ in range(RING)]
        XS = [carve(D) for _ in range(2)]
        base = top[0]

        def col(name, j=0, n=1):
            return COLS[:, COL[name] + j:COL[name] + j + n]

        def con(name, n, off=0):
            return a["con"][:, CON[name] + off:CON[name] + off + n]

        psum_at = [0]
        psum_readers = [[] for _ in range(8)]

        held = set()

        def bank():
            while psum_at[0] % 8 in held:
                psum_at[0] += 1
            b = psum_at[0] % 8
            psum_at[0] += 1
            w = psum_readers[b]
            psum_readers[b] = []
            return b, w

        def free(b, *tokens):
            psum_readers[b] += tokens

        def kcols(w, c0, n):
            return [(w.rearrange("(c p) n -> p c n", p=P)[:, :, c0:c0 + n], 8, 0, n)]

        w_in, w_in2 = a["w_in"], a["w_in_2"]
        FEAT1 = [("qa", QA, 256), ("ka", KA, 256), ("qb", QB, 256), ("qb", QB + 256, 128),
                 ("kb", KB, 256), ("kb", KB + 256, 128), ("qc", QC, 256), ("qc", QC + 256, 128),
                 ("kvc", KC, 256), ("ksl", KSL, 128), ("kwn", KWN, 128), ("fa", FA, 4)]
        TOK1 = [(VA, 256, 0), (VB, 256, 256), (VB + 256, 128, 512), (VSL, 128, 640), (VWN, 146, 768)]
        plan = [(kcols(w_in, c0, n), n) for _, c0, n in FEAT1]
        plan += [(kcols(w_in, c0, n), n) for c0, n, _ in TOK1]
        for w in (a["cmp_k_w1"], a["cmp_v_w1"]):
            for half in range(2):
                plan.append(([(w.rearrange("(c p) n -> p c n", p=P)[:, half * 8:half * 8 + 8, :], 8, 0, 256)], 256))
        for mm in range(4):
            parts = [(a["w_pa"], 0, 2), (a["w_pb"], 2, 3), (a["w_pc"], 5, 3)]
            plan.append(([(w.rearrange("(c p) n -> p c n", p=P)[:, :, mm * 256:mm * 256 + 256], k, c, 256)
                          for w, c, k in parts], 256))
            for j in range(3):
                plan.append((kcols(w_in, GATES + j * D + mm * 256, 256), 256))
        plan += [(kcols(a["w_o"], c * 256, 256), 256) for c in range(4)]
        for j in range(11):
            plan += [(kcols(a["w_up"], j * 256, 256), 256), (kcols(a["w_up"], FF + j * 256, 256), 256)]
        DOWN = [(0, 4), (4, 4), (8, 4), (12, 4), (16, 4), (20, 2)]
        for half in range(2):
            for k0, kn in DOWN:
                plan.append(([(a["w_down"].rearrange("(c p) n -> p c n", p=P)
                               [:, k0:k0 + kn, half * 512:half * 512 + 512], kn, 0, 512)], 512))
        for j in range(2):
            plan += [(kcols(w_in2, s * 512 + j * 256, 256), 256) for s in (0, 1, 2)]
        plan += [(kcols(w_in2, c0, 256), 256) for c0 in (1536, 1792, 3072, 3328, 2048, 2304)]
        plan += [(kcols(w_in2, 2560 + j * 256, 256), 256) for j in range(2)]
        plan += [(kcols(a["w_out_2"], c * 256, 256), 256) for c in range(4)]
        plan += [(kcols(a["peer_wq_2"], c * 256, 256), 256) for c in range(8)]

        ring_sem = [[newsem(f"s_w{i}"), 0] for i in range(RING)]
        landed = {}
        nxt = [0]

        def load_weights(i, *tokens):
            if i >= len(plan):
                return
            parts, width = plan[i]
            s = i % RING
            for src, k, c, w in parts:
                dst = ring[s].rearrange("p (c n) -> p c n", n=256 if width <= 256 else 512)[:, c:c + k, 0:w]
                landed[i] = SP.dma(lambda e, dst=dst, src=src: e.dma_start(dst, src), ring_sem[s], *tokens)

        def weights():
            i = nxt[0]
            nxt[0] += 1
            width = plan[i][1]
            return i, ring[i % RING].rearrange("p (c n) -> p c n", n=256 if width <= 256 else 512), landed[i]

        def done(i, token):
            load_weights(i + RING, token)

        def barrier():
            lasts = [q.last for q in (PE, DVE, AC, GP)]
            for q in (PE, DVE, AC, GP, SP):
                q.wait(*lasts)

        def mm(out, lhsT, rhs, start, stop):
            return lambda e: e.matmul(out, lhsT, rhs, start=start, stop=stop)

        small = [newsem("s_small"), 0]
        big = [newsem("s_tab"), 0]
        x_sem = [[newsem(f"s_x{t}"), 0] for t in range(NT)]

        xv = a["x"].rearrange("(t p) d -> t p d", p=P)
        x_in = [AC.dma(lambda e, t=t: e.dma_start(X[:, t, :], xv[t]), x_sem[t]) for t in range(NT)]
        for dst, src in ((COLS, a["cols"]), (FIX, con("ident", 145))):
            t_small = AC.dma(lambda e, dst=dst, src=src: e.dma_start(dst, src), small)
        for i in range(RING):
            load_weights(i)

        QK = carve(19, S)
        VT = carve(NT, 914)
        TAB = carve(13, 512)
        BV = carve(914)
        SEL = carve(4, P)
        FS = carve(3, 512)
        Y = carve(NT, D)
        NM = carve(22, NT)
        LS = carve(22, NT)
        RL = carve(22, NT)
        CQ = carve(NT, 4)
        AL = carve(4, NT, 6)
        GS = carve(NT, 18)
        early = top[0]
        CT = carve(2, NT, 3, 32)
        CM = carve(2, NT, 3, 32)
        FB = carve(2, 16, 62)
        HID = carve(2, 2, 62)
        KCT = carve(62)
        VCB = carve(2, 192)
        CE = carve(2, NT, 3, 32)
        CS = carve(2, NT, 3)
        PCT = carve(2, NT, P)
        W2 = [carve(2, 64), carve(2, 64)]
        top[0] = early
        PB = [carve(512) for _ in range(3)]
        PT = [carve(512) for _ in range(3)]
        FT = [carve(512) for _ in range(2)]

        for dst, src in ((TAB, con("tab", 13 * 512).rearrange("p (a b) -> p a b", a=13)),
                         (BV, a["rows"][0:1, ROW["bv"]:ROW["bv"] + 914].to_broadcast([P, 914])),
                         (CT, con("ctab", 768).rearrange("p (a b c d) -> p a b c d", a=2, b=NT, c=3)),
                         (CM, con("cmask", 768).rearrange("p (a b c d) -> p a b c d", a=2, b=NT, c=3))):
            t_tab = AC.dma(lambda e, dst=dst, src=src: e.dma_start(dst, src), big)

        def rms(t, ready, ss):
            k = AC(lambda e: e.activation(XS[t % 2], X[:, t, :], ACT.Square, accum_out=SS[:, ss:ss + 1]),
                   ready, t_small, xs_free[t % 2])
            k = AC(lambda e: e.activation(SS[:, ss + 4:ss + 5], SS[:, ss:ss + 1], ACT.Sqrt, bias=EPS, scale=1.0 / D), k)
            return DVE(lambda e: e.reciprocal(SS[:, ss + 8:ss + 9], SS[:, ss + 4:ss + 5]), k)

        xs_free = [[], []]

        def norm_to_ht(gain, ready, keep=None):
            out = []
            for t in range(NT):
                k = rms(t, ready[t], t)
                k = DVE(lambda e, t=t: e.tensor_scalar(XS[t % 2], X[:, t, :], SS[:, t + 8:t + 9], None, ALU.mult), k)
                tr = [keep(t, k)] if keep is not None else []
                for half in range(2):
                    b, w = bank()
                    for c in range(4):
                        src = XS[t % 2][:, (half * 4 + c) * P:(half * 4 + c + 1) * P]
                        k2 = PE(lambda e, b=b, c=c, src=src: e.transpose(banks[b][:, c * P:(c + 1) * P], src, IDENT),
                                k, *w)
                    tr.append(k2)
                    dst = HT[:, half * 4:half * 4 + 4, t * P:(t + 1) * P]
                    g = col(gain, half * 4, 4).unsqueeze(2).to_broadcast([P, 4, P])
                    src = banks[b][:, :].rearrange("p (c n) -> p c n", c=4)
                    k3 = DVE(lambda e, dst=dst, src=src, g=g: e.tensor_tensor(dst, src, g, ALU.mult), k2, t_small)
                    free(b, k3)
                    out.append(k3)
                xs_free[t % 2] = tr
            return out[-1]

        ht_ready = norm_to_ht("g1", x_in)

        def proj_feat(w, j, n, ready, *extra):
            b, bw = bank()
            for c in range(8):
                k = PE.quiet(mm(banks[b][0:n, :], w[:, c, j * P:j * P + n], HT[:, c, :], c == 0, c == 7),
                             ready, *extra, *bw) if c < 7 else \
                    PE(mm(banks[b][0:n, :], w[:, c, j * P:j * P + n], HT[:, c, :], c == 0, c == 7))
            return b, k

        slot = {"qa": 0, "ka": 2, "qb": 4, "kb": 7, "qc": 10, "kvc": 13, "ksl": 15, "kwn": 17}
        seen = {}
        for name, c0, n in FEAT1:
            i, w, tw = weights()
            for j in range((n + P - 1) // P):
                b, k = proj_feat(w, j, min(n, P), ht_ready, tw)
                if name == "fa":
                    bias = COLS[0:4, COL["b_fa"]:COL["b_fa"] + 1]
                    ev = [DVE(lambda e, b=b, bias=bias: e.tensor_scalar(FS[0:4, 0, :], banks[b][0:4, :], bias, None,
                                                                        ALU.add), k)]
                    fa_ready = ev
                elif name in ("ksl", "kwn"):
                    ev = []
                    for g in range(2):
                        for half in range(2):
                            dst = QK[half * 64:half * 64 + 64, slot[name] + g, :]
                            src = banks[b][g * 64:g * 64 + 64, :]
                            bias = COLS[g * 64:g * 64 + 64, COL["b_" + name]:COL["b_" + name] + 1]
                            ev.append(DVE(lambda e, dst=dst, src=src, bias=bias:
                                          e.tensor_scalar(dst, src, bias, None, ALU.add), k))
                else:
                    m = seen.get(name, 0)
                    seen[name] = m + 1
                    bias = col("b_" + name, m) if name != "kvc" else col("b_kc" if m == 0 else "b_vc")
                    dst = QK[:, slot[name] + m, :]
                    if name[0] == "q":
                        ev = [DVE(lambda e, dst=dst, b=b, bias=bias:
                                  e.tensor_scalar(dst, banks[b][:, :], bias, 0.125, ALU.add, ALU.mult), k)]
                    else:
                        ev = [AC(lambda e, dst=dst, b=b, bias=bias:
                                 e.activation(dst, banks[b][:, :], ACT.Identity, bias=bias), k)]
                free(b, *ev)
            done(i, k)

        for c0, n, off in TOK1:
            i, w, tw = weights()
            for t in range(NT):
                b, bw = bank()
                for c in range(7):
                    PE.quiet(mm(banks[b][:, 0:n], HT[:, c, t * P:(t + 1) * P], w[:, c, 0:n], c == 0, False), tw, *bw)
                k = PE(mm(banks[b][:, 0:n], HT[:, 7, t * P:(t + 1) * P], w[:, 7, 0:n], False, True))
                ev = DVE(lambda e, b=b, t=t, n=n, off=off: e.tensor_tensor(
                    VT[:, t, off:off + n], banks[b][:, 0:n], BV[:, off:off + n], ALU.add), k, t_tab)
                free(b, ev)
            done(i, k)
        vt_ready = ev

        gs_ready = AC(lambda e: e.activation(GS, VT[:, :, 896:914], ACT.Sigmoid), vt_ready)

        fb_ready = []
        for kv in range(2):
            for g in range(2):
                for par in range(2):
                    src = QK[g * 64:g * 64 + 64, 13 + kv, :]
                    for hf in range(2):
                        lo = 16 * hf
                        v = src[:, lo:lo + 496].rearrange("p (c l q) -> p l c q", l=8, q=2)[:, :, :, par]
                        pe = COLS[g * 64:g * 64 + 64, COL["pe"] + lo:COL["pe"] + lo + 16]
                        pe = pe.rearrange("p (l q) -> p l q", q=2)[:, :, par].unsqueeze(2).to_broadcast([64, 8, 31])
                        dst = FB[par * 64:par * 64 + 64, kv, hf * 8:hf * 8 + 8, g * 31:g * 31 + 31]
                        fb_ready.append(DVE(lambda e, dst=dst, v=v, pe=pe: e.tensor_tensor(dst, v, pe, ALU.add),
                                            DVE.last, AC.last))
        hid_ready = []
        for kv in range(2):
            two = [weights(), weights()]
            for m in range(2):
                b, bw = bank()
                for c in range(16):
                    i, w, tw = two[c // 8]
                    op = mm(banks[b][:, 0:62], w[:, c % 8, m * P:m * P + P], FB[:, kv, c, :], c == 0, c == 15)
                    PE.wait(tw, *bw, fb_ready)
                    if c == 15:
                        k = PE(op)
                    else:
                        PE.quiet(op)
                ev = AC(lambda e, b=b, kv=kv, m=m: e.activation(HID[:, kv, m, :], banks[b][:, 0:62],
                                                                ACT.Gelu_apprx_tanh), k)
                free(b, ev)
                hid_ready.append(ev)
            done(two[0][0], k)
            done(two[1][0], k)
        w2_sem = [newsem("s_cmpw"), 0]
        t_w2 = [AC.dma(lambda e, n=n, j=j: e.dma_start(W2[j], a[n].rearrange("(c p) n -> p c n", p=P)), w2_sem)
                for j, n in enumerate(("cmp_k_w2", "cmp_v_w2"))][-1]
        b, bw = bank()
        PE.quiet(mm(banks[b][0:64, 0:62], W2[0][:, 0, :], HID[:, 0, 0, :], True, False), *bw, hid_ready, t_w2)
        k = PE(mm(banks[b][0:64, 0:62], W2[0][:, 1, :], HID[:, 0, 1, :], False, True))
        kct_ready = [DVE(lambda e, b=b, h=h: e.tensor_copy(KCT[h * 64:h * 64 + 64, :], banks[b][0:64, 0:62]), k)
                     for h in range(2)]
        free(b, *kct_ready)
        vcb0 = DVE(lambda e: e.memset(VCB, 0.0))
        vcb_ready = []
        for g in range(2):
            b, bw = bank()
            PE.quiet(mm(banks[b][0:31, 0:64], HID[:, 1, 0, g * 31:g * 31 + 31], W2[1][:, 0, :], True, False), *bw)
            k = PE(mm(banks[b][0:31, 0:64], HID[:, 1, 1, g * 31:g * 31 + 31], W2[1][:, 1, :], False, True))
            ev = []
            for h in range(3 * g, 3 * g + 3):
                par, hh = h % 2, h // 2
                ev.append(DVE(lambda e, b=b, par=par, hh=hh: e.tensor_copy(
                    VCB[hh * 32:hh * 32 + 31, par, hh * 64:hh * 64 + 64], banks[b][0:31, 0:64]), k, vcb0))
            free(b, *ev)
            vcb_ready += ev

        ce_ready = []
        for par in range(2):
            b, bw = bank()
            for i in range(NT):
                for hh in range(3):
                    h = 2 * hh + par
                    g = h // 3
                    out = banks[b][:, (i * 3 + hh) * 32:(i * 3 + hh) * 32 + 31]
                    q = QK[par * 64:par * 64 + 64, 10 + hh, i * P:(i + 1) * P]
                    k = PE(mm(out, q, KCT[par * 64:par * 64 + 64, g * 31:g * 31 + 31], True, True), *bw, kct_ready)
            src = banks[b][:, 0:384].rearrange("p (i h c) -> p i h c", i=NT, h=3)
            z = DVE(lambda e, par=par: e.memset(CE[:, par, :, :, :], 0.0))
            k = DVE(lambda e, par=par, src=src: e.tensor_tensor(
                CE[:, par, :, :, 0:31], src[:, :, :, 0:31], CT[:, par, :, :, 0:31], ALU.add), k, z, t_tab)
            free(b, k)
            ce = CE[:, par, :, :, :].rearrange("p i h c -> p (i h) c")
            cs = CS[:, par, :, :].rearrange("p i h -> p (i h)")
            k = DVE(lambda e, ce=ce, cs=cs: e.tensor_reduce(cs, ce[:, :, 0:31], AX, ALU.max), k)
            k = DVE(lambda e, ce=ce, cs=cs: e.tensor_tensor(
                ce[:, :, 0:31], ce[:, :, 0:31], cs.unsqueeze(2).to_broadcast([P, 12, 31]), ALU.subtract), k)
            k = AC(lambda e, ce=ce: e.activation(ce[:, :, 0:31], ce[:, :, 0:31], ACT.Exp), k)
            cm = CM[:, par, :, :, :].rearrange("p i h c -> p (i h) c")
            k = DVE(lambda e, ce=ce, cm=cm: e.tensor_tensor(ce, ce, cm, ALU.mult), k)
            k = DVE(lambda e, ce=ce, cs=cs: e.tensor_reduce(cs, ce, AX, ALU.add), k)
            k = DVE(lambda e, cs=cs: e.tensor_scalar(cs, cs, TINY, None, ALU.max), k)
            k = DVE(lambda e, cs=cs: e.reciprocal(cs, cs), k)
            gate = GS.rearrange("p i (h q b) -> p i h q b", q=2, b=3)[:, :, :, par, 0]
            k = DVE(lambda e, par=par, gate=gate: e.tensor_tensor(
                CS[:, par, :, :], CS[:, par, :, :], gate, ALU.mult), k, gs_ready)
            k = DVE(lambda e, ce=ce, cs=cs: e.tensor_tensor(
                ce, ce, cs.unsqueeze(2).to_broadcast([P, 12, 32]), ALU.mult), k)
            ce_ready.append(k)
        y_c0 = []
        for par in range(2):
            b, bw = bank()
            for i in range(NT):
                k = PE(lambda e, b=b, i=i, par=par: e.transpose(
                    banks[b][0:96, i * P:(i + 1) * P], CE[:, par, i, :, :].rearrange("p h c -> p (h c)"), IDENT),
                    *bw, ce_ready[par])
            pct = AC(lambda e, b=b, par=par: e.copy(PCT[0:96, par, :, :].rearrange("p i n -> p (i n)"),
                                                    banks[b][0:96, :]), k)
            free(b, pct)
            for i in range(NT):
                b, bw = bank()
                k = PE(mm(banks[b][:, 0:192], PCT[0:96, par, i, :], VCB[0:96, par, :], True, True),
                       *bw, pct, vcb_ready)
                y = Y[:, i, 640:1024].rearrange("p (h q d) -> p h q d", q=2, d=64)[:, :, par, :]
                k = DVE(lambda e, b=b, y=y: e.tensor_copy(
                    y, banks[b][:, 0:192].rearrange("p (h d) -> p h d", h=3)), k)
                free(b, k)
                y_c0.append(k)

        FSr = [FS[0:4, j, :] for j in range(3)]
        k = AC(lambda e: e.activation(FSr[1], FSr[0], ACT.Abs), fa_ready)
        k = AC(lambda e: e.activation(FSr[1], FSr[1], ACT.Exp, scale=-1.0), k)
        k1 = AC(lambda e: e.activation(FSr[1], FSr[1], ACT.Ln, bias=1.0), k)
        k = DVE(lambda e: e.tensor_scalar(FSr[0], FSr[0], -1.0, 0.0, ALU.mult, ALU.max), fa_ready, k1)
        k = DVE(lambda e: e.tensor_tensor(FSr[1], FSr[1], FSr[0], ALU.add), k, k1)
        k2 = DVE(lambda e: e.memset(FSr[0], 1.0), k)
        cneg = DVE(lambda e: e.tensor_tensor_scan(FSr[2], FSr[0], FSr[1], 0.0, ALU.mult, ALU.add), k, k2)
        b, bw = bank()
        for i in range(NT):
            k = PE(lambda e, b=b, i=i: e.transpose(banks[b][:, i * 4:i * 4 + 4], FS[0:4, 2, i * P:(i + 1) * P],
                                                   IDENT[0:4, 0:4]), *bw, cneg)
        cq_ready = DVE(lambda e, b=b: e.tensor_copy(CQ.rearrange("p i h -> p (i h)"), banks[b][:, 0:16]), k)
        free(b, cq_ready)
        sel_ready = DVE(lambda e: e.tensor_copy(
            SEL[0:4, :, :], IDENT[0:4, 0:4].unsqueeze(2).to_broadcast([4, 4, P])), t_small)
        barrier()

        heads = []
        for h in range(4):
            heads.append(("fox", h, (0 + h // 2, h % 2), 2 + h // 2, h * 64, h * 64, 0))
        for h in range(6):
            heads.append(("dil", h, (4 + h // 2, h % 2), 7 + h // 2, 256 + h * 64, 256 + h * 64, 1 + h))
        for h in range(6):
            heads.append(("sel", h, (10 + h // 2, h % 2), 15 + h // 3, 640 + (h // 3) * 64, 640 + h * 64, 7 + h))
        for h in range(6):
            heads.append(("win", h, (10 + h // 2, h % 2), 17 + h // 3, 768 + (h // 3) * 64, 640 + h * 64, 7 + h))
        units = [(n, hd, i) for n, hd in enumerate(heads) for i in range(NT)]
        st = {}
        pb_free = [[], [], []]
        pt_free = [[], [], []]
        ft_free = [[], []]
        fox_n = [0]
        fox_bank = []
        y_done = {}

        def scores(u):
            n, (kind, h, (qs, par), ks, _, _, tab), i = units[u]
            j0 = max(0, i - 1) if kind == "dil" and h < 2 else 0
            w = (i + 1 - j0) * P
            b, bw = bank()
            q = QK[par * 64:par * 64 + 64, qs, i * P:(i + 1) * P]
            kk = QK[par * 64:par * 64 + 64, ks, j0 * P:(i + 1) * P]
            k = PE(mm(banks[b][:, 0:w], q, kk, True, True), *bw)
            t = TAB[:, tab, 384 - P * (i - j0):512]
            ready = None
            if kind == "fox":
                if i == 0:
                    cb, cw = bank()
                    held.add(cb)
                    fox_bank[:] = [cb, PE(mm(banks[cb][:, :], SEL[0:4, h, :], FS[0:4, 2, :], True, True), *cw)]
                cb = fox_bank[0]
                f = fox_n[0] % 2
                fox_n[0] += 1
                dst = FT[f][:, 0:w]
                ready = DVE(lambda e: e.tensor_scalar(dst, banks[cb][:, 0:w], CQ[:, i, h:h + 1], None, ALU.subtract),
                            fox_bank[1], cq_ready, ft_free[f], t_tab)
                if i == NT - 1:
                    held.discard(cb)
                    free(cb, ready)
                ready = DVE(lambda e, t=t: e.tensor_tensor(dst, dst, t, ALU.add), ready)
                t = dst
            s = PB[u % 3][:, 0:w]
            k = DVE(lambda e: e.tensor_tensor_reduce(out=s, in0=banks[b][:, 0:w], in1=t, scale=-1.0, scalar=3.0e38,
                                                     op0=ALU.add, op1=ALU.min, accum_out=NM[:, n, i:i + 1]),
                    k, ready, pb_free[u % 3], t_tab)
            free(b, k)
            if kind == "fox":
                ft_free[f] = [k]
            k = AC(lambda e: e.activation(s, s, ACT.Exp, bias=NM[:, n, i:i + 1], scale=-1.0,
                                          accum_out=LS[:, n, i:i + 1]), k)
            r = DVE(lambda e: e.reciprocal(RL[:, n, i:i + 1], LS[:, n, i:i + 1]), k)
            if kind in ("sel", "win"):
                g = GS[:, i, h * 3 + (1 if kind == "sel" else 2):h * 3 + (2 if kind == "sel" else 3)]
                r = DVE(lambda e: e.tensor_tensor(RL[:, n, i:i + 1], RL[:, n, i:i + 1], g, ALU.mult), r, gs_ready)
            st[u] = (j0, w, k, r)

        def turn(u):
            j0, w, k, r = st[u]
            b, bw = bank()
            for j in range(w // P):
                k2 = PE(lambda e, j=j: e.transpose(banks[b][:, j * P:(j + 1) * P], PB[u % 3][:, j * P:(j + 1) * P],
                                                   IDENT), k, *bw)
            pb_free[u % 3] = [k2]
            if u % 2:
                k3 = AC(lambda e: e.copy(PT[u % 3][:, 0:w], banks[b][:, 0:w]), k2, pt_free[u % 3])
            else:
                k3 = DVE(lambda e: e.tensor_copy(PT[u % 3][:, 0:w], banks[b][:, 0:w]), k2, pt_free[u % 3])
            free(b, k3)
            st[u] = (j0, w, k3, r)

        def values(u):
            n, (kind, h, _, _, vc, yc, _), i = units[u]
            j0, w, k, r = st.pop(u)
            b, bw = bank()
            nb = w // P
            for j in range(nb):
                op = mm(banks[b][:, 0:64], PT[u % 3][:, j * P:(j + 1) * P], VT[:, j0 + j, vc:vc + 64],
                        j == 0, j == nb - 1)
                PE.wait(k, *bw)
                if j == nb - 1:
                    k2 = PE(op)
                else:
                    PE.quiet(op)
            pt_free[u % 3] = [k2]
            y = Y[:, i, yc:yc + 64]
            rl = RL[:, n, i:i + 1]
            if kind in ("sel", "win"):
                k3 = DVE(lambda e: e.scalar_tensor_tensor(y, banks[b][:, 0:64], rl, y, ALU.mult, ALU.add),
                         k2, r, y_c0, y_done.get((i, yc)))
            else:
                k3 = DVE(lambda e: e.tensor_scalar(y, banks[b][:, 0:64], rl, None, ALU.mult), k2, r)
            free(b, k3)
            y_done[i, yc] = k3

        for u in range(len(units) + 3):
            if u < len(units):
                scores(u)
            if 2 <= u and u - 2 < len(units):
                turn(u - 2)
            if 3 <= u:
                values(u - 3)

        k = AC(lambda e: e.activation(AL[:, 0, :, :], LS[:, 4:10, :].rearrange("p h i -> p i h"), ACT.Ln), DVE.last)
        k = DVE(lambda e: e.tensor_tensor(AL[:, 0, :, :], AL[:, 0, :, :], NM[:, 4:10, :].rearrange("p h i -> p i h"),
                                          ALU.subtract), k)
        lse = AL[:, 0, :, :].rearrange("p i (g q) -> p i q g", q=2)
        mx = AL[:, 1, :, 0:2]
        k = DVE(lambda e: e.tensor_reduce(mx, lse, AX, ALU.max), k)
        w3 = AL[:, 2, :, :].rearrange("p i (g q) -> p i q g", q=2)
        k = DVE(lambda e: e.tensor_tensor(w3, lse, mx.unsqueeze(3).to_broadcast([P, NT, 2, 3]), ALU.subtract), k)
        k = AC(lambda e: e.activation(AL[:, 2, :, :], AL[:, 2, :, :], ACT.Exp), k)
        k = DVE(lambda e: e.tensor_reduce(mx, w3, AX, ALU.add), k)
        k = DVE(lambda e: e.reciprocal(mx, mx), k)
        k = DVE(lambda e: e.tensor_tensor(w3, w3, mx.unsqueeze(3).to_broadcast([P, NT, 2, 3]), ALU.mult), k)
        for i in range(NT):
            y = Y[:, i, 256:640].rearrange("p (h d) -> p h d", h=6)
            al = AL[:, 2, i, :].unsqueeze(2).to_broadcast([P, 6, 64])
            k2 = DVE(lambda e, y=y, al=al: e.tensor_tensor(y, y, al, ALU.mult), k, DVE.last)
        y_ready = k2

        barrier()
        YT = QK[:, 0:8, :]
        MG = QK[:, 8:16, :]
        GT = [PB[0], PB[1], PB[2]]
        yt_ready = []
        for t in range(NT):
            for half in range(2):
                b, bw = bank()
                for c in range(4):
                    src = Y[:, t, (half * 4 + c) * P:(half * 4 + c + 1) * P]
                    k = PE(lambda e, b=b, c=c, src=src: e.transpose(banks[b][:, c * P:(c + 1) * P], src, IDENT),
                           *bw, y_ready)
                dst = YT[:, half * 4:half * 4 + 4, t * P:(t + 1) * P]
                src = banks[b][:, :].rearrange("p (c n) -> p c n", c=4)
                if half:
                    ev = AC(lambda e, dst=dst, src=src: e.copy(dst, src), k)
                else:
                    ev = DVE(lambda e, dst=dst, src=src: e.tensor_copy(dst, src), k)
                free(b, ev)
                yt_ready.append(ev)

        gt_free = [[], [], []]
        mg_ready = []
        for m4 in range(4):
            wp = weights()
            wg = [weights() for _ in range(3)]
            for j2 in range(2):
                m = m4 * 2 + j2
                for j, (c0, cn) in enumerate(((0, 2), (2, 3), (5, 3))):
                    bg, kg = proj_feat(wg[j][1], j2, P, ht_ready, wg[j][2])
                    g = GT[j]
                    kg = AC(lambda e, bg=bg, g=g, m=m, j=j: e.activation(
                        g, banks[bg][:, :], ACT.Sigmoid, bias=col("b_gate", j * 8 + m)), kg, gt_free[j])
                    free(bg, kg)
                    b, bw = bank()
                    for c in range(cn):
                        op = mm(banks[b][:, :], wp[1][:, c0 + c, j2 * P:(j2 + 1) * P], YT[:, c0 + c, :],
                                c == 0, c == cn - 1)
                        PE.wait(wp[2], *bw, yt_ready)
                        k = PE(op)
                    if j == 0:
                        k = DVE(lambda e, b=b, g=g, m=m: e.tensor_tensor(MG[:, m, :], banks[b][:, :], g, ALU.mult),
                                k, kg)
                        km = k
                    else:
                        k = DVE(lambda e, b=b, g=g: e.tensor_tensor(g, banks[b][:, :], g, ALU.mult), k, kg)
                        km = DVE(lambda e, g=g, m=m: e.tensor_tensor(MG[:, m, :], MG[:, m, :], g, ALU.add), k, km)
                    free(b, k)
                    gt_free[j] = [km]
            mg_ready.append(km)
            for i, _, _ in [wp] + wg:
                done(i, PE.last)

        def add_rows(src, ready):
            out = [None] * NT
            for c4 in range(4):
                i, w, tw = weights()
                for t in range(NT):
                    b, bw = bank()
                    for c in range(8):
                        op = mm(banks[b][:, 0:256], src[:, c, t * P:(t + 1) * P], w[:, c, :], c == 0, c == 7)
                        PE.wait(tw, *bw, ready)
                        if c == 7:
                            k = PE(op)
                        else:
                            PE.quiet(op)
                    x = X[:, t, c4 * 256:c4 * 256 + 256]
                    out[t] = DVE(lambda e, b=b, x=x: e.tensor_tensor(x, x, banks[b][:, 0:256], ALU.add), k)
                    free(b, out[t])
                done(i, k)
            return out

        x_ready = add_rows(MG, mg_ready)
        ht_ready = norm_to_ht("g2", x_ready)

        barrier()
        top[0] = base
        UT = carve(NFF, S)
        AB = [carve(S) for _ in range(3)]
        FG = carve(D)
        fg_sem = [newsem("s_fg"), 0]
        t_fg = SP.dma(lambda e: e.dma_start(
            FG, a["rows"][0:1, ROW["final_g"]:ROW["final_g"] + D].to_broadcast([P, D])), fg_sem)
        ab_free = [[], [], []]
        for jb in range(11):
            wa, wb = weights(), weights()
            for j2 in range(2):
                m = jb * 2 + j2
                ba, ka = proj_feat(wa[1], j2, P, ht_ready, wa[2])
                bb, kb = proj_feat(wb[1], j2, P, ht_ready, wb[2])
                y = AB[m % 3]
                pa = banks[ba]
                k = AC(lambda e, y=y, pa=pa, m=m: e.activation(y, pa[:, :], ACT.Identity, bias=col("cb", m),
                                                              scale=col("cw", 44 + m)), ka, ab_free[m % 3])
                k = DVE(lambda e, y=y, pa=pa, m=m: e.scalar_tensor_tensor(
                    y[:, 1:S], pa[:, 0:S - 1], col("cw", 22 + m), y[:, 1:S], ALU.mult, ALU.add), k)
                k = DVE(lambda e, y=y, pa=pa, m=m: e.scalar_tensor_tensor(
                    y[:, 2:S], pa[:, 0:S - 2], col("cw", m), y[:, 2:S], ALU.mult, ALU.add), k)
                free(ba, k)
                k = AC(lambda e, y=y: e.activation(y, y, ACT.Gelu_apprx_tanh), k)
                k = DVE(lambda e, y=y, bb=bb, m=m: e.tensor_tensor(UT[:, m, :], y, banks[bb][:, :], ALU.mult), k, kb)
                free(bb, k)
                ab_free[m % 3] = [k]
            done(wa[0], kb)
            done(wb[0], kb)
        ut_ready = k
        for half in range(2):
            bs = [bank() for _ in range(NT)]
            for k0, kn in DOWN:
                i, w, tw = weights()
                for c in range(kn):
                    for t in range(NT):
                        PE.wait(tw, *bs[t][1], ut_ready)
                        k = PE(mm(banks[bs[t][0]][:, :], UT[:, k0 + c, t * P:(t + 1) * P], w[:, c, :],
                                  k0 + c == 0, k0 + c == NFF - 1))
                done(i, k)
            for t in range(NT):
                x = X[:, t, half * 512:half * 512 + 512]
                kx = DVE(lambda e, x=x, b=bs[t][0]: e.tensor_tensor(x, x, banks[b][:, :], ALU.add), k)
                free(bs[t][0], kx)
        x_ready = []
        for t in range(NT):
            k = rms(t, kx, t)
            k = DVE(lambda e, t=t: e.scalar_tensor_tensor(X[:, t, :], X[:, t, :], SS[:, t + 8:t + 9], FG,
                                                          ALU.mult, ALU.mult), k, t_fg)
            x_ready.append(k)
        ht_ready = norm_to_ht("gm2", x_ready)

        barrier()
        top[0] = base
        MIX = carve(8, S)
        HM, SM, BLK, ONE = carve(P), carve(512), carve(P), carve(P)
        for dst, name, n in ((HM, "hmask", P), (SM, "smask", 512), (BLK, "blk", P), (ONE, "all", P)):
            t_c2 = SP.dma(lambda e, dst=dst, name=name, n=n: e.dma_start(dst, con(name, n)), fg_sem)
        LB = carve(6, 4)
        TM = [carve(S) for _ in range(6)]
        QD, KD, KE, SG = carve(4, S), carve(4, S), carve(4, S), carve(4, S)
        FH = carve(4, S)
        V2 = carve(NT, S)
        EG = carve(4, S)
        DEC = carve(4, 16)
        KET = carve(NT, 4, P)
        ATB = carve(4, P)
        ST = carve(16, 4 * P)
        l0, l1 = col("lb", 0, 4), col("lb", 4, 4)
        k = DVE(lambda e: e.tensor_tensor(LB[:, 0, :], l0, l1, ALU.max))
        k1 = DVE(lambda e: e.tensor_tensor(LB[:, 1, :], l0, LB[:, 0, :], ALU.subtract), k)
        k1 = DVE(lambda e: e.tensor_tensor(LB[:, 2, :], l1, LB[:, 0, :], ALU.subtract), k, k1)
        k = AC(lambda e: e.activation(LB[:, 3:5, :], LB[:, 1:3, :], ACT.Exp), k1)
        k = DVE(lambda e: e.tensor_tensor(LB[:, 4, :], LB[:, 3, :], LB[:, 4, :], ALU.add), k)
        k = DVE(lambda e: e.reciprocal(LB[:, 4, :], LB[:, 4, :]), k)
        k = DVE(lambda e: e.tensor_tensor(LB[:, 0, :], LB[:, 3, :], LB[:, 4, :], ALU.mult), k)
        lb_ready = DVE(lambda e: e.tensor_scalar(LB[:, 5, :], LB[:, 0, :], -1.0, 1.0, ALU.mult, ALU.add), k)

        tm_free = None
        for j4 in range(2):
            wc, wh, wb = weights(), weights(), weights()
            for j2 in range(2):
                m = j4 * 2 + j2
                bc, kc = proj_feat(wc[1], j2, P, ht_ready, wc[2])
                bh, kh = proj_feat(wh[1], j2, P, ht_ready, wh[2])
                bb, kb = proj_feat(wb[1], j2, P, ht_ready, wb[2])
                u, y = TM[0], TM[1]
                k = AC(lambda e, bc=bc: e.copy(TM[2], banks[bc][:, :]), kc, tm_free)
                free(bc, k)
                k = DVE(lambda e, bh=bh: e.tensor_tensor(u, TM[2], banks[bh][:, :], ALU.mult), k, kh)
                free(bh, k)
                k = DVE(lambda e, m=m: e.tensor_scalar(y, u, col("cw2", 8 + m), None, ALU.mult), k)
                k = DVE(lambda e, m=m: e.scalar_tensor_tensor(
                    y[:, 1:S], u[:, 0:S - 1], col("cw2", 4 + m), y[:, 1:S], ALU.mult, ALU.add), k)
                k = DVE(lambda e, m=m: e.scalar_tensor_tensor(
                    y[:, 2:S], u[:, 0:S - 2], col("cw2", m), y[:, 2:S], ALU.mult, ALU.add), k)
                k = DVE(lambda e, bb=bb: e.tensor_tensor(y, y, banks[bb][:, :], ALU.mult), k, kb)
                free(bb, k)
                ky = k
                k = AC(lambda e: e.activation(TM[3], y, ACT.Square), ky)
                b, bw = bank()
                k = PE(mm(banks[b][:, :], BLK, TM[3], True, True), *bw, k, t_c2)
                k = AC(lambda e, b=b: e.activation(TM[4], banks[b][:, :], ACT.Sqrt, bias=EPS), k)
                free(b, k)
                k = DVE(lambda e: e.reciprocal(TM[4], TM[4]), k)
                tm_free = DVE(lambda e, m=m: e.scalar_tensor_tensor(
                    MIX[:, m, :], y, col("cg2", m), TM[4], ALU.mult, ALU.mult), k)
            for i, _, _ in (wc, wh, wb):
                done(i, kb)
        for n, dst, fn in ((0, QD, ACT.Silu), (1, SG, ACT.Silu), (2, FH, ACT.Sigmoid)):
            for j4 in range(2):
                i, w, tw = weights()
                for j2 in range(2):
                    b, k = proj_feat(w, j2, P, ht_ready, tw)
                    d = dst[:, j4 * 2 + j2, :]
                    ev = AC(lambda e, d=d, b=b, fn=fn: e.activation(d, banks[b][:, :], fn), k)
                    free(b, ev)
                done(i, k)
        f_ready = ev
        for j4 in range(2):
            i, w, tw = weights()
            for t in range(NT):
                b, bw = bank()
                for c in range(8):
                    PE.wait(tw, *bw)
                    k = PE(mm(banks[b][:, 0:256], HT[:, c, t * P:(t + 1) * P], w[:, c, :], c == 0, c == 7))
                ev = AC(lambda e, b=b, t=t, j4=j4: e.copy(V2[:, t, j4 * 256:j4 * 256 + 256], banks[b][:, 0:256]), k)
                free(b, ev)
            done(i, k)
        v2_ready = ev
        for h in range(4):
            k = DVE(lambda e, h=h: e.tensor_scalar(FH[:, h, :], FH[:, h, :], LB[:, 5, h:h + 1], LB[:, 0, h:h + 1],
                                                   ALU.mult, ALU.add), f_ready, lb_ready)
        kf = k
        k = AC(lambda e: e.activation(EG, FH, ACT.Ln), kf)
        kl = k
        k1h = DVE(lambda e: e.tensor_scalar(FH, FH, -1.0, 1.0, ALU.mult, ALU.add), kl)
        hg_ready = []
        for h in range(4):
            G = KD[:, h, :]
            k = DVE(lambda e, h=h, G=G: e.tensor_tensor_scan(G, SM, EG[:, h, :], 0.0, ALU.mult, ALU.add), kl, t_c2)
            G3 = G.rearrange("p (n c) -> p n c", c=32)
            k2 = DVE(lambda e, h=h, G3=G3: e.tensor_tensor(
                KE[:, h, :].rearrange("p (n c) -> p n c", c=32), G3[:, :, 31:32].to_broadcast([P, 16, 32]), G3,
                ALU.subtract), k)
            ke = AC(lambda e, h=h: e.activation(KE[:, h, :], KE[:, h, :], ACT.Exp), k2)
            kg = AC(lambda e, h=h, G=G: e.activation(EG[:, h, :], G, ACT.Exp), k)
            kn = AC(lambda e, h=h, G=G: e.activation(G, G, ACT.Exp, scale=-1.0), k2, kg)
            k3 = DVE(lambda e, h=h: e.tensor_tensor(KE[:, h, :], KE[:, h, :], FH[:, h, :], ALU.mult), ke, k1h)
            k4 = DVE(lambda e, h=h, G=G: e.tensor_tensor(G, G, FH[:, h, :], ALU.mult), kn)
            k5 = DVE(lambda e, h=h: e.scalar_tensor_tensor(QD[:, h, :], QD[:, h, :], 128.0 ** -0.5, EG[:, h, :],
                                                           ALU.mult, ALU.mult), kg)
            k6 = DVE(lambda e, h=h: e.tensor_copy(
                DEC[:, h, :], EG[:, h, :].rearrange("p (n c) -> p n c", c=32)[:, :, 31]), kg)
            hg_ready += [k3, k4, k5, k6]
        ket_ready = []
        for t in range(NT):
            b, bw = bank()
            for h in range(4):
                k = PE(lambda e, b=b, h=h, t=t: e.transpose(
                    banks[b][:, h * P:(h + 1) * P], KE[:, h, t * P:(t + 1) * P], IDENT), *bw, hg_ready)
            ev = AC(lambda e, b=b, t=t: e.copy(KET[:, t, :, :].rearrange("p h n -> p (h n)"), banks[b][:, :]), k)
            free(b, ev)
            ket_ready.append(ev)
        st_ready = []
        for t in range(NT):
            for j in range(4):
                n = t * 4 + j
                b, bw = bank()
                for h in range(4):
                    k = PE(mm(banks[b][:, h * P:(h + 1) * P], KET[j * 32:j * 32 + 32, t, h, :],
                              V2[j * 32:j * 32 + 32, t, h * P:(h + 1) * P], True, True),
                           *bw, ket_ready[t], v2_ready)
                if n == 0:
                    k = DVE(lambda e, b=b: e.tensor_copy(ST[:, 0, :], banks[b][:, :]), k)
                else:
                    prev = DVE.last
                    for h in range(4):
                        k2 = DVE(lambda e, b=b, h=h, n=n: e.scalar_tensor_tensor(
                            ST[:, n, h * P:(h + 1) * P], ST[:, n - 1, h * P:(h + 1) * P], DEC[:, h, n:n + 1],
                            banks[b][:, h * P:(h + 1) * P], ALU.mult, ALU.add), k, prev)
                    k = k2
                free(b, k)
                st_ready.append(k)
        zero = DVE(lambda e: e.memset(ATB, 0.0))
        hm = HM.bitcast(U32)
        for h in range(4):
            bo, bow = bank()
            ba, baw = bank()
            for t in range(NT):
                k = PE(mm(banks[ba][:, t * P:(t + 1) * P], KD[:, h, t * P:(t + 1) * P], QD[:, h, t * P:(t + 1) * P],
                          True, True), *baw, hg_ready)
            for t in range(NT):
                ka = DVE(lambda e, t=t, ba=ba: e.copy_predicated(ATB[:, t, :], hm, banks[ba][:, t * P:(t + 1) * P]),
                         k, zero, PE.last if h else None)
            free(ba, ka)
            for t in range(NT):
                PE(mm(banks[bo][:, t * P:(t + 1) * P], V2[:, t, h * P:(h + 1) * P], ATB[:, t, :], True, False),
                   ka, *bow)
                for j in range(4):
                    n = t * 4 + j
                    if n == 0:
                        continue
                    k = PE(mm(banks[bo][:, n * 32:n * 32 + 32], ST[:, n - 1, h * P:(h + 1) * P],
                              QD[:, h, n * 32:n * 32 + 32], False, j == 3), st_ready[n - 1])
            o = banks[bo]
            kq = AC(lambda e, o=o: e.activation(TM[0], o[:, :], ACT.Square), k, tm_free)
            b, bw = bank()
            k = PE(mm(banks[b][:, :], ONE, TM[0], True, True), *bw, kq)
            k = AC(lambda e, b=b: e.activation(TM[1], banks[b][:, :], ACT.Sqrt, bias=EPS), k, tm_free)
            free(b, k)
            k = DVE(lambda e: e.reciprocal(TM[1], TM[1]), k)
            k = DVE(lambda e, o=o: e.tensor_tensor(TM[2], o[:, :], TM[1], ALU.mult), k)
            free(bo, k)
            tm_free = DVE(lambda e, h=h: e.scalar_tensor_tensor(MIX[:, 4 + h, :], TM[2], col("hg"), SG[:, h, :],
                                                                ALU.mult, ALU.mult), k)
        x_ready = add_rows(MIX, tm_free)

        barrier()
        top[0] = base
        H2 = carve(NT, D)
        NF = carve(D)
        KEYS = carve(16, P)
        QT = carve(16, S)
        SR = [carve(P) for _ in range(2)]
        T16 = [carve(8, 2, 16) for _ in range(2)]
        I16 = [carve(8, 2, 16).bitcast(U32) for _ in range(2)]
        IF = carve(8, 2, 16)
        CAND = carve(8, 256)
        CSC = carve(8, 16)
        CIX = carve(8, 16).bitcast(U32)
        HL = carve(2, 8, 16)
        HLI = carve(2, 8, 16).bitcast(U32)
        OH = carve(8, 16, 16)
        EX = carve(3, 8, 16)
        GM = carve(8)
        EI = [carve(P).bitcast(U32) for _ in range(2)]
        GW = [carve(P) for _ in range(2)]
        AA = [carve(P) for _ in range(2)]
        ACC = [carve(D) for _ in range(2)]
        slots = [ring[j // 2][:, (j % 2) * D:(j % 2) * D + D] for j in range(2 * RING)]
        slots += [HTF[:, j * D:(j + 1) * D] for j in range(4)] + [carve(D) for _ in range(4)]
        NS = len(slots)
        JK = carve(D)
        SQ = carve(D)
        OUTB = [carve(D) for _ in range(2)]

        SP.dma(lambda e: e.dma_start(KEYS, a["keys"].rearrange("p (j n) -> p j n", j=16)), fg_sem)
        SP.dma(lambda e: e.dma_start(
            JK, a["rows"][0:1, ROW["norm_ffn"]:ROW["norm_ffn"] + D].to_broadcast([P, D])), fg_sem)
        t_nf = SP.dma(lambda e: e.dma_start(
            NF, a["rows"][0:1, ROW["norm_f"]:ROW["norm_f"] + D].to_broadcast([P, D])), fg_sem)

        h2_ready = []

        def keep(t, k):
            h2_ready.append(DVE(lambda e: e.tensor_tensor(H2[:, t, :], XS[t % 2], JK, ALU.mult), k, t_nf))
            return h2_ready[-1]

        ht_ready = norm_to_ht("gf2", x_ready, keep)
        qt_ready = []
        for c8 in range(8):
            i, w, tw = weights()
            for j2 in range(2):
                b, k = proj_feat(w, j2, P, ht_ready, tw)
                m = c8 * 2 + j2
                ev = AC(lambda e, b=b, m=m: e.copy(QT[:, m, :], banks[b][:, :]), k)
                free(b, ev)
            done(i, k)
        qt_ready = ev

        gat = {}

        def top_sixteen(values, indices, s, rest, ready):
            lo, hi = values[:, 0:8], values[:, 8:16]
            k1 = DVE(lambda e: e.max(lo, s), ready, DVE.last)
            k2 = DVE(lambda e: e.max_index(indices[:, 0:8], lo, s), k1)
            k2 = DVE(lambda e: e.match_replace(rest, lo, s, -3.0e38), k2)
            k3 = DVE(lambda e: e.max(hi, rest), k2)
            k4 = DVE(lambda e: e.max_index(indices[:, 8:16], hi, rest), k3)
            return k2, k4

        def choose(t):
            par = t % 2
            top16, ix16 = T16[par], I16[par]
            for b4 in range(4):
                b, bw = bank()
                for c in range(4):
                    m = b4 * 4 + c
                    k = PE(mm(banks[b][:, c * P:(c + 1) * P], QT[:, m, t * P:(t + 1) * P], KEYS[:, m, :], True, True),
                           *bw, qt_ready, t_nf)
                for c in range(4):
                    m = b4 * 4 + c
                    h, half = m // 2, m % 2
                    s = banks[b][:, c * P:(c + 1) * P]
                    lo, hi = top16[:, h, half, 0:8], top16[:, h, half, 8:16]
                    k2, k4 = top_sixteen(top16[:, h, half, :], ix16[:, h, half, :], s, SR[m % 2], k)
                    yield
                free(b, k2)
            kf = DVE(lambda e: e.tensor_copy(IF, ix16), k4, DVE.last)
            cand = CAND.rearrange("p h (a b) -> p h a b", a=16)
            k = k4
            for h in range(8):
                s1 = top16[:, h, 0, :].unsqueeze(2).to_broadcast([P, 16, 16])
                s2 = top16[:, h, 1, :].unsqueeze(1).to_broadcast([P, 16, 16])
                k = DVE(lambda e, h=h, s1=s1, s2=s2: e.tensor_tensor(cand[:, h, :, :], s1, s2, ALU.add), k4,
                        DVE.last)
                _, k = top_sixteen(CSC[:, h, :], CIX[:, h, :], CAND[:, h, :], CAND[:, h, :], k)
                yield
            k1 = DVE(lambda e: e.tensor_scalar(HLI[:, 0, :, :], CIX, 4, None, ALU.logical_shift_right), k)
            k2 = DVE(lambda e: e.tensor_scalar(HLI[:, 1, :, :], CIX, 15, None, ALU.bitwise_and), k)
            k = DVE(lambda e: e.tensor_copy(HL, HLI), k1, k2)
            yield
            for half in range(2):
                hl = HL[:, half, :, :].rearrange("p h j -> p (h j)").unsqueeze(2).to_broadcast([P, 128, 16])
                io = IOTA.unsqueeze(1).to_broadcast([P, 128, 16])
                oh = OH.rearrange("p h j a -> p (h j) a")
                k = DVE(lambda e, oh=oh, hl=hl, io=io: e.tensor_tensor(oh, hl, io, ALU.is_equal), k, DVE.last)
                ib = IF[:, :, half, :].unsqueeze(2).to_broadcast([P, 8, 16, 16])
                k = DVE(lambda e, ib=ib: e.tensor_tensor(OH, OH, ib, ALU.mult), k, kf)
                yield
                k = DVE(lambda e, half=half: e.tensor_reduce(EX[:, half, :, :], OH, AX, ALU.add), k)
                yield
            k = DVE(lambda e: e.scalar_tensor_tensor(EX[:, 2, :, :], EX[:, 0, :, :], 128.0, EX[:, 1, :, :],
                                                     ALU.mult, ALU.add), k)
            ei = DVE(lambda e: e.tensor_copy(EI[par].rearrange("p (h j) -> p h j", h=8), EX[:, 2, :, :]), k,
                     gat.get(("issued", t - 2)))
            gw = GW[par].rearrange("p (h j) -> p h j", h=8)
            k = DVE(lambda e: e.tensor_tensor(gw, CSC, CSC[:, :, 0:1].to_broadcast([P, 8, 16]), ALU.subtract), k)
            k = AC(lambda e: e.activation(gw, gw, ACT.Exp), k)
            k = DVE(lambda e: e.tensor_reduce(GM, gw, AX, ALU.add), k)
            k = DVE(lambda e: e.reciprocal(GM, GM), k)
            k = DVE(lambda e: e.tensor_tensor(gw, gw, GM.unsqueeze(2).to_broadcast([P, 8, 16]), ALU.mult), k)
            gat[t] = (ei, k)

        barrier()
        slot_sem = [[newsem(f"s_g{i}"), 0] for i in range(NS)]
        slot_free = [None] * NS
        jobs = [(t, which, k) for t in range(NT) for which in range(2) for k in range(P)]
        where = {}

        def gather(g):
            t, which, k = jobs[g]
            s = g % NS
            tab = a["peer_u_2"] if which == 0 else a["peer_v_2"]
            off = EI[t % 2][:, k:k + 1]
            where[g] = GP.dma(lambda e: e.indirect_dma_start(
                out=slots[s], out_offset=None, in_=tab, in_offset=bass.IndirectOffsetOnAxis(ap=off, axis=0)),
                slot_sem[s], gat[t][0], slot_free[s])

        for _ in choose(0):
            pass
        AHEAD = NS
        for g in range(AHEAD):
            gather(g)
        nextc = None
        out_sem = [[newsem(f"s_out{j}"), 0] for j in range(NT)]
        ov = a["out"].rearrange("(t p) d -> t p d", p=P)
        acc_chain = None
        for g, (t, which, k) in enumerate(jobs):
            if which == 0 and k == 0:
                nextc = choose(t + 1) if t + 1 < NT else iter(())
                acc_chain = DVE(lambda e, t=t: e.tensor_copy(ACC[t % 2], X[:, t, :]))
            s = g % NS
            if which == 0:
                tok = DVE(lambda e, s=s, t=t, k=k: e.tensor_tensor_reduce(
                    out=SQ, in0=slots[s], in1=H2[:, t, :], scale=1.0, scalar=0.0, op0=ALU.mult, op1=ALU.add,
                    accum_out=AA[t % 2][:, k:k + 1]), where[g], h2_ready[t], DVE.last)
                if k == P - 1:
                    kk = AC(lambda e, t=t: e.activation(AA[t % 2], AA[t % 2], ACT.Gelu), tok)
                    w_ready = DVE(lambda e, t=t: e.tensor_tensor(AA[t % 2], AA[t % 2], GW[t % 2], ALU.mult),
                                  kk, gat[t][1])
            else:
                tok = DVE(lambda e, s=s, t=t, k=k: e.scalar_tensor_tensor(
                    ACC[t % 2], slots[s], AA[t % 2][:, k:k + 1], ACC[t % 2], ALU.mult, ALU.add),
                    where[g], w_ready, acc_chain)
                acc_chain = tok
            slot_free[s] = tok
            if (t, which, k) == (t, 0, P - 1) or g + AHEAD >= len(jobs) or jobs[g + AHEAD][0] == t:
                pass
            if k % 3 == 0:
                next(nextc, None)
            if which == 1 and k == P - 1 - NS:
                for _ in nextc:
                    pass
            if g + AHEAD < len(jobs):
                gather(g + AHEAD)
                if jobs[g + AHEAD][1:] == (1, P - 1):
                    gat["issued", jobs[g + AHEAD][0]] = where[g + AHEAD]
            if which == 1 and k == P - 1:
                acc = ACC[t % 2]
                kk = AC(lambda e, acc=acc: e.activation(JK, acc, ACT.Square, accum_out=SS[:, 12:13]), tok, AC.last,
                        DVE.last)
                kk = AC(lambda e: e.activation(SS[:, 13:14], SS[:, 12:13], ACT.Sqrt, bias=EPS, scale=1.0 / D), kk)
                kk = DVE(lambda e: e.reciprocal(SS[:, 14:15], SS[:, 13:14]), kk)
                kk = DVE(lambda e, t=t, acc=acc: e.scalar_tensor_tensor(OUTB[t % 2], acc, SS[:, 14:15], NF,
                                                                        ALU.mult, ALU.mult), kk, t_nf,
                         (out_sem[t - 2][0], 16) if t >= 2 else None)
                out_tok = SP.dma(lambda e, t=t: e.dma_start(ov[t], OUTB[t % 2]), out_sem[t], kk)
        for s in out_sem:
            SP.wait((s[0], s[1]))
        for q in (SP,):
            q.wait(*[(s[0], s[1]) for s in slot_sem + ring_sem + [small, big, w2_sem, fg_sem]])

        def run(q):
            def body(e):
                for op in q.ops:
                    op(e)
            return body

        block.tensor(run(PE))
        block.vector(run(DVE))
        block.scalar(run(AC))
        block.gpsimd(run(GP))
        block.sync(run(SP))


def kernel(**inputs):
    import concourse.bacc as _bacc
    from concourse.bass_utils import run_bass_kernel_spmd as _run

    x = {n: np.ascontiguousarray(v) for n, v in inputs.items()}

    def pad(v, n=P):
        return np.concatenate([v, np.zeros((n - v.shape[0],) + v.shape[1:], v.dtype)], 0) if v.shape[0] < n else v

    def by(v):
        return v.reshape(-1, P).T

    b = x["b_in"][0]
    cols = np.concatenate([
        by(x["norm1_g"][0]), by(b[QA:QA + 256]), by(b[KA:KA + 256]), by(b[QB:QB + 384]), by(b[KB:KB + 384]),
        by(b[QC:QC + 384]), by(b[KC:KC + 128]), by(b[VC:VC + 128]), by(b[KSL:KSL + 128]), by(b[KWN:KWN + 128]),
        pad(b[FA:FA + 4].reshape(4, 1)), by(b[GATES:]), by(x["norm2_g"][0]),
        by(x["conv_w"][0].reshape(-1)), by(x["conv_b"][0]), by(x["norm_mix_2"][0]),
        by(x["conv_w_2"][0].reshape(-1)), by(x["conv_gain_2"][0]), by(x["hg_lb_logits_2"].reshape(-1)),
        by(x["hg_gain_2"][0]), by(x["norm_ffn_2"][0]),
        np.concatenate([x["cmp_pe"][0].T, x["cmp_pe"][0].T], 0)], 1)
    rows = np.concatenate([b[VA:VA + 256], b[VB:VB + 384], b[VSL:VSL + 128], b[VWN:VWN + 128], b[GC:GC + 18],
                           x["final_g"], x["norm_ffn_2"][0], x["norm_f_2"]])[None]
    keys = x["peer_keys_2"][0].transpose(3, 0, 1, 2).reshape(P, 16 * P)
    arrays = {"x": x["x"][0], "cols": cols, "rows": rows, "keys": keys, "con": constants()}
    for n in ("w_in", "cmp_k_w1", "cmp_k_w2", "cmp_v_w1", "cmp_v_w2", "w_pa", "w_pb", "w_pc", "w_o", "w_up",
              "w_down", "w_in_2", "w_out_2", "peer_wq_2", "peer_u_2", "peer_v_2"):
        arrays[n] = x[n][0]
    nc = _bacc.Bacc("TRN2", target_bir_lowering=False, num_devices=1)
    sent, aps = {}, {}
    for n, v in arrays.items():
        v = np.ascontiguousarray(v)
        sent[f"in_{n}"] = v
        aps[n] = nc.dram_tensor(f"in_{n}", v.shape, mybir.dt.from_np(v.dtype), kind="ExternalInput").ap()
    aps["out"] = nc.dram_tensor("out_0", (S, D), F32, kind="ExternalOutput").ap()
    build(nc, aps)
    r = _run(nc, [sent], core_ids=[0])
    return r.results[0]["out_0"].reshape(1, S, D)
```

```python
from contextlib import ExitStack

import numpy as np
import concourse.bass as bass
from concourse import mybir

ALU = mybir.AluOpType
ACT = mybir.ActivationFunctionType
F32 = mybir.dt.float32
U32 = mybir.dt.uint32
AX = mybir.AxisListType.X

P = 128
S = 512
D = 1024
NT = S // P
GB = 2
T = GB * P
STEP = 1.5
HEAD = 0
NEG = -1e30
TINY = 1e-30
FF = 2816
NFF = FF // P

QA, KA, VA, FA = 0, 256, 512, 768
QB, KB, VB = 772, 1156, 1540
QC, KC, VC, KSL, VSL, KWN, VWN, GC, GATES = 1924, 2308, 2436, 2564, 2692, 2820, 2948, 3076, 3094

COL = {}
_at = 0
for _name, _n in (("g1", 8), ("b_qa", 2), ("b_ka", 2), ("b_qb", 3), ("b_kb", 3), ("b_qc", 3), ("b_kc", 1),
                  ("b_vc", 1), ("b_ksl", 1), ("b_kwn", 1), ("b_fa", 1), ("b_gate", 24), ("g2", 8),
                  ("cw", 66), ("cb", 22), ("gm2", 8), ("cw2", 12), ("cg2", 4), ("lb", 8), ("hg", 1),
                  ("gf2", 8), ("pe", 32)):
    COL[_name] = _at
    _at += _n
NCOL = _at

ROW = {}
_at = 0
for _name, _n in (("bv", 914), ("final_g", 1024), ("norm_ffn", 1024), ("norm_f", 1024)):
    ROW[_name] = _at
    _at += _n
NROW = _at

TAB_W = [512, 256, 256] + [512] * 10
TAB_AT = [sum(TAB_W[:n]) for n in range(13)]

CON = {}
_at = 0
for _name, _n in (("ident", 128), ("iota", 16), ("eps", 1), ("tab", 6144), ("ctab", 768), ("cmask", 768),
                  ("hmask", 128), ("smask", 512), ("blk", 128), ("all", 128)):
    CON[_name] = _at
    _at += _n
NCON = _at


def constants():
    c = np.zeros((P, NCON), np.float32)
    p = np.arange(P)
    c[:, CON["ident"]:CON["ident"] + P] = np.eye(P, dtype=np.float32)
    c[:, CON["iota"]:CON["iota"] + 16] = np.arange(16, dtype=np.float32)
    c[:, CON["eps"]] = 1e-6
    slopes = np.exp2(-8.0 * np.arange(1, 13, dtype=np.float32) / 12).astype(np.float32)
    dist = p[:, None] - (np.arange(512)[None, :] - 384)
    dil, nsa = slopes[0::2], slopes[1::2]
    tabs = [np.where(dist >= 0, 0.0, NEG)]
    assert len(TAB_W) == 13
    for h in range(6):
        w, r = ((128, 1), (512, 4), (2048, 16))[h // 2]
        ok = (dist >= 0) & (dist <= w) & (dist % r == 0)
        tabs.append(np.where(ok, -dil[h] * dist.astype(np.float32), NEG)[:, 512 - TAB_W[1 + h]:])
    for h in range(6):
        tabs.append(np.where(dist >= 0, -nsa[h] * dist.astype(np.float32), NEG))
    c[:, CON["tab"]:CON["tab"] + 6144] = np.concatenate(tabs, 1).astype(np.float32)
    ct = np.full((P, 2, NT, 3, 32), NEG, np.float32)
    cm = np.zeros((P, 2, NT, 3, 32), np.float32)
    end = np.arange(31) * 16 + 31
    for par in range(2):
        for i in range(NT):
            d = (i * P + p)[:, None] - end[None, :]
            for hh in range(3):
                ct[:, par, i, hh, :31] = np.where(d >= 0, -nsa[2 * hh + par] * d.astype(np.float32), NEG)
                cm[:, par, i, hh, :31] = d >= 0
    c[:, CON["ctab"]:CON["ctab"] + 768] = ct.reshape(P, 768)
    c[:, CON["cmask"]:CON["cmask"] + 768] = cm.reshape(P, 768)
    c[:, CON["hmask"]:CON["hmask"] + P] = (p[:, None] // 32 == p[None, :] // 32) & (p[:, None] <= p[None, :])
    c[:, CON["smask"]:CON["smask"] + 512] = np.arange(512) % 32 != 0
    c[:, CON["blk"]:CON["blk"] + P] = (p[:, None] // 64 == p[None, :] // 64) / 64.0
    c[:, CON["all"]:CON["all"] + P] = 1 / 128.0
    return c


class Queue:

    def __init__(self, sem):
        self.sem, self.n, self.ops, self.seen = sem, 0, [], {}

    def wait(self, *tokens):
        for t in tokens:
            if t is None:
                continue
            if isinstance(t, list):
                self.wait(*t)
                continue
            sem, value = t
            if self.seen.get(id(sem), 0) >= value:
                continue
            self.seen[id(sem)] = value
            self.ops.append(lambda e, sem=sem, value=value: e.wait_ge(sem, value))

    def __call__(self, fn, *tokens):
        self.wait(*tokens)
        self.n += 1
        self.ops.append(lambda e: fn(e).then_inc(self.sem, 1))
        return (self.sem, self.n)

    def quiet(self, fn, *tokens):
        self.wait(*tokens)
        self.ops.append(fn)

    def dma(self, fn, sem, *tokens):
        self.wait(*tokens)
        sem[1] += 16
        self.ops.append(lambda e, s=sem[0]: fn(e).then_inc(s, 16))
        return (sem[0], sem[1])

    @property
    def last(self):
        return (self.sem, self.n)


def build(nc, a):
    ctx = ExitStack()
    with ctx:
        def newsem(name):
            return ctx.enter_context(nc.semaphore(name))

        arena = ctx.enter_context(nc.sbuf_tensor("arena", [P, 53000], F32))
        banks = [ctx.enter_context(nc.psum_tensor(f"bank{i}", [P, 512], F32)) for i in range(8)]
        PE, DVE, AC, GP, SP = (Queue(newsem(n)) for n in ("s_pe", "s_dve", "s_act", "s_pool", "s_sp"))
        block = ctx.enter_context(nc.Block())

        top = [0]

        def carve(*shape):
            n = 1
            for s in shape:
                n *= s
            at = top[0]
            top[0] += n
            assert top[0] <= 53000, top[0]
            v = arena[:, at:at + n]
            if len(shape) == 2:
                v = v.rearrange("p (a b) -> p a b", a=shape[0])
            elif len(shape) == 3:
                v = v.rearrange("p (a b c) -> p a b c", a=shape[0], b=shape[1])
            elif len(shape) == 4:
                v = v.rearrange("p (a b c d) -> p a b c d", a=shape[0], b=shape[1], c=shape[2])
            return v

        X = carve(GB, D)
        HT = carve(8, T)
        COLS = carve(NCOL)
        FIX = carve(145)
        IDENT, IOTA, EPS = FIX[:, 0:128], FIX[:, 128:144], FIX[:, 144:145]
        SS = carve(16)
        RING = 4
        ring = [carve(2048) for _ in range(RING)]
        xs_at = top[0]
        XS = [carve(D) for _ in range(2)]
        KF = carve(11, S)
        VT = carve(NT, 914)
        SEL = carve(4, P)
        FC = carve(S)
        HID = carve(2, 2, 62)
        KCT = carve(62)
        VCB = carve(2, 192)
        AH = carve(NFF, 2)
        UH = carve(4, 2)
        STP = carve(512)
        slots8 = [carve(D) for _ in range(8)]
        H2 = carve(GB, D)
        ACC = [carve(D) for _ in range(GB)]
        NF = carve(D)
        EI = [carve(P).bitcast(U32) for _ in range(2)]
        GW = [carve(P) for _ in range(2)]
        AA = [carve(P) for _ in range(2)]
        NM, LS, RL = carve(22, GB), carve(22, GB), carve(22, GB)
        CQ, AL, GS, CS = carve(GB, 4), carve(4, GB, 6), carve(GB, 18), carve(2, GB * 3)
        base = top[0]

        def col(name, j=0, n=1):
            return COLS[:, COL[name] + j:COL[name] + j + n]

        def con(name, n, off=0):
            return a["con"][:, CON[name] + off:CON[name] + off + n]

        psum_at = [0, 0]
        psum_readers = [[] for _ in range(8)]
        held = set()
        spent = [0.0]
        side = [None]

        def tick():
            while side[0] is not None and spent[0] > 0:
                cost = next(side[0], None)
                if cost is None:
                    side[0] = None
                else:
                    spent[0] -= cost

        def bank():
            if side[0] is None:
                spent[0] = 0.0
            tick()
            while psum_at[0] % 6 in held:
                psum_at[0] += 1
            b = psum_at[0] % 6
            psum_at[0] += 1
            w = psum_readers[b]
            psum_readers[b] = []
            return b, w

        def side_bank():
            b = 6 + psum_at[1] % 2
            psum_at[1] += 1
            w = psum_readers[b]
            psum_readers[b] = []
            return b, w

        def free(b, *tokens):
            psum_readers[b] += tokens

        def kcols(w, c0, n):
            return [(w.rearrange("(c p) n -> p c n", p=P)[:, :, c0:c0 + n], 8, 0, n)]

        w_in, w_in2 = a["w_in"], a["w_in_2"]
        FEAT1 = [("qa", QA, 256), ("ka", KA, 256), ("qb", QB, 256), ("qb", QB + 256, 128),
                 ("kb", KB, 256), ("kb", KB + 256, 128), ("qc", QC, 256), ("qc", QC + 256, 128),
                 ("kvc", KC, 256), ("ksl", KSL, 128), ("kwn", KWN, 128), ("fa", FA, 4)]
        TOK1 = [(VA, 256, 0), (VB, 256, 256), (VB + 256, 128, 512), (VSL, 128, 640), (VWN, 146, 768)]
        plan = [(kcols(w_in, c0, n), n) for _, c0, n in FEAT1]
        plan += [(kcols(w_in, c0, n), n) for c0, n, _ in TOK1]
        for w in (a["cmp_k_w1"], a["cmp_v_w1"]):
            for half in range(2):
                plan.append(([(w.rearrange("(c p) n -> p c n", p=P)[:, half * 8:half * 8 + 8, :], 8, 0, 256)], 256))
        for mm in range(4):
            parts = [(a["w_pa"], 0, 2), (a["w_pb"], 2, 3), (a["w_pc"], 5, 3)]
            plan.append(([(w.rearrange("(c p) n -> p c n", p=P)[:, :, mm * 256:mm * 256 + 256], k, c, 256)
                          for w, c, k in parts], 256))
            for j in range(3):
                plan.append((kcols(w_in, GATES + j * D + mm * 256, 256), 256))
        plan += [(kcols(a["w_o"], c * 256, 256), 256) for c in range(4)]
        for j in range(11):
            plan += [(kcols(a["w_up"], j * 256, 256), 256), (kcols(a["w_up"], FF + j * 256, 256), 256)]
        DOWN = [(0, 4), (4, 4), (8, 4), (12, 4), (16, 4), (20, 2)]
        for half in range(2):
            for k0, kn in DOWN:
                plan.append(([(a["w_down"].rearrange("(c p) n -> p c n", p=P)
                               [:, k0:k0 + kn, half * 512:half * 512 + 512], kn, 0, 512)], 512))
        for j in range(2):
            plan += [(kcols(w_in2, s * 512 + j * 256, 256), 256) for s in (0, 1, 2)]
        plan += [(kcols(w_in2, c0, 256), 256) for c0 in (1536, 1792, 3072, 3328, 2048, 2304)]
        plan += [(kcols(w_in2, 2560 + j * 256, 256), 256) for j in range(2)]
        plan += [(kcols(a["w_out_2"], c * 256, 256), 256) for c in range(4)]
        plan += [(kcols(a["peer_wq_2"], c * 256, 256), 256) for c in range(8)]

        plan = plan * (NT // GB)

        ring_sem = [[newsem(f"s_w{i}"), 0] for i in range(RING)]
        landed = {}
        nxt = [0]

        def load_weights(i, *tokens):
            if i >= len(plan):
                return
            parts, width = plan[i]
            s = i % RING
            for src, k, c, w in parts:
                dst = ring[s].rearrange("p (c n) -> p c n", n=256 if width <= 256 else 512)[:, c:c + k, 0:w]
                landed[i] = SP.dma(lambda e, dst=dst, src=src: e.dma_start(dst, src), ring_sem[s], *tokens)

        def weights():
            i = nxt[0]
            nxt[0] += 1
            width = plan[i][1]
            return i, ring[i % RING].rearrange("p (c n) -> p c n", n=256 if width <= 256 else 512), landed[i]

        def done(i, token):
            load_weights(i + RING, token)

        def barrier():
            lasts = [q.last for q in (PE, DVE, AC, GP)]
            for q in (PE, DVE, AC, GP, SP):
                q.wait(*lasts)

        def mm(out, lhsT, rhs, start, stop):
            spent[0] += 4 * rhs.shape[-1] / 2400.0
            return lambda e: e.matmul(out, lhsT, rhs, start=start, stop=stop)

        small = [newsem("s_small"), 0]
        x_sem = [[newsem(f"s_x{t}"), 0] for t in range(NT)]

        xv = a["x"].rearrange("(t p) d -> t p d", p=P)

        def load_x(g, *tokens):
            return [AC.dma(lambda e, t=t: e.dma_start(X[:, t, :], xv[GB * g + t]), x_sem[GB * g + t], *tokens)
                    for t in range(GB)]

        x_in = load_x(0)
        for dst, src in ((COLS, a["cols"]), (FIX, con("ident", 145))):
            t_small = AC.dma(lambda e, dst=dst, src=src: e.dma_start(dst, src), small)
        for i in range(RING):
            load_weights(i)
        sems = []

        def load_all(*pairs, wait=()):
            s = [newsem(f"s_l{len(sems)}"), 0]
            sems.append(s)
            for dst, src in pairs:
                t = AC.dma(lambda e, dst=dst, src=src: e.dma_start(dst, src), s, *wait)
            return t

        def row(name, n):
            return a["rows"][0:1, ROW[name]:ROW[name] + n].to_broadcast([P, n])

        t_nf = load_all((NF, row("norm_f", D)))
        DVE(lambda e: e.memset(AH, 0.0))
        DVE(lambda e: e.memset(UH, 0.0))
        DVE(lambda e: e.memset(STP, 0.0))
        vcb0 = DVE(lambda e: e.memset(VCB, 0.0))
        sel_ready = DVE(lambda e: e.tensor_copy(
            SEL[0:4, :, :], IDENT[0:4, 0:4].unsqueeze(2).to_broadcast([4, 4, P])), t_small)

        xs_free = [[], []]

        def rms(t, ready):
            k = AC(lambda e: e.activation(XS[t % 2], X[:, t, :], ACT.Square, accum_out=SS[:, t:t + 1]),
                   ready, t_small, xs_free[t % 2])
            k = AC(lambda e: e.activation(SS[:, t + 4:t + 5], SS[:, t:t + 1], ACT.Sqrt, bias=EPS, scale=1.0 / D), k)
            return DVE(lambda e: e.reciprocal(SS[:, t + 8:t + 9], SS[:, t + 4:t + 5]), k)

        def norm_to_ht(gain, ready, keep=None):
            out = []
            for t in range(GB):
                k = rms(t, ready[t])
                k = DVE(lambda e, t=t: e.tensor_scalar(XS[t % 2], X[:, t, :], SS[:, t + 8:t + 9], None, ALU.mult), k)
                tr = [keep(t, k)] if keep is not None else []
                for half in range(2):
                    b, w = bank()
                    for c in range(4):
                        src = XS[t % 2][:, (half * 4 + c) * P:(half * 4 + c + 1) * P]
                        k2 = PE(lambda e, b=b, c=c, src=src: e.transpose(banks[b][:, c * P:(c + 1) * P], src, IDENT),
                                k, *w)
                    tr.append(k2)
                    dst = HT[:, half * 4:half * 4 + 4, t * P:(t + 1) * P]
                    gn = col(gain, half * 4, 4).unsqueeze(2).to_broadcast([P, 4, P])
                    src = banks[b][:, :].rearrange("p (c n) -> p c n", c=4)
                    k3 = DVE(lambda e, dst=dst, src=src, gn=gn: e.tensor_tensor(dst, src, gn, ALU.mult), k2, t_small,
                             PE.last)
                    free(b, k3)
                    out.append(k3)
                xs_free[t % 2] = tr
            return out

        def proj_feat(w, j, n, ready, *extra):
            b, bw = bank()
            PE.wait(ready, *extra, *bw)
            for c in range(8):
                op = mm(banks[b][0:n, 0:T], w[:, c, j * P:j * P + n], HT[:, c, :], c == 0, c == 7)
                if c < 7:
                    PE.quiet(op)
                else:
                    k = PE(op)
            return b, k

        def add_rows(src, ready):
            out = [None] * GB
            for c4 in range(4):
                i, w, tw = weights()
                for t in range(GB):
                    b, bw = bank()
                    PE.wait(tw, *bw, ready)
                    for c in range(8):
                        op = mm(banks[b][:, 0:256], src[:, c, t * P:(t + 1) * P], w[:, c, :], c == 0, c == 7)
                        if c == 7:
                            k = PE(op)
                        else:
                            PE.quiet(op)
                    x = X[:, t, c4 * 256:c4 * 256 + 256]
                    out[t] = DVE(lambda e, b=b, x=x: e.tensor_tensor(x, x, banks[b][:, 0:256], ALU.add), k)
                    free(b, out[t])
                done(i, k)
            return out

        slot = {"qa": 0, "qb": 2, "qc": 5, "ka": 0, "kb": 2, "ksl": 5, "kwn": 7, "kvc": 9}
        cx = {}

        def project(g, ready):
            tok = slice(g * T, (g + 1) * T)
            QF = carve(8, T)
            FW = XS[1][:, 0:2 * T].rearrange("p (a b) -> p a b", a=2)
            BV = XS[0][:, 0:914]
            ht_ready = norm_to_ht("g1", ready)
            t_bv = load_all((BV, row("bv", 914)), wait=(xs_free[0], xs_free[1]))
            seen = {}
            for name, c0, n in FEAT1:
                i, w, tw = weights()
                for j in range((n + P - 1) // P):
                    b, k = proj_feat(w, j, min(n, P), ht_ready, tw)
                    if name == "fa":
                        bias = COLS[0:4, COL["b_fa"]:COL["b_fa"] + 1]
                        ev = [DVE(lambda e, b=b, bias=bias: e.tensor_scalar(
                            FW[0:4, 0, :], banks[b][0:4, 0:T], bias, None, ALU.add), k, xs_free[1])]
                        fa_ready = ev
                    elif name in ("ksl", "kwn"):
                        ev = []
                        for q in range(2):
                            for half in range(2):
                                dst = KF[half * 64:half * 64 + 64, slot[name] + q, tok]
                                src = banks[b][q * 64:q * 64 + 64, 0:T]
                                bias = COLS[q * 64:q * 64 + 64, COL["b_" + name]:COL["b_" + name] + 1]
                                ev.append(DVE(lambda e, dst=dst, src=src, bias=bias:
                                              e.tensor_scalar(dst, src, bias, None, ALU.add), k))
                    else:
                        m = seen.get(name, 0)
                        seen[name] = m + 1
                        bias = col("b_" + name, m) if name != "kvc" else col("b_kc" if m == 0 else "b_vc")
                        if name[0] == "q":
                            dst = QF[:, slot[name] + m, :]
                            ev = [DVE(lambda e, dst=dst, b=b, bias=bias: e.tensor_scalar(
                                dst, banks[b][:, 0:T], bias, 0.125, ALU.add, ALU.mult), k)]
                        else:
                            dst = KF[:, slot[name] + m, tok]
                            ev = [AC(lambda e, dst=dst, b=b, bias=bias:
                                     e.activation(dst, banks[b][:, 0:T], ACT.Identity, bias=bias), k)]
                    free(b, *ev)
                done(i, k)
            for c0, n, off in TOK1:
                i, w, tw = weights()
                for t in range(GB):
                    b, bw = bank()
                    PE.wait(tw, *bw)
                    for c in range(7):
                        PE.quiet(mm(banks[b][:, 0:n], HT[:, c, t * P:(t + 1) * P], w[:, c, 0:n], c == 0, False))
                    k = PE(mm(banks[b][:, 0:n], HT[:, 7, t * P:(t + 1) * P], w[:, 7, 0:n], False, True))
                    ev = DVE(lambda e, b=b, t=GB * g + t, n=n, off=off: e.tensor_tensor(
                        VT[:, t, off:off + n], banks[b][:, 0:n], BV[:, off:off + n], ALU.add), k, t_bv)
                    free(b, ev)
                done(i, k)
            cx.update(QF=QF, FW=FW, fa=fa_ready, vt=ev, ht=ht_ready)

        def attend(g):
            QF, FW = cx["QF"], cx["FW"]
            TABF = carve(6144)
            Y = carve(GB, D)
            zone = top[0]
            CT = carve(2, GB * 96)
            CM = carve(2, GB * 96)
            CE = carve(2, GB * 3, 32)
            PCT = carve(2, GB, P)
            W2 = [carve(2, 64), carve(2, 64)]
            assert top[0] <= zone + 2048
            t_tab = load_all((TABF, con("tab", 6144)))
            views = [con(n, 768).rearrange("p (a b) -> p a b", a=2)[:, :, g * GB * 96:(g + 1) * GB * 96]
                     for n in ("ctab", "cmask")]
            t_w2 = load_all((W2[0], a["cmp_k_w2"].rearrange("(c p) n -> p c n", p=P)),
                            (W2[1], a["cmp_v_w2"].rearrange("(c p) n -> p c n", p=P)),
                            (CT, views[0]), (CM, views[1]))
            gs_ready = AC(lambda e: e.activation(GS, VT[:, GB * g:GB * g + GB, 896:914], ACT.Sigmoid), cx["vt"])

            c0, nc_ = (0, 15) if g == 0 else (15 + 16 * (g - 1), 16)
            ntot = c0 + nc_
            FB = XS[0].rearrange("p (a b c) -> p a b c", a=2, b=16)[:, :, :, 0:2 * nc_]
            fb_ready = []
            for kv in range(2):
                for q in range(2):
                    for par in range(2):
                        for hf in range(2):
                            lo = 16 * (hf + c0)
                            v = KF[q * 64:q * 64 + 64, slot["kvc"] + kv, lo:lo + 16 * nc_]
                            v = v.rearrange("p (c l q) -> p l c q", l=8, q=2)[:, :, :, par]
                            pe = COLS[q * 64:q * 64 + 64, COL["pe"] + 16 * hf:COL["pe"] + 16 * hf + 16]
                            pe = pe.rearrange("p (l q) -> p l q", q=2)[:, :, par].unsqueeze(2)
                            pe = pe.to_broadcast([64, 8, nc_])
                            dst = FB[par * 64:par * 64 + 64, kv, hf * 8:hf * 8 + 8, q * nc_:q * nc_ + nc_]
                            fb_ready.append(DVE(lambda e, dst=dst, v=v, pe=pe: e.tensor_tensor(dst, v, pe, ALU.add),
                                                cx["vt"]))
            hid_ready = []
            for kv in range(2):
                two = [weights(), weights()]
                for m in range(2):
                    b, bw = bank()
                    PE.wait(two[0][2], two[1][2], *bw, fb_ready)
                    for c in range(16):
                        op = mm(banks[b][:, 0:2 * nc_], two[c // 8][1][:, c % 8, m * P:m * P + P], FB[:, kv, c, :],
                                c == 0, c == 15)
                        if c == 15:
                            k = PE(op)
                        else:
                            PE.quiet(op)
                    dst = HID[:, kv, m, :].rearrange("p (q c) -> p q c", q=2)[:, :, c0:ntot]
                    src = banks[b][:, 0:2 * nc_].rearrange("p (q c) -> p q c", q=2)
                    ev = AC(lambda e, src=src, dst=dst: e.activation(dst, src, ACT.Gelu_apprx_tanh), k)
                    free(b, ev)
                    hid_ready.append(ev)
                done(two[0][0], k)
                done(two[1][0], k)
            kct_ready = []
            for q in range(2):
                b, bw = bank()
                lo, hi = q * 31 + c0, q * 31 + ntot
                PE.quiet(mm(banks[b][0:64, 0:nc_], W2[0][:, 0, :], HID[:, 0, 0, lo:hi], True, False),
                         *bw, hid_ready, t_w2)
                k = PE(mm(banks[b][0:64, 0:nc_], W2[0][:, 1, :], HID[:, 0, 1, lo:hi], False, True))
                ev = [DVE(lambda e, b=b, h=h, lo=lo, hi=hi: e.tensor_copy(
                    KCT[h * 64:h * 64 + 64, lo:hi], banks[b][0:64, 0:nc_]), k) for h in range(2)]
                kct_ready += ev
                free(b, *ev)
            vcb_ready = []
            for q in range(2):
                b, bw = bank()
                lo, hi = q * 31, q * 31 + ntot
                PE.quiet(mm(banks[b][0:ntot, 0:64], HID[:, 1, 0, lo:hi], W2[1][:, 0, :], True, False), *bw)
                k = PE(mm(banks[b][0:ntot, 0:64], HID[:, 1, 1, lo:hi], W2[1][:, 1, :], False, True))
                ev = []
                for h in range(3 * q, 3 * q + 3):
                    par, hh = h % 2, h // 2
                    ev.append(DVE(lambda e, b=b, par=par, hh=hh: e.tensor_copy(
                        VCB[hh * 32:hh * 32 + ntot, par, hh * 64:hh * 64 + 64], banks[b][0:ntot, 0:64]), k, vcb0))
                free(b, *ev)
                vcb_ready += ev

            ce_ready = []
            for par in range(2):
                b, bw = bank()
                for i in range(GB):
                    for hh in range(3):
                        q = (2 * hh + par) // 3
                        out = banks[b][:, (i * 3 + hh) * 32:(i * 3 + hh) * 32 + ntot]
                        k = PE(mm(out, QF[par * 64:par * 64 + 64, 5 + hh, i * P:(i + 1) * P],
                                  KCT[par * 64:par * 64 + 64, q * 31:q * 31 + ntot], True, True), *bw, kct_ready)
                ce, cs = CE[:, par, :, :], CS[:, par, :]
                ct = CT[:, par, :].rearrange("p (i c) -> p i c", c=32)
                cm = CM[:, par, :].rearrange("p (i c) -> p i c", c=32)
                src = banks[b][:, 0:GB * 96].rearrange("p (i c) -> p i c", c=32)
                z = DVE(lambda e, ce=ce: e.memset(ce, 0.0))
                k = DVE(lambda e, ce=ce, src=src, ct=ct: e.tensor_tensor(
                    ce[:, :, 0:ntot], src[:, :, 0:ntot], ct[:, :, 0:ntot], ALU.add), k, z, t_w2)
                free(b, k)
                k = DVE(lambda e, ce=ce, cs=cs: e.tensor_reduce(cs, ce[:, :, 0:ntot], AX, ALU.max), k)
                k = DVE(lambda e, ce=ce, cs=cs: e.tensor_tensor(
                    ce[:, :, 0:ntot], ce[:, :, 0:ntot], cs.unsqueeze(2).to_broadcast([P, GB * 3, ntot]),
                    ALU.subtract), k)
                k = AC(lambda e, ce=ce: e.activation(ce[:, :, 0:ntot], ce[:, :, 0:ntot], ACT.Exp), k)
                k = DVE(lambda e, ce=ce, cm=cm: e.tensor_tensor(ce, ce, cm, ALU.mult), k)
                k = DVE(lambda e, ce=ce, cs=cs: e.tensor_reduce(cs, ce, AX, ALU.add), k)
                k = DVE(lambda e, cs=cs: e.tensor_scalar(cs, cs, TINY, None, ALU.max), k)
                k = DVE(lambda e, cs=cs: e.reciprocal(cs, cs), k)
                gate = GS.rearrange("p i (h q b) -> p i h q b", q=2, b=3)[:, :, :, par, 0]
                cs3 = cs.rearrange("p (i h) -> p i h", h=3)
                k = DVE(lambda e, cs3=cs3, gate=gate: e.tensor_tensor(cs3, cs3, gate, ALU.mult), k, gs_ready)
                k = DVE(lambda e, ce=ce, cs=cs: e.tensor_tensor(
                    ce, ce, cs.unsqueeze(2).to_broadcast([P, GB * 3, 32]), ALU.mult), k)
                ce_ready.append(k)
            y_c0 = []
            for par in range(2):
                b, bw = bank()
                for i in range(GB):
                    k = PE(lambda e, b=b, i=i, par=par: e.transpose(
                        banks[b][0:96, i * P:(i + 1) * P], CE[:, par, 3 * i:3 * i + 3, :].rearrange("p h c -> p (h c)"),
                        IDENT), *bw, ce_ready[par])
                pct = AC(lambda e, b=b, par=par: e.copy(PCT[0:96, par, :, :].rearrange("p i n -> p (i n)"),
                                                        banks[b][0:96, 0:T]), k)
                free(b, pct)
                for i in range(GB):
                    b, bw = bank()
                    k = PE(mm(banks[b][:, 0:192], PCT[0:96, par, i, :], VCB[0:96, par, :], True, True),
                           *bw, pct, vcb_ready)
                    y = Y[:, i, 640:1024].rearrange("p (h q d) -> p h q d", q=2, d=64)[:, :, par, :]
                    k = DVE(lambda e, b=b, y=y: e.tensor_copy(
                        y, banks[b][:, 0:192].rearrange("p (h d) -> p h d", h=3)), k)
                    free(b, k)
                    y_c0.append(k)

            F0, F1 = FW[0:4, 0, :], FW[0:4, 1, :]
            k = AC(lambda e: e.activation(F1, F0, ACT.Abs), cx["fa"])
            k = AC(lambda e: e.activation(F1, F1, ACT.Exp, scale=-1.0), k)
            k1 = AC(lambda e: e.activation(F1, F1, ACT.Ln, bias=1.0), k)
            k = DVE(lambda e: e.tensor_scalar(F0, F0, -1.0, 0.0, ALU.mult, ALU.max), cx["fa"], k1)
            k = DVE(lambda e: e.tensor_tensor(F1, F1, F0, ALU.add), k, k1)
            k2 = DVE(lambda e: e.memset(F0, 1.0), k)
            first = 0.0 if g == 0 else FC[0:4, g * T - 1:g * T]
            cneg = DVE(lambda e: e.tensor_tensor_scan(FC[0:4, g * T:(g + 1) * T], F0, F1, first, ALU.mult, ALU.add),
                       k, k2)
            b, bw = bank()
            for i in range(GB):
                k = PE(lambda e, b=b, i=i: e.transpose(
                    banks[b][:, i * 4:i * 4 + 4], FC[0:4, (g * GB + i) * P:(g * GB + i + 1) * P], IDENT[0:4, 0:4]),
                    *bw, cneg)
            cq_ready = DVE(lambda e, b=b: e.tensor_copy(CQ.rearrange("p i h -> p (i h)"), banks[b][:, 0:4 * GB]), k)
            free(b, cq_ready)
            barrier()
            top[0] = zone
            PB = [carve(512) for _ in range(3)]
            PT = [XS[1][:, 0:512], XS[1][:, 512:1024], carve(512)]
            FT = [XS[0][:, 0:512], XS[0][:, 512:1024]]

            heads = []
            for h in range(4):
                heads.append(("fox", h, (0 + h // 2, h % 2), 0 + h // 2, h * 64, h * 64, 0))
            for h in range(6):
                heads.append(("dil", h, (2 + h // 2, h % 2), 2 + h // 2, 256 + h * 64, 256 + h * 64, 1 + h))
            for h in range(6):
                heads.append(("sel", h, (5 + h // 2, h % 2), 5 + h // 3, 640 + (h // 3) * 64, 640 + h * 64, 7 + h))
            for h in range(6):
                heads.append(("win", h, (5 + h // 2, h % 2), 7 + h // 3, 768 + (h // 3) * 64, 640 + h * 64, 7 + h))
            units = [(n, hd, i) for n, hd in enumerate(heads) for i in range(GB)]
            st = {}
            pb_free = [[], [], []]
            pt_free = [[], [], []]
            ft_free = [[], []]
            fox = {"n": 0}
            y_done = {}

            def scores(u):
                n, (kind, h, (qs, par), ks, _, _, tab), il = units[u]
                i = GB * g + il
                j0 = max(0, i - 1) if kind == "dil" and h < 2 else 0
                w = (i + 1 - j0) * P
                b, bw = bank()
                q = QF[par * 64:par * 64 + 64, qs, il * P:(il + 1) * P]
                kk = KF[par * 64:par * 64 + 64, ks, j0 * P:(i + 1) * P]
                k = PE(mm(banks[b][:, 0:w], q, kk, True, True), *bw)
                end = TAB_AT[tab] + TAB_W[tab]
                t = TABF[:, end - w:end]
                ready = None
                if kind == "fox":
                    if il == 0:
                        held.add(b)
                        cb, cw = bank()
                        held.discard(b)
                        held.add(cb)
                        fox["bank"] = cb, PE(mm(banks[cb][:, 0:(g + 1) * T], SEL[0:4, h, :],
                                                FC[0:4, 0:(g + 1) * T], True, True), *cw, sel_ready)
                    cb, kc = fox["bank"]
                    f = fox["n"] % 2
                    fox["n"] += 1
                    dst = FT[f][:, 0:w]
                    ready = DVE(lambda e: e.tensor_scalar(dst, banks[cb][:, 0:w], CQ[:, il, h:h + 1], None,
                                                          ALU.subtract), kc, cq_ready, ft_free[f], t_tab)
                    if il == GB - 1:
                        held.discard(cb)
                        free(cb, ready)
                    ready = DVE(lambda e, t=t: e.tensor_tensor(dst, dst, t, ALU.add), ready)
                    t = dst
                s = PB[u % 3][:, 0:w]
                k = DVE(lambda e: e.tensor_tensor_reduce(
                    out=s, in0=banks[b][:, 0:w], in1=t, scale=-1.0, scalar=3.0e38, op0=ALU.add, op1=ALU.min,
                    accum_out=NM[:, n, il:il + 1]), k, ready, pb_free[u % 3], t_tab)
                free(b, k)
                if kind == "fox":
                    ft_free[f] = [k]
                k = AC(lambda e: e.activation(s, s, ACT.Exp, bias=NM[:, n, il:il + 1], scale=-1.0,
                                              accum_out=LS[:, n, il:il + 1]), k)
                st[u] = (j0, w, k)

            def turn(u):
                j0, w, k = st[u]
                b, bw = bank()
                PE.wait(k, *bw)
                for j in range(w // P):
                    k2 = PE(lambda e, j=j: e.transpose(banks[b][:, j * P:(j + 1) * P], PB[u % 3][:, j * P:(j + 1) * P],
                                                       IDENT))
                pb_free[u % 3] = [k2]
                k3 = AC(lambda e: e.copy(PT[u % 3][:, 0:w], banks[b][:, 0:w]), k2, pt_free[u % 3])
                free(b, k3)
                st[u] = (j0, w, k3)

            def values(u):
                n, (kind, h, _, _, vc, yc, _), il = units[u]
                j0, w, k = st.pop(u)
                rl = RL[:, n, il:il + 1]
                r = DVE(lambda e: e.reciprocal(rl, LS[:, n, il:il + 1]), k)
                if kind in ("sel", "win"):
                    gt = GS[:, il, h * 3 + (1 if kind == "sel" else 2):h * 3 + (2 if kind == "sel" else 3)]
                    r = DVE(lambda e: e.tensor_tensor(rl, rl, gt, ALU.mult), r, gs_ready)
                b, bw = bank()
                nb = w // P
                PE.wait(k, *bw)
                for j in range(nb):
                    op = mm(banks[b][:, 0:64], PT[u % 3][:, j * P:(j + 1) * P], VT[:, j0 + j, vc:vc + 64],
                            j == 0, j == nb - 1)
                    if j == nb - 1:
                        k2 = PE(op)
                    else:
                        PE.quiet(op)
                pt_free[u % 3] = [k2]
                y = Y[:, il, yc:yc + 64]
                if kind in ("sel", "win"):
                    k3 = DVE(lambda e: e.scalar_tensor_tensor(y, banks[b][:, 0:64], rl, y, ALU.mult, ALU.add),
                             k2, r, y_c0, y_done.get((il, yc)))
                else:
                    k3 = DVE(lambda e: e.tensor_scalar(y, banks[b][:, 0:64], rl, None, ALU.mult), k2, r)
                free(b, k3)
                y_done[il, yc] = k3

            for u in range(len(units) + 3):
                if u < len(units):
                    scores(u)
                if 2 <= u and u - 2 < len(units):
                    turn(u - 2)
                if 3 <= u:
                    values(u - 3)

            k = AC(lambda e: e.activation(AL[:, 0, :, :], LS[:, 4:10, :].rearrange("p h i -> p i h"), ACT.Ln),
                   DVE.last)
            k = DVE(lambda e: e.tensor_tensor(AL[:, 0, :, :], AL[:, 0, :, :],
                                              NM[:, 4:10, :].rearrange("p h i -> p i h"), ALU.subtract), k)
            lse = AL[:, 0, :, :].rearrange("p i (g q) -> p i q g", q=2)
            mx = AL[:, 1, :, 0:2]
            k = DVE(lambda e: e.tensor_reduce(mx, lse, AX, ALU.max), k)
            w3 = AL[:, 2, :, :].rearrange("p i (g q) -> p i q g", q=2)
            k = DVE(lambda e: e.tensor_tensor(w3, lse, mx.unsqueeze(3).to_broadcast([P, GB, 2, 3]), ALU.subtract), k)
            k = AC(lambda e: e.activation(AL[:, 2, :, :], AL[:, 2, :, :], ACT.Exp), k)
            k = DVE(lambda e: e.tensor_reduce(mx, w3, AX, ALU.add), k)
            k = DVE(lambda e: e.reciprocal(mx, mx), k)
            k = DVE(lambda e: e.tensor_tensor(w3, w3, mx.unsqueeze(3).to_broadcast([P, GB, 2, 3]), ALU.mult), k)
            for i in range(GB):
                y = Y[:, i, 256:640].rearrange("p (h d) -> p h d", h=6)
                al = AL[:, 2, i, :].unsqueeze(2).to_broadcast([P, 6, 64])
                DVE(lambda e, y=y, al=al: e.tensor_tensor(y, y, al, ALU.mult), k, DVE.last)
            barrier()
            cx.update(Y=Y, YT=TABF[:, 0:8 * T].rearrange("p (c n) -> p c n", c=8),
                      MG=TABF[:, 8 * T:16 * T].rearrange("p (c n) -> p c n", c=8),
                      GT=[PB[j][:, 0:T] for j in range(3)])

        def merge():
            Y, YT, MG, GT = cx["Y"], cx["YT"], cx["MG"], cx["GT"]
            yt_ready = []
            for t in range(GB):
                for half in range(2):
                    b, bw = bank()
                    PE.wait(*bw)
                    for c in range(4):
                        src = Y[:, t, (half * 4 + c) * P:(half * 4 + c + 1) * P]
                        k = PE(lambda e, b=b, c=c, src=src: e.transpose(banks[b][:, c * P:(c + 1) * P], src, IDENT))
                    dst = YT[:, half * 4:half * 4 + 4, t * P:(t + 1) * P]
                    src = banks[b][:, :].rearrange("p (c n) -> p c n", c=4)
                    ev = AC(lambda e, dst=dst, src=src: e.copy(dst, src), k)
                    free(b, ev)
                    yt_ready.append(ev)
            gt_free = [[], [], []]
            mg_ready = []
            for m4 in range(4):
                wp = weights()
                wg = [weights() for _ in range(3)]
                for j2 in range(2):
                    m = m4 * 2 + j2
                    for j, (c0, cn) in enumerate(((0, 2), (2, 3), (5, 3))):
                        bg, kg = proj_feat(wg[j][1], j2, P, None, wg[j][2])
                        gj = GT[j]
                        kg = AC(lambda e, bg=bg, gj=gj, m=m, j=j: e.activation(
                            gj, banks[bg][:, 0:T], ACT.Sigmoid, bias=col("b_gate", j * 8 + m)), kg, gt_free[j])
                        free(bg, kg)
                        b, bw = bank()
                        PE.wait(wp[2], *bw, yt_ready)
                        for c in range(cn):
                            op = mm(banks[b][:, 0:T], wp[1][:, c0 + c, j2 * P:(j2 + 1) * P], YT[:, c0 + c, :],
                                    c == 0, c == cn - 1)
                            k = PE(op)
                        if j == 0:
                            k = DVE(lambda e, b=b, gj=gj, m=m: e.tensor_tensor(
                                MG[:, m, :], banks[b][:, 0:T], gj, ALU.mult), k, kg)
                            km = k
                        else:
                            k = DVE(lambda e, b=b, gj=gj: e.tensor_tensor(gj, banks[b][:, 0:T], gj, ALU.mult), k, kg)
                            km = DVE(lambda e, gj=gj, m=m: e.tensor_tensor(MG[:, m, :], MG[:, m, :], gj, ALU.add),
                                     k, km)
                        free(b, k)
                        gt_free[j] = [km]
                mg_ready.append(km)
                for i, _, _ in [wp] + wg:
                    done(i, PE.last)
            return add_rows(MG, mg_ready)

        def mlp(x_ready):
            ht_ready = norm_to_ht("g2", x_ready)
            barrier()
            top[0] = base
            UT = carve(NFF, T)
            AB = [carve(T) for _ in range(3)]
            A2 = [carve(T + 2) for _ in range(3)]
            FG = carve(D)
            t_fg = load_all((FG, row("final_g", D)))
            ab_free = [[], [], []]
            for jb in range(11):
                wa, wb = weights(), weights()
                for j2 in range(2):
                    m = jb * 2 + j2
                    ba, ka = proj_feat(wa[1], j2, P, ht_ready, wa[2])
                    bb, kb = proj_feat(wb[1], j2, P, None, wb[2])
                    y, a2, pa = AB[m % 3], A2[m % 3], banks[ba]
                    k0 = AC(lambda e, a2=a2, m=m: e.copy(a2[:, 0:2], AH[:, m, :]), ab_free[m % 3])
                    k1 = AC(lambda e, a2=a2, pa=pa: e.copy(a2[:, 2:T + 2], pa[:, 0:T]), ka)
                    k = AC(lambda e, y=y, pa=pa, m=m: e.activation(y, pa[:, 0:T], ACT.Identity, bias=col("cb", m),
                                                                  scale=col("cw", 44 + m)), k1)
                    free(ba, k)
                    AC(lambda e, a2=a2, m=m: e.copy(AH[:, m, :], a2[:, T:T + 2]), k0, k1)
                    k = DVE(lambda e, y=y, a2=a2, m=m: e.scalar_tensor_tensor(
                        y, a2[:, 1:T + 1], col("cw", 22 + m), y, ALU.mult, ALU.add), k)
                    k = DVE(lambda e, y=y, a2=a2, m=m: e.scalar_tensor_tensor(
                        y, a2[:, 0:T], col("cw", m), y, ALU.mult, ALU.add), k)
                    k = AC(lambda e, y=y: e.activation(y, y, ACT.Gelu_apprx_tanh), k)
                    k = DVE(lambda e, y=y, bb=bb, m=m: e.tensor_tensor(UT[:, m, :], y, banks[bb][:, 0:T], ALU.mult),
                            k, kb)
                    free(bb, k)
                    ab_free[m % 3] = [k, AC.last]
                done(wa[0], kb)
                done(wb[0], kb)
            ut_ready = k
            kx = [None] * GB
            for half in range(2):
                bs = [bank() for _ in range(GB)]
                held.update(b for b, _ in bs)
                for k0, kn in DOWN:
                    i, w, tw = weights()
                    for c in range(kn):
                        for t in range(GB):
                            PE.wait(tw, *bs[t][1], ut_ready)
                            k = PE(mm(banks[bs[t][0]][:, :], UT[:, k0 + c, t * P:(t + 1) * P], w[:, c, :],
                                      k0 + c == 0, k0 + c == NFF - 1))
                    done(i, k)
                    tick()
                for t in range(GB):
                    x = X[:, t, half * 512:half * 512 + 512]
                    kx[t] = DVE(lambda e, x=x, b=bs[t][0]: e.tensor_tensor(x, x, banks[b][:, :], ALU.add), k)
                    free(bs[t][0], kx[t])
                held.clear()
            out = []
            for t in range(GB):
                k = rms(t, kx[t])
                out.append(DVE(lambda e, t=t: e.scalar_tensor_tensor(X[:, t, :], X[:, t, :], SS[:, t + 8:t + 9], FG,
                                                                     ALU.mult, ALU.mult), k, t_fg))
            return out

        def mixer(x_ready):
            NC = T // 32
            ht_ready = norm_to_ht("gm2", x_ready)
            barrier()
            top[0] = base
            MIX = carve(8, T)
            HM, SM, BLK, ONE = carve(P), carve(T), carve(P), carve(P)
            t_c2 = load_all((HM, con("hmask", P)), (SM, con("smask", T)), (BLK, con("blk", P)), (ONE, con("all", P)))
            LB = carve(6, 4)
            DEC = carve(4, NC)
            QD, KD, SG = carve(4, T), carve(4, T), carve(4, T)
            zone = top[0]
            FH, EG, KE = carve(4, T), carve(4, T), carve(4, T)
            top[0] = zone
            ST = carve(NC, 512)
            V2 = carve(GB, 512)
            KET = carve(GB, 4, P)
            ATB = carve(GB, P)
            tmp = arena[:, xs_at:xs_at + 2048]
            TM = [tmp[:, j * T:(j + 1) * T] for j in range(5)]
            U2 = tmp[:, 5 * T:6 * T + 2]
            l0, l1 = col("lb", 0, 4), col("lb", 4, 4)
            k = DVE(lambda e: e.tensor_tensor(LB[:, 0, :], l0, l1, ALU.max))
            k1 = DVE(lambda e: e.tensor_tensor(LB[:, 1, :], l0, LB[:, 0, :], ALU.subtract), k)
            k1 = DVE(lambda e: e.tensor_tensor(LB[:, 2, :], l1, LB[:, 0, :], ALU.subtract), k, k1)
            k = AC(lambda e: e.activation(LB[:, 3:5, :], LB[:, 1:3, :], ACT.Exp), k1)
            k = DVE(lambda e: e.tensor_tensor(LB[:, 4, :], LB[:, 3, :], LB[:, 4, :], ALU.add), k)
            k = DVE(lambda e: e.reciprocal(LB[:, 4, :], LB[:, 4, :]), k)
            k = DVE(lambda e: e.tensor_tensor(LB[:, 0, :], LB[:, 3, :], LB[:, 4, :], ALU.mult), k)
            lb_ready = DVE(lambda e: e.tensor_scalar(LB[:, 5, :], LB[:, 0, :], -1.0, 1.0, ALU.mult, ALU.add), k)

            tm_free = None
            for j4 in range(2):
                wc, wh, wb = weights(), weights(), weights()
                for j2 in range(2):
                    m = j4 * 2 + j2
                    bc, kc = proj_feat(wc[1], j2, P, ht_ready, wc[2])
                    bh, kh = proj_feat(wh[1], j2, P, None, wh[2])
                    bb, kb = proj_feat(wb[1], j2, P, None, wb[2])
                    y = TM[1]
                    k = AC(lambda e, bc=bc: e.copy(TM[2], banks[bc][:, 0:T]), kc, tm_free)
                    free(bc, k)
                    k0 = DVE(lambda e, m=m: e.tensor_copy(U2[:, 0:2], UH[:, m, :]), tm_free)
                    k = DVE(lambda e, bh=bh: e.tensor_tensor(U2[:, 2:T + 2], TM[2], banks[bh][:, 0:T], ALU.mult),
                            k, kh, k0)
                    free(bh, k)
                    k2 = DVE(lambda e, m=m: e.tensor_copy(UH[:, m, :], U2[:, T:T + 2]), k, k0)
                    k = DVE(lambda e, m=m: e.tensor_scalar(y, U2[:, 2:T + 2], col("cw2", 8 + m), None, ALU.mult), k2)
                    k = DVE(lambda e, m=m: e.scalar_tensor_tensor(
                        y, U2[:, 1:T + 1], col("cw2", 4 + m), y, ALU.mult, ALU.add), k)
                    k = DVE(lambda e, m=m: e.scalar_tensor_tensor(
                        y, U2[:, 0:T], col("cw2", m), y, ALU.mult, ALU.add), k)
                    ky = DVE(lambda e, bb=bb: e.tensor_tensor(y, y, banks[bb][:, 0:T], ALU.mult), k, kb)
                    free(bb, ky)
                    k = AC(lambda e: e.activation(TM[3], y, ACT.Square), ky)
                    b, bw = bank()
                    k = PE(mm(banks[b][:, 0:T], BLK, TM[3], True, True), *bw, k, t_c2)
                    k = AC(lambda e, b=b: e.activation(TM[4], banks[b][:, 0:T], ACT.Sqrt, bias=EPS), k)
                    free(b, k)
                    k = DVE(lambda e: e.reciprocal(TM[4], TM[4]), k)
                    tm_free = DVE(lambda e, m=m: e.scalar_tensor_tensor(
                        MIX[:, m, :], y, col("cg2", m), TM[4], ALU.mult, ALU.mult), k)
                for i, _, _ in (wc, wh, wb):
                    done(i, kb)
            for dst, fn in ((QD, ACT.Silu), (SG, ACT.Silu), (FH, ACT.Sigmoid)):
                for j4 in range(2):
                    i, w, tw = weights()
                    for j2 in range(2):
                        b, k = proj_feat(w, j2, P, None, tw)
                        d = dst[:, j4 * 2 + j2, :]
                        ev = AC(lambda e, d=d, b=b, fn=fn: e.activation(d, banks[b][:, 0:T], fn), k)
                        free(b, ev)
                    done(i, k)
            f_ready = ev
            for j4 in range(2):
                i, w, tw = weights()
                for t in range(GB):
                    b, bw = bank()
                    PE.wait(tw, *bw)
                    for c in range(8):
                        k = PE(mm(banks[b][:, 0:256], HT[:, c, t * P:(t + 1) * P], w[:, c, :], c == 0, c == 7))
                    ev = AC(lambda e, b=b, t=t, j4=j4: e.copy(V2[:, t, j4 * 256:j4 * 256 + 256],
                                                              banks[b][:, 0:256]), k)
                    free(b, ev)
                done(i, k)
            v2_ready = ev
            for h in range(4):
                kf = DVE(lambda e, h=h: e.tensor_scalar(FH[:, h, :], FH[:, h, :], LB[:, 5, h:h + 1],
                                                        LB[:, 0, h:h + 1], ALU.mult, ALU.add), f_ready, lb_ready)
            kl = AC(lambda e: e.activation(EG, FH, ACT.Ln), kf)
            k1h = DVE(lambda e: e.tensor_scalar(FH, FH, -1.0, 1.0, ALU.mult, ALU.add), kl)
            hg_ready = []
            for h in range(4):
                G = KD[:, h, :]
                k = DVE(lambda e, h=h, G=G: e.tensor_tensor_scan(G, SM, EG[:, h, :], 0.0, ALU.mult, ALU.add),
                        kl, t_c2)
                G3 = G.rearrange("p (n c) -> p n c", c=32)
                k2 = DVE(lambda e, h=h, G3=G3: e.tensor_tensor(
                    KE[:, h, :].rearrange("p (n c) -> p n c", c=32), G3[:, :, 31:32].to_broadcast([P, NC, 32]), G3,
                    ALU.subtract), k)
                ke = AC(lambda e, h=h: e.activation(KE[:, h, :], KE[:, h, :], ACT.Exp), k2)
                kg = AC(lambda e, h=h, G=G: e.activation(EG[:, h, :], G, ACT.Exp), k)
                kn = AC(lambda e, h=h, G=G: e.activation(G, G, ACT.Exp, scale=-1.0), k2, kg)
                k3 = DVE(lambda e, h=h: e.tensor_tensor(KE[:, h, :], KE[:, h, :], FH[:, h, :], ALU.mult), ke, k1h)
                k4 = DVE(lambda e, h=h, G=G: e.tensor_tensor(G, G, FH[:, h, :], ALU.mult), kn)
                k5 = DVE(lambda e, h=h: e.scalar_tensor_tensor(QD[:, h, :], QD[:, h, :], 128.0 ** -0.5, EG[:, h, :],
                                                               ALU.mult, ALU.mult), kg)
                k6 = DVE(lambda e, h=h: e.tensor_copy(
                    DEC[:, h, :], EG[:, h, :].rearrange("p (n c) -> p n c", c=32)[:, :, 31]), kg)
                hg_ready += [k3, k4, k5, k6]
            ket_ready = []
            for t in range(GB):
                b, bw = bank()
                PE.wait(*bw, hg_ready)
                for h in range(4):
                    k = PE(lambda e, b=b, h=h, t=t: e.transpose(
                        banks[b][:, h * P:(h + 1) * P], KE[:, h, t * P:(t + 1) * P], IDENT))
                ev = AC(lambda e, b=b, t=t: e.copy(KET[:, t, :, :].rearrange("p h n -> p (h n)"), banks[b][:, :]), k)
                free(b, ev)
                ket_ready.append(ev)
            st_ready = []
            prev_state = STP
            for n in range(NC):
                t, j = n // 4, n % 4
                b, bw = bank()
                PE.wait(*bw, ket_ready[t], v2_ready)
                for h in range(4):
                    k = PE(mm(banks[b][:, h * P:(h + 1) * P], KET[j * 32:j * 32 + 32, t, h, :],
                              V2[j * 32:j * 32 + 32, t, h * P:(h + 1) * P], True, True))
                prev = DVE.last
                for h in range(4):
                    k2 = DVE(lambda e, b=b, h=h, n=n, ps=prev_state: e.scalar_tensor_tensor(
                        ST[:, n, h * P:(h + 1) * P], ps[:, h * P:(h + 1) * P], DEC[:, h, n:n + 1],
                        banks[b][:, h * P:(h + 1) * P], ALU.mult, ALU.add), k, prev, ket_ready)
                free(b, k2)
                st_ready.append(k2)
                prev_state = ST[:, n, :]
            zero = DVE(lambda e: e.memset(ATB, 0.0))
            hm = HM.bitcast(U32)
            for h in range(4):
                ba, baw = bank()
                PE.wait(*baw, hg_ready)
                for t in range(GB):
                    k = PE(mm(banks[ba][:, t * P:(t + 1) * P], KD[:, h, t * P:(t + 1) * P],
                              QD[:, h, t * P:(t + 1) * P], True, True))
                for t in range(GB):
                    ka = DVE(lambda e, t=t, ba=ba: e.copy_predicated(ATB[:, t, :], hm,
                                                                     banks[ba][:, t * P:(t + 1) * P]), k, zero)
                free(ba, ka)
                bo, bow = bank()
                for t in range(GB):
                    PE(mm(banks[bo][:, t * P:(t + 1) * P], V2[:, t, h * P:(h + 1) * P], ATB[:, t, :], True, False),
                       ka, *bow)
                    for j in range(4):
                        n = t * 4 + j
                        state = ST[:, n - 1, :] if n else STP
                        k = PE(mm(banks[bo][:, n * 32:n * 32 + 32], state[:, h * P:(h + 1) * P],
                                  QD[:, h, n * 32:n * 32 + 32], False, j == 3), st_ready[n - 1] if n else None)
                o = banks[bo]
                kq = AC(lambda e, o=o: e.activation(TM[0], o[:, 0:T], ACT.Square), k, tm_free)
                b, bw = bank()
                k = PE(mm(banks[b][:, 0:T], ONE, TM[0], True, True), *bw, kq)
                k = AC(lambda e, b=b: e.activation(TM[1], banks[b][:, 0:T], ACT.Sqrt, bias=EPS), k, tm_free)
                free(b, k)
                k = DVE(lambda e: e.reciprocal(TM[1], TM[1]), k)
                k = DVE(lambda e, o=o: e.tensor_tensor(TM[2], o[:, 0:T], TM[1], ALU.mult), k)
                free(bo, k)
                tm_free = DVE(lambda e, h=h: e.scalar_tensor_tensor(MIX[:, 4 + h, :], TM[2], col("hg"), SG[:, h, :],
                                                                    ALU.mult, ALU.mult), k)
            AC(lambda e: e.copy(STP, ST[:, NC - 1, :]), PE.last, DVE.last)
            xs_free[0] = xs_free[1] = [tm_free]
            return add_rows(MIX, tm_free)

        out_sem = [[newsem(f"s_out{j}"), 0] for j in range(NT)]
        ov = a["out"].rearrange("(t p) d -> t p d", p=P)
        h2_ready = {}
        gat = {}
        issued = {}

        def queries(g, x_ready):
            barrier()
            top[0] = base + 8 * T
            ex = {"KEYS": carve(16, P), "QT": carve(16, T), "CAND": carve(8, 256),
                  "SR": [carve(P) for _ in range(2)], "T16": carve(8, 2, 16), "I16": carve(8, 2, 16).bitcast(U32),
                  "IF": carve(8, 2, 16), "CSC": carve(8, 16), "CIX": carve(8, 16).bitcast(U32),
                  "HL": carve(2, 8, 16), "HLI": carve(2, 8, 16).bitcast(U32), "EX": carve(2, 8, 16), "GM": carve(8)}
            gain = ex["CAND"].rearrange("p a b -> p (a b)")[:, 0:D]
            t_k = load_all((gain, row("norm_ffn", D)))
            t_keys = load_all((ex["KEYS"], a["keys"].rearrange("p (j n) -> p j n", j=16)))

            def keep(t, k):
                h2_ready[GB * g + t] = DVE(lambda e: e.tensor_tensor(H2[:, t, :], XS[t % 2], gain, ALU.mult), k, t_k)
                return h2_ready[GB * g + t]

            ht_ready = norm_to_ht("gf2", x_ready, keep)
            for t in range(GB):
                old = out_sem[GB * (g - 1) + t] if g else None
                acc = DVE(lambda e, t=t: e.tensor_copy(ACC[t], X[:, t, :]), x_ready[t],
                          (old[0], 16) if old else None)
            for c8 in range(8):
                i, w, tw = weights()
                for j2 in range(2):
                    b, k = proj_feat(w, j2, P, ht_ready, tw)
                    m = c8 * 2 + j2
                    ev = AC(lambda e, b=b, m=m: e.copy(ex["QT"][:, m, :], banks[b][:, 0:T]), k)
                    free(b, ev)
                done(i, k)
            ex["ready"] = [ev, t_keys, acc]
            return ex

        def top_sixteen(values, indices, s, rest, ready):
            lo, hi = values[:, 0:8], values[:, 8:16]
            k1 = DVE(lambda e: e.max(lo, s), ready, DVE.last)
            k2 = DVE(lambda e: e.max_index(indices[:, 0:8], lo, s), k1)
            k2 = DVE(lambda e: e.match_replace(rest, lo, s, -3.0e38), k2)
            k3 = DVE(lambda e: e.max(hi, rest), k2)
            k4 = DVE(lambda e: e.max_index(indices[:, 8:16], hi, rest), k3)
            return k2, k4

        def choose(t, ex):
            par, tl = t % 2, t % GB
            T16, I16, IF, CAND, CSC, CIX = (ex[n] for n in ("T16", "I16", "IF", "CAND", "CSC", "CIX"))
            HL, HLI, EX, GM, SR = (ex[n] for n in ("HL", "HLI", "EX", "GM", "SR"))
            for b4 in range(4):
                b, bw = side_bank()
                PE.wait(*bw, ex["ready"])
                for c in range(4):
                    m = b4 * 4 + c
                    k = PE(mm(banks[b][:, c * P:(c + 1) * P], ex["QT"][:, m, tl * P:(tl + 1) * P],
                              ex["KEYS"][:, m, :], True, True))
                for c in range(4):
                    m = b4 * 4 + c
                    h, half = m // 2, m % 2
                    s = banks[b][:, c * P:(c + 1) * P]
                    k2, k4 = top_sixteen(T16[:, h, half, :], I16[:, h, half, :], s, SR[m % 2], k)
                    if c == 3:
                        free(b, k2)
                    yield 1.3
            kf = DVE(lambda e: e.tensor_copy(IF, I16), k4, DVE.last)
            cand = CAND.rearrange("p h (a b) -> p h a b", a=16)
            for h in range(8):
                s1 = T16[:, h, 0, :].unsqueeze(2).to_broadcast([P, 16, 16])
                s2 = T16[:, h, 1, :].unsqueeze(1).to_broadcast([P, 16, 16])
                k = DVE(lambda e, h=h, s1=s1, s2=s2: e.tensor_tensor(cand[:, h, :, :], s1, s2, ALU.add), k4, DVE.last)
                _, k = top_sixteen(CSC[:, h, :], CIX[:, h, :], CAND[:, h, :], CAND[:, h, :], k)
                yield 2.2
            k1 = DVE(lambda e: e.tensor_scalar(HLI[:, 0, :, :], CIX, 4, None, ALU.logical_shift_right), k)
            k2 = DVE(lambda e: e.tensor_scalar(HLI[:, 1, :, :], CIX, 15, None, ALU.bitwise_and), k)
            k = DVE(lambda e: e.tensor_copy(HL, HLI), k1, k2)
            OH = CAND.rearrange("p h (j a) -> p h j a", j=16)
            for half in range(2):
                hl = HL[:, half, :, :].rearrange("p h j -> p (h j)").unsqueeze(2).to_broadcast([P, 128, 16])
                io = IOTA.unsqueeze(1).to_broadcast([P, 128, 16])
                oh = OH.rearrange("p h j a -> p (h j) a")
                k = DVE(lambda e, oh=oh, hl=hl, io=io: e.tensor_tensor(oh, hl, io, ALU.is_equal), k, DVE.last)
                yield 2.2
                ib = IF[:, :, half, :].unsqueeze(2).to_broadcast([P, 8, 16, 16])
                k = DVE(lambda e, ib=ib: e.tensor_tensor(OH, OH, ib, ALU.mult), k, kf)
                yield 2.2
                k = DVE(lambda e, half=half: e.tensor_reduce(EX[:, half, :, :], OH, AX, ALU.add), k)
                yield 2.2
            k = DVE(lambda e: e.scalar_tensor_tensor(EX[:, 0, :, :], EX[:, 0, :, :], 128.0, EX[:, 1, :, :],
                                                     ALU.mult, ALU.add), k)
            ei = DVE(lambda e: e.tensor_copy(EI[par].rearrange("p (h j) -> p h j", h=8), EX[:, 0, :, :]), k,
                     issued.get(t - 2))
            gw = GW[par].rearrange("p (h j) -> p h j", h=8)
            k = DVE(lambda e: e.tensor_tensor(gw, CSC, CSC[:, :, 0:1].to_broadcast([P, 8, 16]), ALU.subtract), k)
            k = AC(lambda e: e.activation(gw, gw, ACT.Exp), k)
            k = DVE(lambda e: e.tensor_reduce(GM, gw, AX, ALU.add), k)
            k = DVE(lambda e: e.reciprocal(GM, GM), k)
            k = DVE(lambda e: e.tensor_tensor(gw, gw, GM.unsqueeze(2).to_broadcast([P, 8, 16]), ALU.mult), k)
            gat[t] = (ei, k)

        slot_sem = [[newsem(f"s_g{i}"), 0] for i in range(16)]
        slot_free = [None] * 16

        def experts(g, ex, slots):
            yield from choose(GB * g, ex)
            jobs = [(GB * g + t, which, k) for t in range(GB) for which in range(2) for k in range(P)]
            where = {}
            ns = len(slots)

            def gather(n):
                t, which, k = jobs[n]
                s = n % ns
                tab = a["peer_u_2"] if which == 0 else a["peer_v_2"]
                off = EI[t % 2][:, k:k + 1]
                where[n] = GP.dma(lambda e: e.indirect_dma_start(
                    out=slots[s], out_offset=None, in_=tab, in_offset=bass.IndirectOffsetOnAxis(ap=off, axis=0)),
                    slot_sem[s], gat[t][0], slot_free[s])
                if (which, k) == (1, P - 1):
                    issued[t] = where[n]

            for n in range(ns):
                gather(n)
            later = choose(GB * g + 1, ex)
            chain = None
            for n, (t, which, k) in enumerate(jobs):
                tl, s = t % GB, n % ns
                if which == 0:
                    tok = DVE(lambda e, s=s, t=t, tl=tl, k=k: e.tensor_tensor_reduce(
                        out=slots[s], in0=slots[s], in1=H2[:, tl, :], scale=1.0, scalar=0.0, op0=ALU.mult,
                        op1=ALU.add, accum_out=AA[t % 2][:, k:k + 1]), where[n], h2_ready[t], DVE.last)
                    if k == P - 1:
                        kk = AC(lambda e, t=t: e.activation(AA[t % 2], AA[t % 2], ACT.Gelu), tok)
                        w_ready = DVE(lambda e, t=t: e.tensor_tensor(AA[t % 2], AA[t % 2], GW[t % 2], ALU.mult),
                                      kk, gat[t][1])
                else:
                    tok = DVE(lambda e, s=s, t=t, tl=tl, k=k: e.scalar_tensor_tensor(
                        ACC[tl], slots[s], AA[t % 2][:, k:k + 1], ACC[tl], ALU.mult, ALU.add),
                        where[n], w_ready, chain)
                    chain = tok
                slot_free[s] = tok
                if n + ns < len(jobs):
                    if jobs[n + ns][0] not in gat:
                        for _ in later:
                            pass
                    gather(n + ns)
                more = next(later, None)
                yield STEP + (0 if more is None else 0)
                if which == 1 and k == P - 1:
                    acc, h2 = ACC[tl], H2[:, tl, :]
                    kk = AC(lambda e, acc=acc, h2=h2: e.activation(h2, acc, ACT.Square, accum_out=SS[:, 12:13]), tok)
                    kk = AC(lambda e: e.activation(SS[:, 13:14], SS[:, 12:13], ACT.Sqrt, bias=EPS, scale=1.0 / D), kk)
                    kk = DVE(lambda e: e.reciprocal(SS[:, 14:15], SS[:, 13:14]), kk)
                    kk = DVE(lambda e, acc=acc: e.scalar_tensor_tensor(acc, acc, SS[:, 14:15], NF, ALU.mult,
                                                                       ALU.mult), kk, t_nf)
                    AC.dma(lambda e, t=t, acc=acc: e.dma_start(ov[t], acc), out_sem[t], kk)

        for g in range(NT // GB):
            top[0] = base
            project(g, x_in)
            if side[0] is not None:
                while side[0] is not None and GB * g - 1 not in gat:
                    if next(side[0], None) is None:
                        side[0] = None
                spent[0] = 0.0
            barrier()
            attend(g)
            x_ready = merge()
            x_ready = mlp(x_ready)
            x_ready = mixer(x_ready)
            while side[0] is not None:
                if next(side[0], None) is None:
                    side[0] = None
            ex = queries(g, x_ready)
            if g + 1 < NT // GB:
                x_in = load_x(g + 1, DVE.last, AC.last)
                side[0] = experts(g, ex, slots8)
                for _ in range(HEAD):
                    next(side[0])
                spent[0] = 0.0
            else:
                barrier()
                more = [ring[j // 2][:, (j % 2) * D:(j % 2) * D + D] for j in range(2 * RING)]
                for _ in experts(g, ex, slots8 + more):
                    pass
        for s in out_sem + slot_sem + ring_sem + x_sem + sems + [small]:
            SP.wait((s[0], s[1]))

        def run(q):
            def body(e):
                for op in q.ops:
                    op(e)
            return body

        block.tensor(run(PE))
        block.vector(run(DVE))
        block.scalar(run(AC))
        block.gpsimd(run(GP))
        block.sync(run(SP))


def kernel(**inputs):
    import concourse.bacc as _bacc
    from concourse.bass_utils import run_bass_kernel_spmd as _run

    x = {n: np.ascontiguousarray(v) for n, v in inputs.items()}

    def pad(v, n=P):
        return np.concatenate([v, np.zeros((n - v.shape[0],) + v.shape[1:], v.dtype)], 0) if v.shape[0] < n else v

    def by(v):
        return v.reshape(-1, P).T

    b = x["b_in"][0]
    cols = np.concatenate([
        by(x["norm1_g"][0]), by(b[QA:QA + 256]), by(b[KA:KA + 256]), by(b[QB:QB + 384]), by(b[KB:KB + 384]),
        by(b[QC:QC + 384]), by(b[KC:KC + 128]), by(b[VC:VC + 128]), by(b[KSL:KSL + 128]), by(b[KWN:KWN + 128]),
        pad(b[FA:FA + 4].reshape(4, 1)), by(b[GATES:]), by(x["norm2_g"][0]),
        by(x["conv_w"][0].reshape(-1)), by(x["conv_b"][0]), by(x["norm_mix_2"][0]),
        by(x["conv_w_2"][0].reshape(-1)), by(x["conv_gain_2"][0]), by(x["hg_lb_logits_2"].reshape(-1)),
        by(x["hg_gain_2"][0]), by(x["norm_ffn_2"][0]),
        np.concatenate([x["cmp_pe"][0].T, x["cmp_pe"][0].T], 0)], 1)
    rows = np.concatenate([b[VA:VA + 256], b[VB:VB + 384], b[VSL:VSL + 128], b[VWN:VWN + 128], b[GC:GC + 18],
                           x["final_g"], x["norm_ffn_2"][0], x["norm_f_2"]])[None]
    keys = x["peer_keys_2"][0].transpose(3, 0, 1, 2).reshape(P, 16 * P)
    arrays = {"x": x["x"][0], "cols": cols, "rows": rows, "keys": keys, "con": constants()}
    for n in ("w_in", "cmp_k_w1", "cmp_k_w2", "cmp_v_w1", "cmp_v_w2", "w_pa", "w_pb", "w_pc", "w_o", "w_up",
              "w_down", "w_in_2", "w_out_2", "peer_wq_2", "peer_u_2", "peer_v_2"):
        arrays[n] = x[n][0]
    nc = _bacc.Bacc("TRN2", target_bir_lowering=False, num_devices=1)
    sent, aps = {}, {}
    for n, v in arrays.items():
        v = np.ascontiguousarray(v)
        sent[f"in_{n}"] = v
        aps[n] = nc.dram_tensor(f"in_{n}", v.shape, mybir.dt.from_np(v.dtype), kind="ExternalInput").ap()
    aps["out"] = nc.dram_tensor("out_0", (S, D), F32, kind="ExternalOutput").ap()
    build(nc, aps)
    r = _run(nc, [sent], core_ids=[0])
    return r.results[0]["out_0"].reshape(1, S, D)
```

```python
from contextlib import ExitStack

import numpy as np
import concourse.bass as bass
from concourse import mybir

ALU = mybir.AluOpType
ACT = mybir.ActivationFunctionType
F32 = mybir.dt.float32
U32 = mybir.dt.uint32
AX = mybir.AxisListType.X

P = 128
S = 512
D = 1024
NT = S // P
GB = 2
T = GB * P
STEP = 1.8
UNIT = 2.3
CHOICE = 18
STATE, CONV, NORM = 3.5, 3, 4
NEG = -1e30
TINY = 1e-30
FF = 2816
NFF = FF // P

QA, KA, VA, FA = 0, 256, 512, 768
QB, KB, VB = 772, 1156, 1540
QC, KC, VC, KSL, VSL, KWN, VWN, GC, GATES = 1924, 2308, 2436, 2564, 2692, 2820, 2948, 3076, 3094

COL = {}
_at = 0
for _name, _n in (("g1", 8), ("b_qa", 2), ("b_qb", 3), ("b_qc", 3), ("b_ka", 2), ("b_kb", 3), ("b_kc", 1),
                  ("b_vc", 1), ("b_ksl", 1), ("b_kwn", 1), ("b_fa", 1), ("b_gate", 24), ("g2", 8),
                  ("cw", 66), ("cb", 22), ("gm2", 8), ("cw2", 12), ("cg2", 4), ("lb", 8), ("hg", 1),
                  ("gf2", 8), ("pe", 32)):
    COL[_name] = _at
    _at += _n
NCOL = _at

ROW = {}
_at = 0
for _name, _n in (("bv", 914), ("final_g", 1024), ("norm_ffn", 1024), ("norm_f", 1024)):
    ROW[_name] = _at
    _at += _n
NROW = _at

TAB_W = [512, 256, 256] + [512] * 10
TAB_AT = [sum(TAB_W[:n]) for n in range(13)]

CON = {}
_at = 0
for _name, _n in (("ident", 128), ("iota", 16), ("eps", 1), ("tab", 6144), ("ctab", 768), ("cmask", 768),
                  ("hmask", 128), ("smask", 512), ("blk", 128), ("all", 128)):
    CON[_name] = _at
    _at += _n
NCON = _at


def constants():
    c = np.zeros((P, NCON), np.float32)
    p = np.arange(P)
    c[:, CON["ident"]:CON["ident"] + P] = np.eye(P, dtype=np.float32)
    c[:, CON["iota"]:CON["iota"] + 16] = np.arange(16, dtype=np.float32)
    c[:, CON["eps"]] = 1e-6
    slopes = np.exp2(-8.0 * np.arange(1, 13, dtype=np.float32) / 12).astype(np.float32)
    dist = p[:, None] - (np.arange(512)[None, :] - 384)
    dil, nsa = slopes[0::2], slopes[1::2]
    tabs = [np.where(dist >= 0, 0.0, NEG)]
    assert len(TAB_W) == 13
    for h in range(6):
        w, r = ((128, 1), (512, 4), (2048, 16))[h // 2]
        ok = (dist >= 0) & (dist <= w) & (dist % r == 0)
        tabs.append(np.where(ok, -dil[h] * dist.astype(np.float32), NEG)[:, 512 - TAB_W[1 + h]:])
    for h in range(6):
        tabs.append(np.where(dist >= 0, -nsa[h] * dist.astype(np.float32), NEG))
    c[:, CON["tab"]:CON["tab"] + 6144] = np.concatenate(tabs, 1).astype(np.float32)
    ct = np.full((P, 2, NT, 3, 32), NEG, np.float32)
    cm = np.zeros((P, 2, NT, 3, 32), np.float32)
    end = np.arange(31) * 16 + 31
    for par in range(2):
        for i in range(NT):
            d = (i * P + p)[:, None] - end[None, :]
            for hh in range(3):
                ct[:, par, i, hh, :31] = np.where(d >= 0, -nsa[2 * hh + par] * d.astype(np.float32), NEG)
                cm[:, par, i, hh, :31] = d >= 0
    c[:, CON["ctab"]:CON["ctab"] + 768] = ct.reshape(P, 768)
    c[:, CON["cmask"]:CON["cmask"] + 768] = cm.reshape(P, 768)
    c[:, CON["hmask"]:CON["hmask"] + P] = (p[:, None] // 32 == p[None, :] // 32) & (p[:, None] <= p[None, :])
    c[:, CON["smask"]:CON["smask"] + 512] = np.arange(512) % 32 != 0
    c[:, CON["blk"]:CON["blk"] + P] = (p[:, None] // 64 == p[None, :] // 64) / 64.0
    c[:, CON["all"]:CON["all"] + P] = 1 / 128.0
    return c


class Queue:

    def __init__(self, sem):
        self.sem, self.n, self.ops, self.seen = sem, 0, [], {}

    def wait(self, *tokens):
        for t in tokens:
            if t is None:
                continue
            if isinstance(t, list):
                self.wait(*t)
                continue
            sem, value = t
            if self.seen.get(id(sem), 0) >= value:
                continue
            self.seen[id(sem)] = value
            self.ops.append(lambda e, sem=sem, value=value: e.wait_ge(sem, value))

    def __call__(self, fn, *tokens):
        self.wait(*tokens)
        self.n += 1
        self.ops.append(lambda e: fn(e).then_inc(self.sem, 1))
        return (self.sem, self.n)

    def quiet(self, fn, *tokens):
        self.wait(*tokens)
        self.ops.append(fn)

    def dma(self, fn, sem, *tokens):
        self.wait(*tokens)
        sem[1] += 16
        self.ops.append(lambda e, s=sem[0]: fn(e).then_inc(s, 16))
        return (sem[0], sem[1])

    @property
    def last(self):
        return (self.sem, self.n)


def build(nc, a):
    ctx = ExitStack()
    with ctx:
        def newsem(name):
            return ctx.enter_context(nc.semaphore(name))

        arena = ctx.enter_context(nc.sbuf_tensor("arena", [P, 53150], F32))
        banks = [ctx.enter_context(nc.psum_tensor(f"bank{i}", [P, 512], F32)) for i in range(8)]
        PE, DVE, AC, GP, SP = (Queue(newsem(n)) for n in ("s_pe", "s_dve", "s_act", "s_pool", "s_sp"))
        block = ctx.enter_context(nc.Block())

        top = [0]

        def carve(*shape):
            n = 1
            for s in shape:
                n *= s
            at = top[0]
            top[0] += n
            assert top[0] <= 53150, top[0]
            v = arena[:, at:at + n]
            if len(shape) == 2:
                v = v.rearrange("p (a b) -> p a b", a=shape[0])
            elif len(shape) == 3:
                v = v.rearrange("p (a b c) -> p a b c", a=shape[0], b=shape[1])
            elif len(shape) == 4:
                v = v.rearrange("p (a b c d) -> p a b c d", a=shape[0], b=shape[1], c=shape[2])
            return v

        X = carve(GB, D)
        HT = carve(8, T)
        COLS = carve(NCOL)
        FIX = carve(145)
        IDENT, IOTA, EPS = FIX[:, 0:128], FIX[:, 128:144], FIX[:, 144:145]
        SS = carve(16)
        RING = 4
        ring = [carve(2048) for _ in range(RING)]
        xs_at = top[0]
        XS = [carve(D) for _ in range(2)]
        KF = carve(11, S)
        VT = carve(NT, 914)
        SEL = carve(4, P)
        FC = carve(S)
        HID = carve(2, 2, 62)
        KCT = carve(62)
        VCB = carve(2, 192)
        AH = carve(NFF, 2)
        UH = carve(4, 2)
        BQ = carve(8)
        ONER = carve(P)
        STP = carve(512)
        slots_at = top[0]
        slots7 = [carve(D) for _ in range(7)]
        jk_at = top[0]
        JK = carve(D)
        H2 = carve(GB, D)
        ACC = [carve(D) for _ in range(GB)]
        nf_at = top[0]
        NF = carve(D)
        EI = [carve(P).bitcast(U32) for _ in range(2)]
        GW = [carve(P) for _ in range(2)]
        AA = [carve(P) for _ in range(2)]
        NM, LS, RL = carve(22, GB), carve(22, GB), carve(22, GB)
        CQ, AL, GS, CS = carve(GB, 4), carve(4, GB, 6), carve(GB, 18), carve(2, GB * 3)
        base = top[0]

        def col(name, j=0, n=1):
            return COLS[:, COL[name] + j:COL[name] + j + n]

        def con(name, n, off=0):
            return a["con"][:, CON[name] + off:CON[name] + off + n]

        psum_at = [0, 0]
        psum_readers = [[] for _ in range(8)]
        held = set()
        spent = [0.0]
        side = [None]

        def tick():
            while side[0] is not None and spent[0] > 0:
                cost = next(side[0], None)
                if cost is None:
                    side[0] = None
                else:
                    spent[0] -= cost

        def bank():
            if side[0] is None:
                spent[0] = 0.0
            tick()
            while psum_at[0] % 6 in held:
                psum_at[0] += 1
            b = psum_at[0] % 6
            psum_at[0] += 1
            w = psum_readers[b]
            psum_readers[b] = []
            return b, w

        def side_bank():
            b = 6 + psum_at[1] % 2
            psum_at[1] += 1
            w = psum_readers[b]
            psum_readers[b] = []
            return b, w

        def free(b, *tokens):
            psum_readers[b] += tokens

        def kcols(w, c0, n):
            return [(w.rearrange("(c p) n -> p c n", p=P)[:, :, c0:c0 + n], 8, 0, n)]

        w_in, w_in2 = a["w_in"], a["w_in_2"]
        FEAT1 = [("qa", QA, 256), ("ka", KA, 256), ("qb", QB, 256), ("qb", QB + 256, 128),
                 ("kb", KB, 256), ("kb", KB + 256, 128), ("qc", QC, 256), ("qc", QC + 256, 128),
                 ("kvc", KC, 256), ("ksl", KSL, 128), ("kwn", KWN, 128), ("fa", FA, 4)]
        TOK1 = [(VA, 256, 0), (VB, 256, 256), (VB + 256, 128, 512), (VSL, 128, 640), (VWN, 146, 768)]
        plan = [(kcols(w_in, c0, n), n) for _, c0, n in FEAT1]
        plan += [(kcols(w_in, c0, n), n) for c0, n, _ in TOK1]
        for w in (a["cmp_k_w1"], a["cmp_v_w1"]):
            for half in range(2):
                plan.append(([(w.rearrange("(c p) n -> p c n", p=P)[:, half * 8:half * 8 + 8, :], 8, 0, 256)], 256))
        for mm in range(4):
            parts = [(a["w_pa"], 0, 2), (a["w_pb"], 2, 3), (a["w_pc"], 5, 3)]
            plan.append(([(w.rearrange("(c p) n -> p c n", p=P)[:, :, mm * 256:mm * 256 + 256], k, c, 256)
                          for w, c, k in parts], 256))
            for j in range(3):
                plan.append((kcols(w_in, GATES + j * D + mm * 256, 256), 256))
        plan += [(kcols(a["w_o"], c * 256, 256), 256) for c in range(4)]
        for j in range(11):
            plan += [(kcols(a["w_up"], j * 256, 256), 256), (kcols(a["w_up"], FF + j * 256, 256), 256)]
        DOWN = [(0, 4), (4, 4), (8, 4), (12, 4), (16, 4), (20, 2)]
        for half in range(2):
            for k0, kn in DOWN:
                plan.append(([(a["w_down"].rearrange("(c p) n -> p c n", p=P)
                               [:, k0:k0 + kn, half * 512:half * 512 + 512], kn, 0, 512)], 512))
        plan += [(kcols(w_in2, c0, 256), 256) for c0 in (2048, 2304, 1536, 1792, 3072, 3328, 2560, 2816)]
        for j in range(2):
            plan += [(kcols(w_in2, s * 512 + j * 256, 256), 256) for s in (0, 1, 2)]
        plan += [(kcols(a["w_out_2"], c * 256, 256), 256) for c in range(4)]
        plan += [(kcols(a["peer_wq_2"], c * 256, 256), 256) for c in range(8)]

        plan = plan * (NT // GB)

        ring_sem = [[newsem(f"s_w{i}"), 0] for i in range(RING)]
        landed = {}
        nxt = [0]

        def load_weights(i, *tokens):
            if i >= len(plan):
                return
            parts, width = plan[i]
            s = i % RING
            for src, k, c, w in parts:
                dst = ring[s].rearrange("p (c n) -> p c n", n=256 if width <= 256 else 512)[:, c:c + k, 0:w]
                landed[i] = SP.dma(lambda e, dst=dst, src=src: e.dma_start(dst, src), ring_sem[s], *tokens)

        def weights():
            i = nxt[0]
            nxt[0] += 1
            width = plan[i][1]
            return i, ring[i % RING].rearrange("p (c n) -> p c n", n=256 if width <= 256 else 512), landed[i]

        def done(i, token):
            load_weights(i + RING, token)

        def barrier():
            lasts = [q.last for q in (PE, DVE, AC, GP)]
            for q in (PE, DVE, AC, GP, SP):
                q.wait(*lasts)

        def mm(out, lhsT, rhs, start, stop):
            spent[0] += 4 * rhs.shape[-1] / 2400.0
            return lambda e: e.matmul(out, lhsT, rhs, start=start, stop=stop)

        small = [newsem("s_small"), 0]
        x_sem = [[newsem(f"s_x{t}"), 0] for t in range(NT)]

        xv = a["x"].rearrange("(t p) d -> t p d", p=P)

        def load_x(g, *tokens):
            return [AC.dma(lambda e, t=t: e.dma_start(X[:, t, :], xv[GB * g + t]), x_sem[GB * g + t], *tokens)
                    for t in range(GB)]

        x_in = load_x(0)
        for dst, src in ((COLS, a["cols"]), (FIX, con("ident", 145))):
            t_small = AC.dma(lambda e, dst=dst, src=src: e.dma_start(dst, src), small)
        for i in range(RING):
            load_weights(i, x_in if i else None)
        sems = []

        def load_all(*pairs, wait=()):
            s = [newsem(f"s_l{len(sems)}"), 0]
            sems.append(s)
            for dst, src in pairs:
                t = AC.dma(lambda e, dst=dst, src=src: e.dma_start(dst, src), s, *wait)
            return t

        def row(name, n):
            return a["rows"][0:1, ROW[name]:ROW[name] + n].to_broadcast([P, n])

        nf_in = []
        DVE(lambda e: e.memset(AH, 0.0))
        DVE(lambda e: e.memset(UH, 0.0))
        DVE(lambda e: e.memset(STP, 0.0))
        vcb0 = DVE(lambda e: e.memset(VCB, 0.0))
        DVE(lambda e: e.memset(ONER[0:1, :], 1.0))
        DVE(lambda e: e.tensor_scalar(BQ, col("b_qa", 0, 8), 0.125, None, ALU.mult), t_small)
        sel_ready = DVE(lambda e: e.tensor_copy(
            SEL[0:4, :, :], IDENT[0:4, 0:4].unsqueeze(2).to_broadcast([4, 4, P])), t_small)

        xs_free = [[], []]

        def rms(t, ready):
            k = AC(lambda e: e.activation(XS[t % 2], X[:, t, :], ACT.Square, accum_out=SS[:, t:t + 1]),
                   ready, t_small, xs_free[t % 2])
            k = AC(lambda e: e.activation(SS[:, t + 4:t + 5], SS[:, t:t + 1], ACT.Sqrt, bias=EPS, scale=1.0 / D), k)
            return DVE(lambda e: e.reciprocal(SS[:, t + 8:t + 9], SS[:, t + 4:t + 5]), k)

        def norm_to_ht(gain, ready, keep=None):
            out = []
            rs = [rms(t, ready[t]) for t in range(GB)]
            for t in range(GB):
                k = rs[t]
                k = AC(lambda e, t=t: e.activation(XS[t % 2], X[:, t, :], ACT.Copy, scale=SS[:, t + 8:t + 9]), k)
                tr = [keep(t, k)] if keep is not None else []
                spent[0] += NORM
                for half in range(2):
                    b, w = bank()
                    for c in range(4):
                        src = XS[t % 2][:, (half * 4 + c) * P:(half * 4 + c + 1) * P]
                        k2 = PE(lambda e, b=b, c=c, src=src: e.transpose(banks[b][:, c * P:(c + 1) * P], src, IDENT),
                                k, *w)
                    tr.append(k2)
                    if half:
                        for c in range(4):
                            k3 = AC(lambda e, b=b, c=c, t=t: e.activation(
                                HT[:, 4 + c, t * P:(t + 1) * P], banks[b][:, c * P:(c + 1) * P], ACT.Copy,
                                scale=col(gain, 4 + c)), k2, t_small)
                        free(b, k3)
                        out.append(k3)
                        continue
                    dst = HT[:, half * 4:half * 4 + 4, t * P:(t + 1) * P]
                    gn = col(gain, half * 4, 4).unsqueeze(2).to_broadcast([P, 4, P])
                    src = banks[b][:, :].rearrange("p (c n) -> p c n", c=4)
                    k3 = DVE(lambda e, dst=dst, src=src, gn=gn: e.tensor_tensor(dst, src, gn, ALU.mult), k2, t_small,
                             PE.last)
                    free(b, k3)
                    out.append(k3)
                xs_free[t % 2] = tr
            return out

        def proj_feat(w, j, n, ready, *extra):
            b, bw = bank()
            PE.wait(ready, *extra, *bw)
            for c in range(8):
                op = mm(banks[b][0:n, 0:T], w[:, c, j * P:j * P + n], HT[:, c, :], c == 0, c == 7)
                if c < 7:
                    PE.quiet(op)
                else:
                    k = PE(op)
            return b, k

        def add_rows(src, ready):
            out = [None] * GB
            for c4 in range(4):
                i, w, tw = weights()
                for t in range(GB):
                    b, bw = bank()
                    PE.wait(tw, *bw, ready)
                    for c in range(8):
                        op = mm(banks[b][:, 0:256], src[:, c, t * P:(t + 1) * P], w[:, c, :], c == 0, c == 7)
                        if c == 7:
                            k = PE(op)
                        else:
                            PE.quiet(op)
                    x = X[:, t, c4 * 256:c4 * 256 + 256]
                    out[t] = DVE(lambda e, b=b, x=x: e.tensor_tensor(x, x, banks[b][:, 0:256], ALU.add), k)
                    free(b, out[t])
                done(i, k)
            return out

        slot = {"qa": 0, "qb": 2, "qc": 5, "ka": 0, "kb": 2, "ksl": 5, "kwn": 7, "kvc": 9}
        cx = {}

        def project(g, ready):
            tok = slice(g * T, (g + 1) * T)
            QF = carve(8, T)
            FW = XS[1][:, 0:2 * T].rearrange("p (a b) -> p a b", a=2)
            if g == 0:
                at = top[0]
                top[0] = slots_at + D
                FW = carve(2, T)
                top[0] = at
            BV = XS[0][0:1, 0:914]
            ht_ready = norm_to_ht("g1", ready)
            t_bv = load_all((BV, a["rows"][0:1, ROW["bv"]:ROW["bv"] + 914]), wait=(xs_free[0], xs_free[1]))
            if g == 0:
                at = top[0]
                cx["tab"] = load_all((carve(6144), con("tab", 6144)))
                top[0] = at
            seen = {}
            for name, c0, n in FEAT1:
                i, w, tw = weights()
                for j in range((n + P - 1) // P):
                    b, k = proj_feat(w, j, min(n, P), ht_ready, tw)
                    if name == "fa":
                        bias = COLS[0:4, COL["b_fa"]:COL["b_fa"] + 1]
                        ev = [AC(lambda e, b=b, bias=bias: e.activation(
                            FW[0:4, 0, :], banks[b][0:4, 0:T], ACT.Identity, bias=bias), k, xs_free[1])]
                        fa_ready = ev
                    elif name in ("ksl", "kwn"):
                        ev = []
                        for q in range(2):
                            for half in range(2):
                                dst = KF[half * 64:half * 64 + 64, slot[name] + q, tok]
                                src = banks[b][q * 64:q * 64 + 64, 0:T]
                                bias = COLS[q * 64:q * 64 + 64, COL["b_" + name]:COL["b_" + name] + 1]
                                ev.append(AC(lambda e, dst=dst, src=src, bias=bias:
                                             e.activation(dst, src, ACT.Identity, bias=bias), k))
                    else:
                        m = seen.get(name, 0)
                        seen[name] = m + 1
                        bias = col("b_" + name, m) if name != "kvc" else col("b_kc" if m == 0 else "b_vc")
                        if name[0] == "q":
                            dst = QF[:, slot[name] + m, :]
                            bias = BQ[:, slot[name] + m:slot[name] + m + 1]
                            ev = [AC(lambda e, dst=dst, b=b, bias=bias: e.activation(
                                dst, banks[b][:, 0:T], ACT.Identity, bias=bias, scale=0.125), k, sel_ready)]
                        else:
                            dst = KF[:, slot[name] + m, tok]
                            ev = [AC(lambda e, dst=dst, b=b, bias=bias:
                                     e.activation(dst, banks[b][:, 0:T], ACT.Identity, bias=bias), k)]
                            if name == "kvc":
                                cx["kvc"] = ev
                    free(b, *ev)
                done(i, k)
            F0, F1 = FW[0:4, 0, :], FW[0:4, 1, :]
            k = AC(lambda e: e.activation(F1, F0, ACT.Abs), fa_ready)
            k = AC(lambda e: e.activation(F1, F1, ACT.Exp, scale=-1.0), k)
            k1 = AC(lambda e: e.activation(F1, F1, ACT.Ln, bias=1.0), k)
            k = DVE(lambda e: e.tensor_scalar(F0, F0, -1.0, 0.0, ALU.mult, ALU.max), fa_ready, k1)
            k = DVE(lambda e: e.tensor_tensor(F1, F1, F0, ALU.add), k, k1)
            k2 = DVE(lambda e: e.memset(F0, 1.0), k)
            first = 0.0 if g == 0 else FC[0:4, g * T - 1:g * T]
            cneg = DVE(lambda e: e.tensor_tensor_scan(FC[0:4, g * T:(g + 1) * T], F0, F1, first, ALU.mult, ALU.add),
                       k, k2)
            cx["cneg"] = cneg
            for c0, n, off in TOK1:
                i, w, tw = weights()
                for t in range(GB):
                    b, bw = bank()
                    PE.wait(tw, t_bv, sel_ready, *bw)
                    PE.quiet(mm(banks[b][:, 0:n], ONER[0:1, :], BV[:, off:off + n], True, False))
                    for c in range(7):
                        PE.quiet(mm(banks[b][:, 0:n], HT[:, c, t * P:(t + 1) * P], w[:, c, 0:n], False, False))
                    k = PE(mm(banks[b][:, 0:n], HT[:, 7, t * P:(t + 1) * P], w[:, 7, 0:n], False, True))
                    ev = AC(lambda e, b=b, t=GB * g + t, n=n, off=off: e.copy(
                        VT[:, t, off:off + n], banks[b][:, 0:n]), k)
                    free(b, ev)
                done(i, k)
            cx.update(QF=QF, FW=FW, fa=fa_ready, vt=ev, ht=ht_ready)

        def attend(g, settle):
            QF = cx["QF"]
            TABF = carve(6144)
            Y = carve(GB, D)
            zone = top[0]
            if g == 0:
                top[0] = slots_at
                FBF = carve(D)
                carve(2, T)
                W2 = [carve(2, 64), carve(2, 64)]
            else:
                FBF = XS[0]
                W2 = [XS[1][:, 512 + 128 * j:640 + 128 * j].rearrange("p (a b) -> p a b", a=2) for j in range(2)]
            if g:
                top[0] = jk_at
            CE = carve(2, GB * 3, 32)
            PCT = carve(2, GB, P)
            assert not g or top[0] <= jk_at + D
            if g:
                top[0] = nf_at
            CT = carve(2, GB * 96)
            CM = carve(2, GB * 96)
            assert top[0] <= (nf_at + D if g else slots_at + 7 * D)
            views = [con(n, 768).rearrange("p (a b) -> p a b", a=2)[:, :, g * GB * 96:(g + 1) * GB * 96]
                     for n in ("ctab", "cmask")]
            t_w2 = load_all((W2[0], a["cmp_k_w2"].rearrange("(c p) n -> p c n", p=P)),
                            (W2[1], a["cmp_v_w2"].rearrange("(c p) n -> p c n", p=P)),
                            wait=(xs_free[1],))
            gs_ready = AC(lambda e: e.activation(GS, VT[:, GB * g:GB * g + GB, 896:914], ACT.Sigmoid), cx["vt"])

            y_c0 = []
            compressed_ready = []

            def compressed():
                c0, nc_ = (0, 15) if g == 0 else (15 + 16 * (g - 1), 16)
                ntot = c0 + nc_
                FB = FBF.rearrange("p (a b c) -> p a b c", a=2, b=16)[:, :, :, 0:2 * nc_]
                fb_ready = []
                for kv in range(2):
                    for q in range(2):
                        for par in range(2):
                            for hf in range(2):
                                lo = 16 * (hf + c0)
                                v = KF[q * 64:q * 64 + 64, slot["kvc"] + kv, lo:lo + 16 * nc_]
                                v = v.rearrange("p (c l q) -> p l c q", l=8, q=2)[:, :, :, par]
                                pe = COLS[q * 64:q * 64 + 64, COL["pe"] + 16 * hf:COL["pe"] + 16 * hf + 16]
                                pe = pe.rearrange("p (l q) -> p l q", q=2)[:, :, par].unsqueeze(2)
                                pe = pe.to_broadcast([64, 8, nc_])
                                dst = FB[par * 64:par * 64 + 64, kv, hf * 8:hf * 8 + 8, q * nc_:q * nc_ + nc_]
                                fb_ready.append(DVE(lambda e, dst=dst, v=v, pe=pe: e.tensor_tensor(dst, v, pe, ALU.add),
                                                    cx["vt"] if g else cx["kvc"]))
                hid_ready = []
                for kv in range(2):
                    two = [weights(), weights()]
                    for m in range(2):
                        b, bw = bank()
                        PE.wait(two[0][2], two[1][2], *bw, fb_ready)
                        for c in range(16):
                            op = mm(banks[b][:, 0:2 * nc_], two[c // 8][1][:, c % 8, m * P:m * P + P], FB[:, kv, c, :],
                                    c == 0, c == 15)
                            if c == 15:
                                k = PE(op)
                            else:
                                PE.quiet(op)
                        dst = HID[:, kv, m, :].rearrange("p (q c) -> p q c", q=2)[:, :, c0:ntot]
                        src = banks[b][:, 0:2 * nc_].rearrange("p (q c) -> p q c", q=2)
                        ev = AC(lambda e, src=src, dst=dst: e.activation(dst, src, ACT.Gelu_apprx_tanh), k)
                        free(b, ev)
                        hid_ready.append(ev)
                    done(two[0][0], k)
                    done(two[1][0], k)
                    yield
                kct_ready = []
                for q in range(2):
                    b, bw = bank()
                    lo, hi = q * 31 + c0, q * 31 + ntot
                    PE.quiet(mm(banks[b][0:64, 0:nc_], W2[0][:, 0, :], HID[:, 0, 0, lo:hi], True, False),
                             *bw, hid_ready, t_w2)
                    k = PE(mm(banks[b][0:64, 0:nc_], W2[0][:, 1, :], HID[:, 0, 1, lo:hi], False, True))
                    ev = [DVE(lambda e, b=b, h=h, lo=lo, hi=hi: e.tensor_copy(
                        KCT[h * 64:h * 64 + 64, lo:hi], banks[b][0:64, 0:nc_]), k) for h in range(2)]
                    kct_ready += ev
                    free(b, *ev)
                yield
                vcb_ready = []
                for q in range(2):
                    b, bw = bank()
                    lo, hi = q * 31, q * 31 + ntot
                    PE.quiet(mm(banks[b][0:ntot, 0:64], HID[:, 1, 0, lo:hi], W2[1][:, 0, :], True, False), *bw)
                    k = PE(mm(banks[b][0:ntot, 0:64], HID[:, 1, 1, lo:hi], W2[1][:, 1, :], False, True))
                    ev = []
                    for h in range(3 * q, 3 * q + 3):
                        par, hh = h % 2, h // 2
                        ev.append(DVE(lambda e, b=b, par=par, hh=hh: e.tensor_copy(
                            VCB[hh * 32:hh * 32 + ntot, par, hh * 64:hh * 64 + 64], banks[b][0:ntot, 0:64]), k, vcb0))
                    free(b, *ev)
                    vcb_ready += ev

                compressed_ready.append(k)
                yield
                ce_ready = []
                for par in range(2):
                    b, bw = bank()
                    for i in range(GB):
                        for hh in range(3):
                            q = (2 * hh + par) // 3
                            out = banks[b][:, (i * 3 + hh) * 32:(i * 3 + hh) * 32 + ntot]
                            k = PE(mm(out, QF[par * 64:par * 64 + 64, 5 + hh, i * P:(i + 1) * P],
                                      KCT[par * 64:par * 64 + 64, q * 31:q * 31 + ntot], True, True), *bw, kct_ready)
                    ce, cs = CE[:, par, :, :], CS[:, par, :]
                    ct = CT[:, par, :].rearrange("p (i c) -> p i c", c=32)
                    cm = CM[:, par, :].rearrange("p (i c) -> p i c", c=32)
                    src = banks[b][:, 0:GB * 96].rearrange("p (i c) -> p i c", c=32)
                    z = DVE(lambda e, ce=ce: e.memset(ce, 0.0))
                    k = DVE(lambda e, ce=ce, src=src, ct=ct: e.tensor_tensor(
                        ce[:, :, 0:ntot], src[:, :, 0:ntot], ct[:, :, 0:ntot], ALU.add), k, z, t_ct)
                    free(b, k)
                    k = DVE(lambda e, ce=ce, cs=cs: e.tensor_reduce(cs, ce[:, :, 0:ntot], AX, ALU.max), k)
                    yield
                    k = DVE(lambda e, ce=ce, cs=cs: e.tensor_tensor(
                        ce[:, :, 0:ntot], ce[:, :, 0:ntot], cs.unsqueeze(2).to_broadcast([P, GB * 3, ntot]),
                        ALU.subtract), k)
                    k = AC(lambda e, ce=ce: e.activation(ce[:, :, 0:ntot], ce[:, :, 0:ntot], ACT.Exp), k)
                    yield
                    k = DVE(lambda e, ce=ce, cm=cm: e.tensor_tensor(ce, ce, cm, ALU.mult), k)
                    k = DVE(lambda e, ce=ce, cs=cs: e.tensor_reduce(cs, ce, AX, ALU.add), k)
                    k = DVE(lambda e, cs=cs: e.tensor_scalar(cs, cs, TINY, None, ALU.max), k)
                    yield
                    k = DVE(lambda e, cs=cs: e.reciprocal(cs, cs), k)
                    gate = GS.rearrange("p i (h q b) -> p i h q b", q=2, b=3)[:, :, :, par, 0]
                    yield
                    cs3 = cs.rearrange("p (i h) -> p i h", h=3)
                    k = DVE(lambda e, cs3=cs3, gate=gate: e.tensor_tensor(cs3, cs3, gate, ALU.mult), k, gs_ready)
                    k = DVE(lambda e, ce=ce, cs=cs: e.tensor_tensor(
                        ce, ce, cs.unsqueeze(2).to_broadcast([P, GB * 3, 32]), ALU.mult), k)
                    ce_ready.append(k)
                for par in range(2):
                    b, bw = bank()
                    for i in range(GB):
                        k = PE(lambda e, b=b, i=i, par=par: e.transpose(
                            banks[b][0:96, i * P:(i + 1) * P], CE[:, par, 3 * i:3 * i + 3, :].rearrange("p h c -> p (h c)"),
                            IDENT), *bw, ce_ready[par])
                    pct = AC(lambda e, b=b, par=par: e.copy(PCT[0:96, par, :, :].rearrange("p i n -> p (i n)"),
                                                            banks[b][0:96, 0:T]), k)
                    free(b, pct)
                    for i in range(GB):
                        b, bw = bank()
                        k = PE(mm(banks[b][:, 0:192], PCT[0:96, par, i, :], VCB[0:96, par, :], True, True),
                               *bw, pct, vcb_ready)
                        y = Y[:, i, 640:1024].rearrange("p (h q d) -> p h q d", q=2, d=64)[:, :, par, :]
                        k = DVE(lambda e, b=b, y=y: e.tensor_copy(
                            y, banks[b][:, 0:192].rearrange("p (h d) -> p h d", h=3)), k)
                        free(b, k)
                        y_c0.append(k)
                    yield

            t_ct = load_all((CT, views[0]), (CM, views[1]))
            branch = compressed()
            for _ in range(1 if not g else 4):
                next(branch)
            settle()
            t_tab = load_all((TABF, con("tab", 6144))) if g else cx["tab"]

            cneg = cx["cneg"]
            b, bw = bank()
            for i in range(GB):
                k = PE(lambda e, b=b, i=i: e.transpose(
                    banks[b][:, i * 4:i * 4 + 4], FC[0:4, (g * GB + i) * P:(g * GB + i + 1) * P], IDENT[0:4, 0:4]),
                    *bw, cneg)
            cq_ready = DVE(lambda e, b=b: e.tensor_copy(CQ.rearrange("p i h -> p (i h)"), banks[b][:, 0:4 * GB]), k)
            free(b, cq_ready)
            top[0] = zone
            PB = [carve(512) for _ in range(3)]
            xs_ready = [xs_free[0], xs_free[1], list(compressed_ready)]
            PT = [XS[1][:, 0:512], XS[1][:, 512:1024], carve(512)]
            FT = [XS[0][:, 0:512], XS[0][:, 512:1024]]

            heads = []
            for h in range(4):
                heads.append(("fox", h, (0 + h // 2, h % 2), 0 + h // 2, h * 64, h * 64, 0))
            for h in range(6):
                heads.append(("dil", h, (2 + h // 2, h % 2), 2 + h // 2, 256 + h * 64, 256 + h * 64, 1 + h))
            for h in range(6):
                heads.append(("sel", h, (5 + h // 2, h % 2), 5 + h // 3, 640 + (h // 3) * 64, 640 + h * 64, 7 + h))
            for h in range(6):
                heads.append(("win", h, (5 + h // 2, h % 2), 7 + h // 3, 768 + (h // 3) * 64, 640 + h * 64, 7 + h))
            units = [(n, hd, i) for n, hd in enumerate(heads) for i in range(GB)]
            st = {}
            pb_free = [[], [], []]
            pt_free = [xs_ready, xs_ready, []]
            ft_free = [[xs_ready, cx["vt"]], [xs_ready, cx["vt"]]]
            fox = {"n": 0}
            y_done = {}

            def scores(u):
                n, (kind, h, (qs, par), ks, _, _, tab), il = units[u]
                i = GB * g + il
                j0 = max(0, i - 1) if kind == "dil" and h < 2 else 0
                w = (i + 1 - j0) * P
                b, bw = bank()
                spent[0] += UNIT
                q = QF[par * 64:par * 64 + 64, qs, il * P:(il + 1) * P]
                kk = KF[par * 64:par * 64 + 64, ks, j0 * P:(i + 1) * P]
                k = PE(mm(banks[b][:, 0:w], q, kk, True, True), *bw)
                end = TAB_AT[tab] + TAB_W[tab]
                t = TABF[:, end - w:end]
                ready = None
                if kind == "fox":
                    if il == 0:
                        held.add(b)
                        cb, cw = bank()
                        held.discard(b)
                        held.add(cb)
                        fox["bank"] = cb, PE(mm(banks[cb][:, 0:(g + 1) * T], SEL[0:4, h, :],
                                                FC[0:4, 0:(g + 1) * T], True, True), *cw, sel_ready)
                    cb, kc = fox["bank"]
                    f = fox["n"] % 2
                    fox["n"] += 1
                    dst = FT[f][:, 0:w]
                    ready = DVE(lambda e: e.tensor_scalar(dst, banks[cb][:, 0:w], CQ[:, il, h:h + 1], None,
                                                          ALU.subtract), kc, cq_ready, ft_free[f], t_tab)
                    if il == GB - 1:
                        held.discard(cb)
                        free(cb, ready)
                    ready = DVE(lambda e, t=t: e.tensor_tensor(dst, dst, t, ALU.add), ready)
                    t = dst
                s = PB[u % 3][:, 0:w]
                k = DVE(lambda e: e.tensor_tensor_reduce(
                    out=s, in0=banks[b][:, 0:w], in1=t, scale=-1.0, scalar=3.0e38, op0=ALU.add, op1=ALU.min,
                    accum_out=NM[:, n, il:il + 1]), k, ready, pb_free[u % 3], t_tab)
                free(b, k)
                if kind == "fox":
                    ft_free[f] = [k]
                k = AC(lambda e: e.activation(s, s, ACT.Exp, bias=NM[:, n, il:il + 1], scale=-1.0,
                                              accum_out=LS[:, n, il:il + 1]), k)
                st[u] = (j0, w, k)

            def turn(u):
                j0, w, k = st[u]
                b, bw = bank()
                PE.wait(k, *bw)
                for j in range(w // P):
                    k2 = PE(lambda e, j=j: e.transpose(banks[b][:, j * P:(j + 1) * P], PB[u % 3][:, j * P:(j + 1) * P],
                                                       IDENT))
                pb_free[u % 3] = [k2]
                k3 = AC(lambda e: e.copy(PT[u % 3][:, 0:w], banks[b][:, 0:w]), k2, pt_free[u % 3])
                free(b, k3)
                st[u] = (j0, w, k3)

            def values(u):
                n, (kind, h, _, _, vc, yc, _), il = units[u]
                j0, w, k = st.pop(u)
                rl = RL[:, n, il:il + 1]
                r = DVE(lambda e: e.reciprocal(rl, LS[:, n, il:il + 1]), k)
                if kind in ("sel", "win"):
                    gt = GS[:, il, h * 3 + (1 if kind == "sel" else 2):h * 3 + (2 if kind == "sel" else 3)]
                    r = DVE(lambda e: e.tensor_tensor(rl, rl, gt, ALU.mult), r, gs_ready)
                b, bw = bank()
                nb = w // P
                PE.wait(k, *bw)
                for j in range(nb):
                    op = mm(banks[b][:, 0:64], PT[u % 3][:, j * P:(j + 1) * P], VT[:, j0 + j, vc:vc + 64],
                            j == 0, j == nb - 1)
                    if j == nb - 1:
                        k2 = PE(op)
                    else:
                        PE.quiet(op)
                pt_free[u % 3] = [k2]
                y = Y[:, il, yc:yc + 64]
                if kind in ("sel", "win"):
                    k3 = DVE(lambda e: e.scalar_tensor_tensor(y, banks[b][:, 0:64], rl, y, ALU.mult, ALU.add),
                             k2, r, y_c0, y_done.get((il, yc)))
                else:
                    k3 = AC(lambda e: e.activation(y, banks[b][:, 0:64], ACT.Copy, scale=rl), k2, r)
                free(b, k3)
                y_done[il, yc] = k3

            first_sel = 10 * GB
            for u in range(len(units) + 3):
                next(branch, None)
                if u == first_sel:
                    for _ in branch:
                        pass
                if u < len(units):
                    scores(u)
                if 2 <= u and u - 2 < len(units):
                    turn(u - 2)
                if 3 <= u:
                    values(u - 3)

            if g == 1:
                nf_in.append(load_all((NF, row("norm_f", D)), wait=(y_c0,)))

            k = AC(lambda e: e.activation(AL[:, 0, :, :], LS[:, 4:10, :].rearrange("p h i -> p i h"), ACT.Ln),
                   DVE.last)
            k = DVE(lambda e: e.tensor_tensor(AL[:, 0, :, :], AL[:, 0, :, :],
                                              NM[:, 4:10, :].rearrange("p h i -> p i h"), ALU.subtract), k)
            lse = AL[:, 0, :, :].rearrange("p i (g q) -> p i q g", q=2)
            mx = AL[:, 1, :, 0:2]
            k = DVE(lambda e: e.tensor_reduce(mx, lse, AX, ALU.max), k)
            w3 = AL[:, 2, :, :].rearrange("p i (g q) -> p i q g", q=2)
            k = DVE(lambda e: e.tensor_tensor(w3, lse, mx.unsqueeze(3).to_broadcast([P, GB, 2, 3]), ALU.subtract), k)
            k = AC(lambda e: e.activation(AL[:, 2, :, :], AL[:, 2, :, :], ACT.Exp), k)
            k = DVE(lambda e: e.tensor_reduce(mx, w3, AX, ALU.add), k)
            k = DVE(lambda e: e.reciprocal(mx, mx), k)
            k = DVE(lambda e: e.tensor_tensor(w3, w3, mx.unsqueeze(3).to_broadcast([P, GB, 2, 3]), ALU.mult), k)
            for i in range(GB):
                y = Y[:, i, 256:640].rearrange("p (h d) -> p h d", h=6)
                al = AL[:, 2, i, :].unsqueeze(2).to_broadcast([P, 6, 64])
                DVE(lambda e, y=y, al=al: e.tensor_tensor(y, y, al, ALU.mult), k, DVE.last, AC.last)
            barrier()
            cx.update(Y=Y, YT=TABF[:, 0:8 * T].rearrange("p (c n) -> p c n", c=8),
                      MG=TABF[:, 8 * T:16 * T].rearrange("p (c n) -> p c n", c=8),
                      GT=[PB[j][:, 0:T] for j in range(3)])

        def merge():
            Y, YT, MG, GT = cx["Y"], cx["YT"], cx["MG"], cx["GT"]
            yt_ready = []
            for t in range(GB):
                for half in range(2):
                    b, bw = bank()
                    PE.wait(*bw)
                    for c in range(4):
                        src = Y[:, t, (half * 4 + c) * P:(half * 4 + c + 1) * P]
                        k = PE(lambda e, b=b, c=c, src=src: e.transpose(banks[b][:, c * P:(c + 1) * P], src, IDENT))
                    dst = YT[:, half * 4:half * 4 + 4, t * P:(t + 1) * P]
                    src = banks[b][:, :].rearrange("p (c n) -> p c n", c=4)
                    ev = AC(lambda e, dst=dst, src=src: e.copy(dst, src), k)
                    free(b, ev)
                    yt_ready.append(ev)
            gt_free = [[], [], []]
            mg_ready = []
            for m4 in range(4):
                wp = weights()
                km = [None, None]
                for j, (c0, cn) in enumerate(((0, 2), (2, 3), (5, 3))):
                    wg = weights()
                    for j2 in range(2):
                        m = m4 * 2 + j2
                        f = (j * 2 + j2) % 3
                        gj = GT[f]
                        bg, kg = proj_feat(wg[1], j2, P, None, wg[2])
                        kg = AC(lambda e, bg=bg, gj=gj, m=m, j=j: e.activation(
                            gj, banks[bg][:, 0:T], ACT.Sigmoid, bias=col("b_gate", j * 8 + m)), kg, gt_free[f])
                        free(bg, kg)
                        b, bw = bank()
                        PE.wait(wp[2], *bw, yt_ready)
                        for c in range(cn):
                            k = PE(mm(banks[b][:, 0:T], wp[1][:, c0 + c, j2 * P:(j2 + 1) * P], YT[:, c0 + c, :],
                                      c == 0, c == cn - 1))
                        if j == 0:
                            k = DVE(lambda e, b=b, gj=gj, m=m: e.tensor_tensor(
                                MG[:, m, :], banks[b][:, 0:T], gj, ALU.mult), k, kg)
                            km[j2] = k
                        else:
                            k = DVE(lambda e, b=b, gj=gj: e.tensor_tensor(gj, banks[b][:, 0:T], gj, ALU.mult), k, kg)
                            km[j2] = DVE(lambda e, gj=gj, m=m: e.tensor_tensor(MG[:, m, :], MG[:, m, :], gj,
                                                                               ALU.add), k, km[j2])
                        free(b, k)
                        gt_free[f] = [km[j2]]
                    done(wg[0], PE.last)
                done(wp[0], PE.last)
                mg_ready += km
            return add_rows(MG, mg_ready)

        def mlp(x_ready):
            ht_ready = norm_to_ht("g2", x_ready)
            barrier()
            top[0] = base
            UT = carve(NFF, T)
            AB = [carve(T) for _ in range(3)]
            A2 = [carve(T + 2) for _ in range(3)]
            FG = carve(D)
            t_fg = load_all((FG, row("final_g", D)))
            ab_free = [[], [], []]
            for jb in range(11):
                wa, wb = weights(), weights()
                for j2 in range(2):
                    m = jb * 2 + j2
                    ba, ka = proj_feat(wa[1], j2, P, ht_ready, wa[2])
                    bb, kb = proj_feat(wb[1], j2, P, None, wb[2])
                    y, a2, pa = AB[m % 3], A2[m % 3], banks[ba]
                    k0 = AC(lambda e, a2=a2, m=m: e.copy(a2[:, 0:2], AH[:, m, :]), ab_free[m % 3])
                    k1 = AC(lambda e, a2=a2, pa=pa: e.copy(a2[:, 2:T + 2], pa[:, 0:T]), ka)
                    k = AC(lambda e, y=y, pa=pa, m=m: e.activation(y, pa[:, 0:T], ACT.Identity, bias=col("cb", m),
                                                                  scale=col("cw", 44 + m)), k1)
                    free(ba, k)
                    AC(lambda e, a2=a2, m=m: e.copy(AH[:, m, :], a2[:, T:T + 2]), k0, k1)
                    k = DVE(lambda e, y=y, a2=a2, m=m: e.scalar_tensor_tensor(
                        y, a2[:, 1:T + 1], col("cw", 22 + m), y, ALU.mult, ALU.add), k)
                    k = DVE(lambda e, y=y, a2=a2, m=m: e.scalar_tensor_tensor(
                        y, a2[:, 0:T], col("cw", m), y, ALU.mult, ALU.add), k)
                    k = AC(lambda e, y=y: e.activation(y, y, ACT.Gelu_apprx_tanh), k)
                    k = DVE(lambda e, y=y, bb=bb, m=m: e.tensor_tensor(UT[:, m, :], y, banks[bb][:, 0:T], ALU.mult),
                            k, kb)
                    free(bb, k)
                    ab_free[m % 3] = [k, AC.last]
                done(wa[0], kb)
                done(wb[0], kb)
            ut_ready = k
            kx = [None] * GB
            for half in range(2):
                bs = [bank() for _ in range(GB)]
                held.update(b for b, _ in bs)
                for k0, kn in DOWN:
                    i, w, tw = weights()
                    for c in range(kn):
                        for t in range(GB):
                            PE.wait(tw, *bs[t][1], ut_ready)
                            k = PE(mm(banks[bs[t][0]][:, :], UT[:, k0 + c, t * P:(t + 1) * P], w[:, c, :],
                                      k0 + c == 0, k0 + c == NFF - 1))
                    done(i, k)
                    tick()
                for t in range(GB):
                    x = X[:, t, half * 512:half * 512 + 512]
                    kx[t] = DVE(lambda e, x=x, b=bs[t][0]: e.tensor_tensor(x, x, banks[b][:, :], ALU.add), k)
                    free(bs[t][0], kx[t])
                held.clear()
            out = []
            for t in range(GB):
                k = rms(t, kx[t])
                out.append(DVE(lambda e, t=t: e.scalar_tensor_tensor(X[:, t, :], X[:, t, :], SS[:, t + 8:t + 9], FG,
                                                                     ALU.mult, ALU.mult), k, t_fg))
            return out

        def mixer(g, x_ready):
            NC = T // 32
            ht_ready = norm_to_ht("gm2", x_ready)
            barrier()
            top[0] = base
            MIX = carve(8, T)
            HM, SM, BLK, ONE = carve(P), carve(T), carve(P), carve(P)
            t_c2 = load_all((HM, con("hmask", P)), (SM, con("smask", T)), (BLK, con("blk", P)), (ONE, con("all", P)))
            LB = carve(6, 4)
            DEC = carve(4, NC)
            QD, KD, SG = carve(4, T), carve(4, T), carve(4, T)
            zone = top[0]
            FH, EG, KE = carve(4, T), carve(4, T), carve(4, T)
            top[0] = zone
            ST = carve(NC, 512)
            TW = None
            if g == 0:
                ST = arena[:, slots_at:slots_at + NC * 512].rearrange("p (a b) -> p a b", a=NC)
                TW = [arena[:, slots_at + NC * 512 + j * T:slots_at + NC * 512 + j * T + T] for j in range(4)]
            V2 = carve(GB, 512)
            KET = carve(GB, 4, P)
            ATB = carve(GB, P)
            tmp = arena[:, xs_at:xs_at + 2048]
            TM = [tmp[:, j * T:(j + 1) * T] for j in range(5)]
            U2 = tmp[:, 5 * T:6 * T + 2]
            l0, l1 = col("lb", 0, 4), col("lb", 4, 4)
            k = DVE(lambda e: e.tensor_tensor(LB[:, 0, :], l0, l1, ALU.max))
            k1 = DVE(lambda e: e.tensor_tensor(LB[:, 1, :], l0, LB[:, 0, :], ALU.subtract), k)
            k1 = DVE(lambda e: e.tensor_tensor(LB[:, 2, :], l1, LB[:, 0, :], ALU.subtract), k, k1)
            k = AC(lambda e: e.activation(LB[:, 3:5, :], LB[:, 1:3, :], ACT.Exp), k1)
            k = DVE(lambda e: e.tensor_tensor(LB[:, 4, :], LB[:, 3, :], LB[:, 4, :], ALU.add), k)
            k = DVE(lambda e: e.reciprocal(LB[:, 4, :], LB[:, 4, :]), k)
            k = DVE(lambda e: e.tensor_tensor(LB[:, 0, :], LB[:, 3, :], LB[:, 4, :], ALU.mult), k)
            lb_ready = DVE(lambda e: e.tensor_scalar(LB[:, 5, :], LB[:, 0, :], -1.0, 1.0, ALU.mult, ALU.add), k)

            convs = {}

            def conv(m):
                j4, j2 = m // 2, m % 2
                if j2 == 0:
                    convs["w"] = weights(), weights(), weights()
                wc, wh, wb = convs["w"]
                spent[0] += CONV
                bc, kc = proj_feat(wc[1], j2, P, None, wc[2])
                bh, kh = proj_feat(wh[1], j2, P, None, wh[2])
                bb, kb = proj_feat(wb[1], j2, P, None, wb[2])
                y = TM[1]
                free_tm = convs.get("free")
                k = AC(lambda e: e.copy(TM[2], banks[bc][:, 0:T]), kc, free_tm)
                free(bc, k)
                k0 = DVE(lambda e: e.tensor_copy(U2[:, 0:2], UH[:, m, :]), free_tm)
                k = DVE(lambda e: e.tensor_tensor(U2[:, 2:T + 2], TM[2], banks[bh][:, 0:T], ALU.mult), k, kh, k0)
                free(bh, k)
                k2 = DVE(lambda e: e.tensor_copy(UH[:, m, :], U2[:, T:T + 2]), k, k0)
                k = DVE(lambda e: e.tensor_scalar(y, U2[:, 2:T + 2], col("cw2", 8 + m), None, ALU.mult), k2)
                k = DVE(lambda e: e.scalar_tensor_tensor(y, U2[:, 1:T + 1], col("cw2", 4 + m), y, ALU.mult,
                                                         ALU.add), k)
                k = DVE(lambda e: e.scalar_tensor_tensor(y, U2[:, 0:T], col("cw2", m), y, ALU.mult, ALU.add), k)
                ky = DVE(lambda e: e.tensor_tensor(y, y, banks[bb][:, 0:T], ALU.mult), k, kb)
                free(bb, ky)
                k3 = AC(lambda e: e.activation(TM[3], y, ACT.Square), ky)

                def finish():
                    b, bw = bank()
                    k = PE(mm(banks[b][:, 0:T], BLK, TM[3], True, True), *bw, k3, t_c2)
                    k = AC(lambda e: e.activation(TM[4], banks[b][:, 0:T], ACT.Sqrt, bias=EPS), k)
                    free(b, k)
                    k = DVE(lambda e: e.reciprocal(TM[4], TM[4]), k)
                    convs["free"] = DVE(lambda e: e.scalar_tensor_tensor(
                        MIX[:, m, :], y, col("cg2", m), TM[4], ALU.mult, ALU.mult), k)

                if j2:
                    for i, _, _ in convs["w"]:
                        done(i, kb)
                return finish

            for dst, fn in ((FH, ACT.Sigmoid), (QD, ACT.Silu), (SG, ACT.Silu)):
                for j4 in range(2):
                    i, w, tw = weights()
                    for j2 in range(2):
                        b, k = proj_feat(w, j2, P, ht_ready, tw)
                        d = dst[:, j4 * 2 + j2, :]
                        ev = AC(lambda e, d=d, b=b, fn=fn: e.activation(d, banks[b][:, 0:T], fn), k)
                        free(b, ev)
                    done(i, k)
                if dst is FH:
                    f_ready = ev
            for j4 in range(2):
                i, w, tw = weights()
                for t in range(GB):
                    b, bw = bank()
                    PE.wait(tw, *bw)
                    for c in range(8):
                        k = PE(mm(banks[b][:, 0:256], HT[:, c, t * P:(t + 1) * P], w[:, c, :], c == 0, c == 7))
                    ev = AC(lambda e, b=b, t=t, j4=j4: e.copy(V2[:, t, j4 * 256:j4 * 256 + 256],
                                                              banks[b][:, 0:256]), k)
                    free(b, ev)
                done(i, k)
            v2_ready = ev
            for h in range(4):
                kf = DVE(lambda e, h=h: e.tensor_scalar(FH[:, h, :], FH[:, h, :], LB[:, 5, h:h + 1],
                                                        LB[:, 0, h:h + 1], ALU.mult, ALU.add), f_ready, lb_ready)
            kl = AC(lambda e: e.activation(EG, FH, ACT.Ln), kf)
            k1h = DVE(lambda e: e.tensor_scalar(FH, FH, -1.0, 1.0, ALU.mult, ALU.add), kl)
            hg_ready = {}
            ket_ready = {}
            st_ready = {}
            part = {}
            zero = DVE(lambda e: e.memset(ATB, 0.0))
            hm = HM.bitcast(U32)

            def gates(h):
                G = KD[:, h, :]
                k = DVE(lambda e: e.tensor_tensor_scan(G, SM, EG[:, h, :], 0.0, ALU.mult, ALU.add), kl, t_c2)
                G3 = G.rearrange("p (n c) -> p n c", c=32)
                k2 = DVE(lambda e: e.tensor_tensor(
                    KE[:, h, :].rearrange("p (n c) -> p n c", c=32), G3[:, :, 31:32].to_broadcast([P, NC, 32]), G3,
                    ALU.subtract), k)
                ke = AC(lambda e: e.activation(KE[:, h, :], KE[:, h, :], ACT.Exp), k2)
                kg = AC(lambda e: e.activation(EG[:, h, :], G, ACT.Exp), k)
                kn = AC(lambda e: e.activation(G, G, ACT.Exp, scale=-1.0), k2, kg)
                k3 = DVE(lambda e: e.tensor_tensor(KE[:, h, :], KE[:, h, :], FH[:, h, :], ALU.mult), ke, k1h)
                k4 = DVE(lambda e: e.tensor_tensor(G, G, FH[:, h, :], ALU.mult), kn)
                k5 = DVE(lambda e: e.scalar_tensor_tensor(QD[:, h, :], QD[:, h, :], 128.0 ** -0.5, EG[:, h, :],
                                                          ALU.mult, ALU.mult), kg)
                k6 = DVE(lambda e: e.tensor_copy(
                    DEC[:, h, :], EG[:, h, :].rearrange("p (n c) -> p n c", c=32)[:, :, 31]), kg)
                hg_ready[h] = [k3, k4, k5, k6]

            def turn_keys(h):
                b, bw = bank()
                PE.wait(*bw, hg_ready[h])
                for t in range(GB):
                    k = PE(lambda e, t=t: e.transpose(banks[b][:, t * P:(t + 1) * P], KE[:, h, t * P:(t + 1) * P],
                                                      IDENT))
                ket_ready[h] = AC(lambda e: e.copy(KET[:, :, h, :], banks[b][:, 0:T].rearrange(
                    "p (t n) -> p t n", t=GB)), k)
                free(b, ket_ready[h])

            def states(h):
                hs = slice(h * P, (h + 1) * P)
                tok, got = None, []
                for j in range(4):
                    spent[0] += STATE
                    b, bw = bank()
                    PE.wait(*bw, list(ket_ready.values()), v2_ready)
                    for t in range(GB):
                        k = PE(mm(banks[b][:, t * P:(t + 1) * P], KET[j * 32:j * 32 + 32, t, h, :],
                                  V2[j * 32:j * 32 + 32, t, hs], True, True))
                    got.append((b, k))
                for n in range(NC):
                    t, (b, k) = n // 4, got[n % 4]
                    ps = ST[:, n - 1, hs] if n else STP[:, hs]
                    tok = DVE(lambda e, t=t, n=n, ps=ps, b=b: e.scalar_tensor_tensor(
                        ST[:, n, hs], ps, DEC[:, h, n:n + 1], banks[b][:, t * P:(t + 1) * P], ALU.mult,
                        ALU.add), k, tok, list(ket_ready.values()))
                    free(b, tok)
                st_ready[h] = tok

            def within(h):
                ba, baw = bank()
                PE.wait(*baw, hg_ready[h])
                for t in range(GB):
                    k = PE(mm(banks[ba][:, t * P:(t + 1) * P], KD[:, h, t * P:(t + 1) * P],
                              QD[:, h, t * P:(t + 1) * P], True, True))
                for t in range(GB):
                    ka = DVE(lambda e, t=t: e.copy_predicated(ATB[:, t, :], hm, banks[ba][:, t * P:(t + 1) * P]),
                             k, zero)
                free(ba, ka)
                part["a", h] = ka

            def outputs(h):
                spent[0] += STATE
                bo, bow = bank()
                for t in range(GB):
                    PE(mm(banks[bo][:, t * P:(t + 1) * P], V2[:, t, h * P:(h + 1) * P], ATB[:, t, :], True, False),
                       part["a", h], *bow)
                    for j in range(4):
                        n = t * 4 + j
                        state = ST[:, n - 1, :] if n else STP
                        k = PE(mm(banks[bo][:, n * 32:n * 32 + 32], state[:, h * P:(h + 1) * P],
                                  QD[:, h, n * 32:n * 32 + 32], False, j == 3), st_ready[h])
                held.add(bo)
                sq = TW[2 * (h % 2)]
                kq = AC(lambda e: e.activation(sq, banks[bo][:, 0:T], ACT.Square), k, part.get(h - 2), tm_free)
                part["o", h] = bo, kq

            def normed(h):
                bo, kq = part["o", h]
                sq, y = TW[2 * (h % 2)], TW[2 * (h % 2) + 1]
                b, bw = bank()
                k = PE(mm(banks[b][:, 0:T], ONE, sq, True, True), *bw, kq)
                k = AC(lambda e: e.activation(y, banks[b][:, 0:T], ACT.Sqrt, bias=EPS), k, part.get(h - 2), tm_free)
                free(b, k)
                k = DVE(lambda e: e.reciprocal(y, y), k)
                k = DVE(lambda e: e.tensor_tensor(y, banks[bo][:, 0:T], y, ALU.mult), k)
                free(bo, k)
                held.discard(bo)
                part[h] = DVE(lambda e: e.scalar_tensor_tensor(MIX[:, 4 + h, :], y, col("hg"), SG[:, h, :],
                                                               ALU.mult, ALU.mult), k)

            if g == 0:
                tm_free = None
                for h in range(6):
                    if 1 <= h <= 4:
                        turn_keys(h - 1)
                    if h < 4:
                        finish = conv(h)
                    if h >= 2:
                        outputs(h - 2)
                    if 1 <= h <= 4:
                        states(h - 1)
                        within(h - 1)
                    if h < 4:
                        gates(h)
                        finish()
                    if h >= 2:
                        normed(h - 2)
                part[3] = [part[3], convs["free"]]
            else:
                for h in range(4):
                    finish = conv(h)
                    gates(h)
                    finish()
                tm_free = convs["free"]
                TW = TM
                for h in range(4):
                    turn_keys(h)
                for h in range(4):
                    states(h)
                for h in range(5):
                    if h < 4:
                        within(h)
                        outputs(h)
                    if h:
                        normed(h - 1)
            tm_free = part[3]
            AC(lambda e: e.copy(STP, ST[:, NC - 1, :]), PE.last, DVE.last)
            xs_free[0] = xs_free[1] = [tm_free]
            return add_rows(MIX, tm_free)

        out_sem = [[newsem(f"s_out{j}"), 0] for j in range(NT)]
        ov = a["out"].rearrange("(t p) d -> t p d", p=P)
        h2_ready = {}
        gat = {}
        issued = {}

        def queries(g, x_ready, start):
            barrier()
            top[0] = base + 8 * T
            ex = {"KEYS": carve(16, P), "QT": carve(16, T), "CAND": carve(8, 256),
                  "SR": [carve(P) for _ in range(2)], "T16": carve(8, 2, 16), "I16": carve(8, 2, 16).bitcast(U32),
                  "IF": carve(8, 2, 16), "CSC": carve(8, 16), "CIX": carve(8, 16).bitcast(U32),
                  "HL": carve(2, 8, 16), "HLI": carve(2, 8, 16).bitcast(U32), "EX": carve(2, 8, 16), "GM": carve(8)}
            gain = ex["CAND"].rearrange("p a b -> p (a b)")[:, 0:D]
            t_k = load_all((gain, row("norm_ffn", D)))
            t_keys = load_all((ex["KEYS"], a["keys"].rearrange("p (j n) -> p j n", j=16)))

            def keep(t, k):
                h2_ready[GB * g + t] = DVE(lambda e: e.tensor_tensor(H2[:, t, :], XS[t % 2], gain, ALU.mult), k, t_k,
                                           DVE.last)
                return h2_ready[GB * g + t]

            ht_ready = norm_to_ht("gf2", x_ready, keep)
            if g == 0:
                for t in range(GB):
                    DVE(lambda e, t=t: e.tensor_copy(ACC[t], X[:, t, :]), x_ready[t])
                ex["x"] = load_x(g + 1, DVE.last, AC.last)
            for c8 in range(8):
                i, w, tw = weights()
                for j2 in range(2):
                    b, k = proj_feat(w, j2, P, ht_ready, tw)
                    m = c8 * 2 + j2
                    ev = AC(lambda e, b=b, m=m: e.copy(ex["QT"][:, m, :], banks[b][:, 0:T]), k)
                    free(b, ev)
                done(i, k)
                ex["ready"] = [ev, t_keys]
                if c8 == 0:
                    ex["experts"] = start(ex)
                if c8 % 2:
                    for _ in range(2):
                        next(ex["experts"])
            return ex

        def top_sixteen(jobs, *ready):
            ready = ready + (DVE.last,)
            k1, k2, k3, k4, k5 = {}, {}, {}, {}, {}
            for n, (v, ix, s, rest) in enumerate(jobs):
                k1[n] = DVE(lambda e, v=v, s=s: e.max(v[:, 0:8], s), *ready)
            for n, (v, ix, s, rest) in enumerate(jobs):
                k2[n] = DVE(lambda e, v=v, ix=ix, s=s: e.max_index(ix[:, 0:8], v[:, 0:8], s), k1[n])
            for n, (v, ix, s, rest) in enumerate(jobs):
                k3[n] = DVE(lambda e, v=v, rest=rest, s=s: e.match_replace(rest, v[:, 0:8], s, -3.0e38), k2[n])
            for n, (v, ix, s, rest) in enumerate(jobs):
                k4[n] = DVE(lambda e, v=v, rest=rest: e.max(v[:, 8:16], rest), k3[n])
            for n, (v, ix, s, rest) in enumerate(jobs):
                k5[n] = DVE(lambda e, v=v, ix=ix, rest=rest: e.max_index(ix[:, 8:16], v[:, 8:16], rest), k4[n])
            return k3[len(jobs) - 1], k5[len(jobs) - 1]

        def choose(t, ex):
            par, tl = t % 2, t % GB
            T16, I16, IF, CAND, CSC, CIX = (ex[n] for n in ("T16", "I16", "IF", "CAND", "CSC", "CIX"))
            HL, HLI, EX, GM, SR = (ex[n] for n in ("HL", "HLI", "EX", "GM", "SR"))
            for b4 in range(4):
                b, bw = side_bank()
                PE.wait(*bw, ex["ready"])
                for c in range(4):
                    m = b4 * 4 + c
                    k = PE(mm(banks[b][:, c * P:(c + 1) * P], ex["QT"][:, m, tl * P:(tl + 1) * P],
                              ex["KEYS"][:, m, :], True, True))
                for c in range(0, 4, 2):
                    h = (b4 * 4 + c) // 2
                    jobs = [(T16[:, h, half, :], I16[:, h, half, :], banks[b][:, (c + half) * P:(c + half + 1) * P],
                             SR[half]) for half in range(2)]
                    k2, k4 = top_sixteen(jobs, k)
                    if c == 2:
                        free(b, k2)
                    yield 2.8
            kf = DVE(lambda e: e.tensor_copy(IF, I16), k4, DVE.last)
            cand = CAND.rearrange("p h (a b) -> p h a b", a=16)
            for h2 in range(0, 8, 2):
                jobs = []
                for h in (h2, h2 + 1):
                    s1 = T16[:, h, 0, :].unsqueeze(2).to_broadcast([P, 16, 16])
                    s2 = T16[:, h, 1, :].unsqueeze(1).to_broadcast([P, 16, 16])
                    k = DVE(lambda e, h=h, s1=s1, s2=s2: e.tensor_tensor(cand[:, h, :, :], s1, s2, ALU.add), k4,
                            DVE.last)
                    jobs.append((CSC[:, h, :], CIX[:, h, :], CAND[:, h, :], CAND[:, h, :]))
                _, k = top_sixteen(jobs, k)
                yield 2.0
            k1 = DVE(lambda e: e.tensor_scalar(HLI[:, 0, :, :], CIX, 4, None, ALU.logical_shift_right), k)
            k2 = DVE(lambda e: e.tensor_scalar(HLI[:, 1, :, :], CIX, 15, None, ALU.bitwise_and), k)
            k = DVE(lambda e: e.tensor_copy(HL, HLI), k1, k2)
            OH = CAND.rearrange("p h (j a) -> p h j a", j=16)
            for half in range(2):
                hl = HL[:, half, :, :].rearrange("p h j -> p (h j)").unsqueeze(2).to_broadcast([P, 128, 16])
                io = IOTA.unsqueeze(1).to_broadcast([P, 128, 16])
                oh = OH.rearrange("p h j a -> p (h j) a")
                k = DVE(lambda e, oh=oh, hl=hl, io=io: e.tensor_tensor(oh, hl, io, ALU.is_equal), k, DVE.last)
                yield 1.0
                ib = IF[:, :, half, :].unsqueeze(2).to_broadcast([P, 8, 16, 16])
                k = DVE(lambda e, ib=ib: e.tensor_tensor(OH, OH, ib, ALU.mult), k, kf)
                yield 1.0
                k = DVE(lambda e, half=half: e.tensor_reduce(EX[:, half, :, :], OH, AX, ALU.add), k)
                yield 1.0
            k = DVE(lambda e: e.scalar_tensor_tensor(EX[:, 0, :, :], EX[:, 0, :, :], 128.0, EX[:, 1, :, :],
                                                     ALU.mult, ALU.add), k)
            ei = DVE(lambda e: e.tensor_copy(EI[par].rearrange("p (h j) -> p h j", h=8), EX[:, 0, :, :]), k,
                     issued.get(t - 2))
            gw = GW[par].rearrange("p (h j) -> p h j", h=8)
            k = DVE(lambda e: e.tensor_tensor(gw, CSC, CSC[:, :, 0:1].to_broadcast([P, 8, 16]), ALU.subtract), k)
            k = AC(lambda e: e.activation(gw, gw, ACT.Exp), k)
            k = DVE(lambda e: e.tensor_reduce(GM, gw, AX, ALU.add), k)
            k = DVE(lambda e: e.reciprocal(GM, GM), k)
            k = DVE(lambda e: e.tensor_tensor(gw, gw, GM.unsqueeze(2).to_broadcast([P, 8, 16]), ALU.mult), k)
            gat[t] = (ei, k)

        slot_sem = [[newsem(f"s_g{i}"), 0] for i in range(16)]
        slot_free = [None] * 16

        def experts(g, ex, slots):
            yield from choose(GB * g, ex)
            jobs = [(GB * g + t, which, k) for t in range(GB) for which in range(2) for k in range(P)]
            where = {}
            ns = len(slots)

            def gather(n):
                t, which, k = jobs[n]
                s = n % ns
                tab = a["peer_u_2"] if which == 0 else a["peer_v_2"]
                off = EI[t % 2][:, k:k + 1]
                where[n] = GP.dma(lambda e: e.indirect_dma_start(
                    out=slots[s], out_offset=None, in_=tab, in_offset=bass.IndirectOffsetOnAxis(ap=off, axis=0)),
                    slot_sem[s], gat[t][0], slot_free[s])
                if (which, k) == (1, P - 1):
                    issued[t] = where[n]

            for n in range(ns):
                gather(n)
            later = choose(GB * g + 1, ex)
            chain = None
            for n, (t, which, k) in enumerate(jobs):
                tl, s = t % GB, n % ns
                if g and (which, k) == (0, 0):
                    chain = DVE(lambda e, tl=tl: e.tensor_copy(ACC[tl], X[:, tl, :]), (out_sem[t - GB][0], 16))
                if n == len(jobs) - P:
                    stage["last values"] = g
                if which == 0:
                    tok = DVE(lambda e, s=s, t=t, tl=tl, k=k: e.tensor_tensor_reduce(
                        out=slots[s], in0=slots[s], in1=H2[:, tl, :], scale=1.0, scalar=0.0, op0=ALU.mult,
                        op1=ALU.add, accum_out=AA[t % 2][:, k:k + 1]), where[n], h2_ready[t], DVE.last)
                    if k == P - 1:
                        kk = AC(lambda e, t=t: e.activation(AA[t % 2], AA[t % 2], ACT.Gelu), tok)
                        w_ready = DVE(lambda e, t=t: e.tensor_tensor(AA[t % 2], AA[t % 2], GW[t % 2], ALU.mult),
                                      kk, gat[t][1])
                else:
                    tok = DVE(lambda e, s=s, t=t, tl=tl, k=k: e.scalar_tensor_tensor(
                        ACC[tl], slots[s], AA[t % 2][:, k:k + 1], ACC[tl], ALU.mult, ALU.add),
                        where[n], w_ready, chain)
                    chain = tok
                slot_free[s] = tok
                if n + ns < len(jobs):
                    if jobs[n + ns][0] not in gat:
                        for _ in later:
                            pass
                    gather(n + ns)
                if g == 0 or n % 12 == 0:
                    next(later, None)
                yield STEP
                if which == 1 and k == P - 1:
                    acc = ACC[tl]
                    kk = AC(lambda e, acc=acc: e.activation(JK, acc, ACT.Square, accum_out=SS[:, 12:13]), tok,
                            AC.last)
                    kk = AC(lambda e: e.activation(SS[:, 13:14], SS[:, 12:13], ACT.Sqrt, bias=EPS, scale=1.0 / D), kk)
                    kk = DVE(lambda e: e.reciprocal(SS[:, 14:15], SS[:, 13:14]), kk)
                    kk = DVE(lambda e, acc=acc: e.scalar_tensor_tensor(acc, acc, SS[:, 14:15], NF, ALU.mult,
                                                                       ALU.mult), kk, nf_in[0])
                    AC.dma(lambda e, t=t, acc=acc: e.dma_start(ov[t], acc), out_sem[t], kk)

        stage = {}

        def advance(until):
            while side[0] is not None and not until():
                if next(side[0], None) is None:
                    side[0] = None
            spent[0] = 0.0

        for g in range(NT // GB):
            top[0] = base
            project(g, x_in)

            def settle(g=g):
                if g:
                    advance(lambda: GB * g - 1 in gat)
                    barrier()

            attend(g, settle)
            x_ready = merge()
            x_ready = mlp(x_ready)
            x_ready = mixer(g, x_ready)
            advance(lambda: stage.get("last values") == g - 1)
            slots = slots7 if g + 1 < NT // GB else slots7 + [
                ring[j // 2][:, (j % 2) * D:(j % 2) * D + D] for j in range(2 * RING)]
            ex = queries(g, x_ready, lambda ex: experts(g, ex, slots))
            if g + 1 < NT // GB:
                x_in = ex["x"]
                side[0] = ex["experts"]
                spent[0] = 0.0
            else:
                for j in range(7, 15):
                    slot_free[j] = PE.last
                last = ex["experts"]
                for _ in range(CHOICE - 8):
                    next(last)
                    for _ in range(6):
                        if side[0] is not None and next(side[0], None) is None:
                            side[0] = None
                advance(lambda: False)
                for _ in last:
                    pass
        for s in out_sem + slot_sem + ring_sem + x_sem + sems + [small]:
            SP.wait((s[0], s[1]))

        def run(q):
            def body(e):
                for op in q.ops:
                    op(e)
            return body

        block.tensor(run(PE))
        block.vector(run(DVE))
        block.scalar(run(AC))
        block.gpsimd(run(GP))
        block.sync(run(SP))


def kernel(**inputs):
    import concourse.bacc as _bacc
    from concourse.bass_utils import run_bass_kernel_spmd as _run

    x = {n: np.ascontiguousarray(v) for n, v in inputs.items()}

    def pad(v, n=P):
        return np.concatenate([v, np.zeros((n - v.shape[0],) + v.shape[1:], v.dtype)], 0) if v.shape[0] < n else v

    def by(v):
        return v.reshape(-1, P).T

    b = x["b_in"][0]
    cols = np.concatenate([
        by(x["norm1_g"][0]), by(b[QA:QA + 256]), by(b[QB:QB + 384]), by(b[QC:QC + 384]), by(b[KA:KA + 256]),
        by(b[KB:KB + 384]), by(b[KC:KC + 128]), by(b[VC:VC + 128]), by(b[KSL:KSL + 128]), by(b[KWN:KWN + 128]),
        pad(b[FA:FA + 4].reshape(4, 1)), by(b[GATES:]), by(x["norm2_g"][0]),
        by(x["conv_w"][0].reshape(-1)), by(x["conv_b"][0]), by(x["norm_mix_2"][0]),
        by(x["conv_w_2"][0].reshape(-1)), by(x["conv_gain_2"][0]), by(x["hg_lb_logits_2"].reshape(-1)),
        by(x["hg_gain_2"][0]), by(x["norm_ffn_2"][0]),
        np.concatenate([x["cmp_pe"][0].T, x["cmp_pe"][0].T], 0)], 1)
    rows = np.concatenate([b[VA:VA + 256], b[VB:VB + 384], b[VSL:VSL + 128], b[VWN:VWN + 128], b[GC:GC + 18],
                           x["final_g"], x["norm_ffn_2"][0], x["norm_f_2"]])[None]
    keys = x["peer_keys_2"][0].transpose(3, 0, 1, 2).reshape(P, 16 * P)
    arrays = {"x": x["x"][0], "cols": cols, "rows": rows, "keys": keys, "con": constants()}
    for n in ("w_in", "cmp_k_w1", "cmp_k_w2", "cmp_v_w1", "cmp_v_w2", "w_pa", "w_pb", "w_pc", "w_o", "w_up",
              "w_down", "w_in_2", "w_out_2", "peer_wq_2", "peer_u_2", "peer_v_2"):
        arrays[n] = x[n][0]
    nc = _bacc.Bacc("TRN2", target_bir_lowering=False, num_devices=1)
    sent, aps = {}, {}
    for n, v in arrays.items():
        v = np.ascontiguousarray(v)
        sent[f"in_{n}"] = v
        aps[n] = nc.dram_tensor(f"in_{n}", v.shape, mybir.dt.from_np(v.dtype), kind="ExternalInput").ap()
    aps["out"] = nc.dram_tensor("out_0", (S, D), F32, kind="ExternalOutput").ap()
    build(nc, aps)
    r = _run(nc, [sent], core_ids=[0])
    return r.results[0]["out_0"].reshape(1, S, D)
```
